# Optimizing a Trainium2 kernel written in Bass

```python
import jax, jax.numpy as jnp
from jax import lax
import numpy as np

D_MODEL = 1024
BATCH = 1
SEQ = 1024
DEPTH = 2

HEAD_DIM = 64
N_HEADS_A = D_MODEL // (2 * HEAD_DIM)
N_HEADS_B = D_MODEL // (2 * HEAD_DIM)
WIDTH_A = N_HEADS_A * HEAD_DIM
WIDTH_B = N_HEADS_B * HEAD_DIM
MIX_WIDTH = WIDTH_A + WIDTH_B
IN_COLS_A = 4 * WIDTH_A
IN_COLS = IN_COLS_A + 3 * WIDTH_B
D_DECAY_LORA = 64
D_AAA_LORA = 64
D_GATE_LORA = 128
DILATED_PAIRS = ((128, 1), (512, 4), (2048, 16))
ROPE_THETA = 10000.0
N_FOURIER_GROUPS = 8
FOURIER_GROUP = D_MODEL // N_FOURIER_GROUPS
D_FF = ((8 * D_MODEL // 3 + 127) // 128) * 128
N_EVEN = (DEPTH + 1) // 2
N_ODD = DEPTH // 2
RMS_EPS = 1e-6
LNX_EPS = 64e-5
L2_EPS = 1e-12
NEG_BIG = -1e30
F32 = jnp.float32

kernel_name = 'hybrid_rwkv7_dilated_fnet_block'

def rmsnorm(x, g):
    xf = x.astype(F32)
    y = xf * lax.rsqrt(jnp.mean(xf * xf, -1, keepdims=True) + RMS_EPS)
    return (y * g.astype(F32)).astype(x.dtype)

def dwconv3(x, w):
    xp = jnp.pad(x, ((0, 0), (1, 1), (0, 0)))
    return xp[:, :-2] * w[0] + xp[:, 1:-1] * w[1] + xp[:, 2:] * w[2]

def rope(x, pos):
    half = x.shape[-1] // 2
    inv = ROPE_THETA ** (-jnp.arange(half, dtype=F32) / half)
    ang = pos.astype(F32)[:, None] * inv[None, :]
    cos = jnp.cos(ang)[None, :, None, :]
    sin = jnp.sin(ang)[None, :, None, :]
    x1 = x[..., :half].astype(F32)
    x2 = x[..., half:].astype(F32)
    return jnp.concatenate([x1 * cos - x2 * sin, x2 * cos + x1 * sin], -1).astype(x.dtype)

def wkv7_scan(r, w, k, v, kk, a, reverse):
    B_, S_, H_, N_ = r.shape
    xs = tuple(jnp.moveaxis(t, 1, 0) for t in (r, w, k, v, kk, a))

    def step(state, inp):
        r_t, w_t, k_t, v_t, kk_t, a_t = inp
        sk = jnp.einsum('bhij,bhj->bhi', state, kk_t)
        state = (state * w_t[:, :, None, :]
                 - sk[..., :, None] * (kk_t * a_t)[:, :, None, :]
                 + v_t[..., :, None] * k_t[:, :, None, :])
        y = jnp.einsum('bhij,bhj->bhi', state, r_t)
        return state, y

    s0 = jnp.zeros((B_, H_, N_, N_), F32)
    _, ys = lax.scan(step, s0, xs, reverse=reverse)
    return jnp.moveaxis(ys, 0, 1)

def rwkv7_mixer(r, k, v, u, w0, w1, w2, a0, a1, a2, g1, g2, k_k, k_a, r_k, lnx_w, lnx_b):
    B_, S_, _ = r.shape
    rf, kf, vf, uf = (t.astype(F32) for t in (r, k, v, u))
    hs = lambda t: t.reshape(B_, S_, N_HEADS_A, HEAD_DIM)
    g = jax.nn.sigmoid(uf @ g1) @ g2
    kk = hs(kf * k_k)
    kk = kk * lax.rsqrt(jnp.sum(kk * kk, -1, keepdims=True) + L2_EPS)
    rh, vh = hs(rf), hs(vf)
    y = 0.0
    bonus = 0.0
    for d in range(2):
        w_log = -jax.nn.softplus(-(w0[d] + jnp.tanh(uf @ w1[d]) @ w2[d])) - 0.5
        decay = jnp.exp(-jnp.exp(w_log))
        a = jax.nn.sigmoid(a0[d] + (uf @ a1[d]) @ a2[d])
        kd = hs(kf * (1.0 + (a - 1.0) * k_a))
        ah = hs(a)
        y = y + wkv7_scan(rh, hs(decay), kd, vh, kk, ah, reverse=(d == 1))
        bonus = bonus + jnp.sum(rh * kd * r_k, -1, keepdims=True) * vh
    mu = jnp.mean(y, -1, keepdims=True)
    var = jnp.mean(jnp.square(y - mu), -1, keepdims=True)
    y = ((y - mu) * lax.rsqrt(var + LNX_EPS)).reshape(B_, S_, WIDTH_A) * lnx_w + lnx_b
    y = (y + bonus.reshape(B_, S_, WIDTH_A)) * g
    return y.astype(r.dtype)

def dilated_branch(q, k, v, window, dilation):
    B_, S_, H_, E_ = q.shape
    hk = window // (2 * dilation)
    M = S_ // dilation
    nb = -(-M // hk)
    Mp = nb * hk

    def blocks(t):
        t = t.reshape(B_, M, dilation, H_, E_)
        t = jnp.pad(t, ((0, 0), (0, Mp - M), (0, 0), (0, 0), (0, 0)))
        return t.reshape(B_, nb, hk, dilation, H_, E_)

    def band(t):
        tp = jnp.pad(t, ((0, 0), (1, 1), (0, 0), (0, 0), (0, 0), (0, 0)))
        return jnp.concatenate([tp[:, :-2], tp[:, 1:-1], tp[:, 2:]], axis=2)

    qb = blocks(q)
    kw = band(blocks(k))
    vw = band(blocks(v))
    s = jnp.einsum('bnqrhe,bnkrhe->bnrhqk', qb, kw).astype(F32) * (E_ ** -0.5)
    blk = jnp.arange(nb)[:, None, None]
    qi = blk * hk + jnp.arange(hk)[None, :, None]
    ki = (blk - 1) * hk + jnp.arange(3 * hk)[None, None, :]
    valid = (jnp.abs(ki - qi) <= hk) & (ki >= 0) & (ki < M)
    s = jnp.where(valid[None, :, None, None], s, NEG_BIG)
    m = jnp.max(s, -1)
    p = jnp.exp(s - m[..., None])
    den = jnp.sum(p, -1)
    num = jnp.einsum('bnrhqk,bnkrhe->bnqrhe', p.astype(v.dtype), vw).astype(F32)

    def unblock(t):
        t = t.reshape((B_, Mp, dilation) + t.shape[4:])[:, :M]
        return t.reshape((B_, S_) + t.shape[3:])

    m = unblock(jnp.moveaxis(m, -1, 2))
    den = unblock(jnp.moveaxis(den, -1, 2))
    num = unblock(num)
    return m, den, num

def dilated_attention(q, k, v):
    outs = [dilated_branch(q, k, v, w, d) for (w, d) in DILATED_PAIRS]
    m_all = jnp.max(jnp.stack([o[0] for o in outs], 0), 0)
    den = 0.0
    num = 0.0
    for m, dn, nm in outs:
        e = jnp.exp(m - m_all)
        den = den + e * dn
        num = num + e[..., None] * nm
    return num / den[..., None]

def parallel_mixer(h, mix_in, mix_conv, w0, w1, w2, a0, a1, a2, g1, g2,
                   k_k, k_a, r_k, lnx_w, lnx_b, mix_out):
    B_, S_, _ = h.shape
    z = h @ mix_in
    za = dwconv3(z[..., :IN_COLS_A], mix_conv)
    r, k, v, u = jnp.split(za, 4, -1)
    ya = rwkv7_mixer(r, k, v, u, w0, w1, w2, a0, a1, a2, g1, g2, k_k, k_a, r_k, lnx_w, lnx_b)
    qb, kb, vb = (t.reshape(B_, S_, N_HEADS_B, HEAD_DIM) for t in jnp.split(z[..., IN_COLS_A:], 3, -1))
    pos = jnp.arange(S_)
    qb = rope(qb, pos)
    kb = rope(kb, pos)
    yb = dilated_attention(qb, kb, vb).astype(h.dtype).reshape(B_, S_, WIDTH_B)
    return jnp.concatenate([ya, yb], -1) @ mix_out

def fourier_mixer(h, fnet_w):
    B_, S_, D_ = h.shape
    hg = h.astype(F32).reshape(B_, S_, N_FOURIER_GROUPS, FOURIER_GROUP)
    f = jnp.fft.fft2(hg, axes=(1, 3), norm='ortho').real
    return f.reshape(B_, S_, D_).astype(h.dtype) @ fnet_w

def conv_glu(h, up, conv, down):
    z = dwconv3(h @ up, conv)
    gate, val = jnp.split(z, 2, -1)
    return (jax.nn.gelu(gate, approximate=True) * val) @ down

def setup_inputs(seed: int = 0) -> dict:
    key = jax.random.key(seed)
    ks = jax.random.split(key, 26)
    nrm = lambda k, shape, s: jax.random.normal(k, shape, F32) * s
    ident3 = lambda k, C, n: jnp.broadcast_to(jnp.array([0.0, 1.0, 0.0], F32)[None, :, None], (n, 3, C)) + nrm(k, (n, 3, C), 0.2)
    return {
        'x': nrm(ks[0], (BATCH, SEQ, D_MODEL), 1.0),
        'c': nrm(ks[1], (BATCH, D_MODEL), 1.0),
        'ada_w': nrm(ks[2], (DEPTH, D_MODEL, 6 * D_MODEL), D_MODEL ** -0.5),
        'ada_b': nrm(ks[3], (DEPTH, 6 * D_MODEL), 0.02),
        'norm_g': 1.0 + nrm(ks[4], (DEPTH, 4, D_MODEL), 0.05),
        'mix_in': nrm(ks[5], (N_EVEN, D_MODEL, IN_COLS), D_MODEL ** -0.5),
        'mix_conv': ident3(ks[6], IN_COLS_A, N_EVEN),
        'rwkv_w0': jax.random.uniform(ks[7], (N_EVEN, 2, WIDTH_A), F32, -6.0, -1.0),
        'rwkv_w1': nrm(ks[8], (N_EVEN, 2, WIDTH_A, D_DECAY_LORA), WIDTH_A ** -0.5),
        'rwkv_w2': nrm(ks[9], (N_EVEN, 2, D_DECAY_LORA, WIDTH_A), 0.1 * D_DECAY_LORA ** -0.5),
        'rwkv_a0': nrm(ks[10], (N_EVEN, 2, WIDTH_A), 0.5),
        'rwkv_a1': nrm(ks[11], (N_EVEN, 2, WIDTH_A, D_AAA_LORA), WIDTH_A ** -0.5),
        'rwkv_a2': nrm(ks[12], (N_EVEN, 2, D_AAA_LORA, WIDTH_A), 0.5 * D_AAA_LORA ** -0.5),
        'rwkv_g1': nrm(ks[13], (N_EVEN, WIDTH_A, D_GATE_LORA), WIDTH_A ** -0.5),
        'rwkv_g2': nrm(ks[14], (N_EVEN, D_GATE_LORA, WIDTH_A), D_GATE_LORA ** -0.5),
        'rwkv_k_k': 0.85 + nrm(ks[15], (N_EVEN, WIDTH_A), 0.1),
        'rwkv_k_a': 1.0 + nrm(ks[16], (N_EVEN, WIDTH_A), 0.1),
        'rwkv_r_k': nrm(ks[17], (N_EVEN, N_HEADS_A, HEAD_DIM), 0.1),
        'rwkv_lnx_w': 1.0 + nrm(ks[18], (N_EVEN, WIDTH_A), 0.05),
        'rwkv_lnx_b': nrm(ks[19], (N_EVEN, WIDTH_A), 0.02),
        'mix_out': nrm(ks[20], (N_EVEN, MIX_WIDTH, D_MODEL), MIX_WIDTH ** -0.5),
        'fnet_w': nrm(ks[21], (N_ODD, D_MODEL, D_MODEL), D_MODEL ** -0.5),
        'ffn_up': nrm(ks[22], (DEPTH, D_MODEL, 2 * D_FF), D_MODEL ** -0.5),
        'ffn_conv': ident3(ks[23], 2 * D_FF, DEPTH),
        'ffn_down': nrm(ks[24], (DEPTH, D_FF, D_MODEL), D_FF ** -0.5),
    }

def reference(x, c, ada_w, ada_b, norm_g, mix_in, mix_conv, rwkv_w0, rwkv_w1, rwkv_w2,
              rwkv_a0, rwkv_a1, rwkv_a2, rwkv_g1, rwkv_g2, rwkv_k_k, rwkv_k_a, rwkv_r_k,
              rwkv_lnx_w, rwkv_lnx_b, mix_out, fnet_w, ffn_up, ffn_conv, ffn_down):
    cs = jax.nn.silu(c)
    for l in range(DEPTH):
        mod = cs @ ada_w[l] + ada_b[l]
        sh1, sc1, gt1, sh2, sc2, gt2 = [m[:, None, :] for m in jnp.split(mod, 6, -1)]
        h = rmsnorm(x, norm_g[l, 0]) * (1.0 + sc1) + sh1
        if l % 2 == 0:
            e = l // 2
            y = parallel_mixer(h, mix_in[e], mix_conv[e], rwkv_w0[e], rwkv_w1[e], rwkv_w2[e],
                               rwkv_a0[e], rwkv_a1[e], rwkv_a2[e], rwkv_g1[e], rwkv_g2[e],
                               rwkv_k_k[e], rwkv_k_a[e], rwkv_r_k[e], rwkv_lnx_w[e], rwkv_lnx_b[e],
                               mix_out[e])
        else:
            y = fourier_mixer(h, fnet_w[l // 2])
        x = x + gt1 * rmsnorm(y, norm_g[l, 1])
        h = rmsnorm(x, norm_g[l, 2]) * (1.0 + sc2) + sh2
        y = conv_glu(h, ffn_up[l], ffn_conv[l], ffn_down[l])
        x = x + gt2 * rmsnorm(y, norm_g[l, 3])
    return x


_drawn_inputs = setup_inputs


def setup_inputs(seed=0):
    import zlib

    import numpy as np

    out = dict(_drawn_inputs(seed))
    spreads = {}
    factors = {'rwkv_w1': 8.0, 'rwkv_w2': 8.0, 'rwkv_lnx_w': 5.297, 'rwkv_lnx_b': 29.067}
    for name, (base, spread) in spreads.items():
        noise = np.random.default_rng([zlib.crc32(name.encode()), seed]).standard_normal(out[name].shape)
        drawn = base * np.exp(spread * noise) if base else spread * noise
        out[name] = __import__('jax').numpy.asarray(drawn.astype(out[name].dtype))
    for name, factor in factors.items():
        out[name] = (out[name] * factor).astype(out[name].dtype)
    return out
```

```python
from contextlib import ExitStack
import math

import numpy as np
import concourse.bass as bass
from concourse import mybir

F32 = mybir.dt.float32
F32R = mybir.dt.float32r
U32 = mybir.dt.uint32
ALU = mybir.AluOpType
ACT = mybir.ActivationFunctionType
AX = mybir.AxisListType

P = 128
D = 1024
S = 1024
KT = D // P
TT = S // P
HALF = 512
HD = 64
NH = 8
WA = NH * HD
DFF = ((8 * D // 3 + 127) // 128) * 128
FT = DFF // P
CHUNK = 512
RMS_EPS = 1e-6
LNX_EPS = 64e-5
L2_EPS = 1e-12
DECAY = -math.exp(-0.5)
NEG_BIG = -1e30


class Scope:

    def __init__(self, nc, ctx, name):
        self.nc, self.ctx, self.name = nc, ctx, name
        self.sems = []

    def sb(self, name, shape, dt=F32):
        return self.ctx.enter_context(self.nc.sbuf_tensor(f"{self.name}_{name}", shape, dt))

    def ps(self, name, shape, dt=F32):
        return self.ctx.enter_context(self.nc.psum_tensor(f"{self.name}_{name}", shape, dt))

    def sem(self, name):
        self.sems.append(self.nc.alloc_semaphore(f"{self.name}_{name}"))
        return self.sems[-1]

    def block(self):
        def end():
            self.nc.clear_and_free_semaphores(self.sems)
            self.nc.all_engine_barrier()

        self.ctx.callback(end)
        return self.ctx.enter_context(self.nc.Block())


class Chain:

    def __init__(self, eng, sem):
        self.eng, self.sem, self.n, self.base = eng, sem, 0, 0

    def link(self, ins):
        self.n += 1
        ins.then_inc(self.sem, 1)
        self.eng.wait_ge(self.sem, self.base + self.n)

    def turn(self, i, steps):
        self.base, self.n = i * steps, 0


def modulation(nc, c, ada_w, ada_b, mod_d):
    L = ada_w.shape[0]
    per = 6 * D // CHUNK
    n = L * per
    with ExitStack() as ctx:
        s = Scope(nc, ctx, "mod")
        w = s.sb("w", [P, 2, KT, CHUNK])
        acc = s.sb("acc", [P, 2, CHUNK])
        ccol = s.sb("ccol", [P, KT])
        sig = s.sb("sig", [P, KT])
        sc = s.sb("sc", [P, KT])
        brow = s.sb("brow", [1, 2, CHUNK])
        row = s.sb("row", [1, 2, CHUNK])
        ones = s.sb("ones", [P, 1])
        ps = s.ps("ps", [P, 2, CHUNK])
        c_loaded, sig_done, sc_done, ones_done = s.sem("c_loaded"), s.sem("sig_done"), s.sem("sc_done"), s.sem("ones_done")
        w_loaded = [s.sem(f"w_loaded{j}") for j in range(2)]
        b_loaded = [s.sem(f"b_loaded{j}") for j in range(2)]
        row_stored = [s.sem(f"row_stored{j}") for j in range(2)]
        acc_done, sum_done, row_done, link_sem = s.sem("acc_done"), s.sem("sum_done"), s.sem("row_done"), s.sem("link")
        block = s.block()

        def w_src(l, e):
            return ada_w[l].rearrange("(t p) (e n) -> e p t n", p=P, n=CHUNK)[bass.ds(e, 1)].rearrange("o p t n -> p (o t) n")

        def b_src(l, e):
            return ada_b[l].rearrange("(e n) -> e n", n=CHUNK)[bass.ds(e, 1)]

        @block.sync
        def _(sp):
            sp.dma_start(ccol[:, :], c.rearrange("o (t p) -> p (o t)", p=P), allow_slow_non_contiguous=True).then_inc(c_loaded, 16)
            for l in range(L):
                with sp.Fori(0, per // 2) as i:
                    for j in range(2):
                        sp.wait_ge(row_done, l * per + i * 2 + (j + 1))
                        sp.dma_start(w[:, j], w_src(l, i * 2 + j)).then_inc(w_loaded[j], 16)
                        sp.dma_start(brow[:, j, :], b_src(l, i * 2 + j)).then_inc(b_loaded[j], 16)

        @block.scalar
        def _(act):
            act.wait_ge(c_loaded, 16)
            nc.scalar.activation(sig[:, :], ccol[:, :], ACT.Sigmoid).then_inc(sig_done, 1)
            for j in range(2):
                act.sem_inc(row_stored[j], 16)
            for l in range(L):
                with act.Fori(0, per // 2) as i:
                    for j in range(2):
                        act.wait_ge(row_done, l * per + i * 2 + (j + 3))
                        dst = mod_d[l].rearrange("(e n) -> e n", n=CHUNK)[bass.ds(i * 2 + j, 1)]
                        act.dma_start(dst, row[:, j, :]).then_inc(row_stored[j], 16)
            for j in range(2):
                act.wait_ge(row_stored[j], 16 + 16 * n // 2)

        @block.vector
        def _(dve):
            ch = Chain(dve, link_sem)
            nc.vector.memset(ones[:, :], 1.0).then_inc(ones_done, 1)
            dve.wait_ge(sig_done, 1)
            ch.link(nc.vector.tensor_tensor(sc[:, :], ccol[:, :], sig[:, :], ALU.mult))
            dve.sem_inc(row_done, 2)
            dve.wait_ge(ones_done, 1)
            for l in range(L):
                with dve.Fori(0, per // 2) as i:
                    ch.turn(i + l * (per // 2), 14)
                    ch.base = ch.base + 1
                    for j in range(2):
                        dve.wait_ge(w_loaded[j], (i + l * (per // 2)) * 16 + 16)
                        for t in range(KT):
                            if t == 0:
                                ins = nc.vector.tensor_scalar(acc[:, j, :], w[:, j, 0, :], sc[:, 0:1], None, ALU.mult)
                            else:
                                ins = nc.vector.scalar_tensor_tensor(acc[:, j, :], w[:, j, t, :], sc[:, t:t + 1],
                                                                     acc[:, j, :], ALU.mult, ALU.add)
                            if t < KT - 1:
                                ch.link(ins)
                            else:
                                ins.then_inc(acc_done, 1)
                        dve.wait_ge(b_loaded[j], (i + l * (per // 2)) * 16 + 16)
                        dve.wait_ge(sum_done, l * per + i * 2 + (j + 1))
                        dve.wait_ge(row_stored[j], (i + l * (per // 2)) * 16 + 16)
                        nc.vector.tensor_tensor(row[:, j, :], ps[0:1, j, :], brow[:, j, :], ALU.add).then_inc(row_done, 1)

        @block.tensor
        def _(pe):
            pe.wait_ge(ones_done, 1)
            for l in range(L):
                with pe.Fori(0, per // 2) as i:
                    for j in range(2):
                        pe.wait_ge(acc_done, l * per + i * 2 + (j + 1))
                        nc.tensor.matmul(ps[0:1, j, :], ones[:, :], acc[:, j, :], start=True, stop=True).then_inc(sum_done, 1)


def norm_to_features(nc, name, x_src, norm_row, mod_row, at, consts, h_hi, h_lo):
    ident = consts["ident"]
    with ExitStack() as ctx:
        s = Scope(nc, ctx, name)
        x = s.sb("x", [P, TT, D])
        sq = s.sb("sq", [P, D])
        ss = s.sb("ss", [P, TT])
        ms = s.sb("ms", [P, TT])
        rstd = s.sb("rstd", [P, TT])
        mhalf = s.sb("mhalf", [P, 1])
        g = s.sb("g", [P, KT])
        scale = s.sb("scale", [P, KT])
        shift = s.sb("shift", [P, KT])
        gain = s.sb("gain", [P, KT])
        h32 = s.sb("h32", [P, 4, HALF])
        ps = s.ps("ps", [P, 4, HALF])
        x_loaded = [s.sem(f"x_loaded{t}") for t in range(TT)]
        col_loaded, gain_done, half_done = s.sem("col_loaded"), s.sem("gain_done"), s.sem("half_done")
        ss_done, ms_done, rstd_done, xs_done = s.sem("ss_done"), s.sem("ms_done"), s.sem("rstd_done"), s.sem("xs_done")
        turned, h32_done, hi_done, lo_done = s.sem("turned"), s.sem("h32_done"), s.sem("hi_done"), s.sem("lo_done")
        link_sem = s.sem("link")
        block = s.block()
        steps = [(half, f) for half in range(2) for f in range(KT)]

        @block.sync
        def _(sp):
            for t in range(TT):
                sp.dma_start(x[:, t, :], x_src[t * P:(t + 1) * P, :]).then_inc(x_loaded[t], 16)
            sp.dma_start(g[:, :], norm_row.rearrange("(t p) -> p t", p=P), allow_slow_non_contiguous=True).then_inc(col_loaded, 16)
            sp.dma_start(shift[:, :], mod_row[at:at + D].rearrange("(t p) -> p t", p=P), allow_slow_non_contiguous=True).then_inc(col_loaded, 16)
            sp.dma_start(scale[:, :], mod_row[at + D:at + 2 * D].rearrange("(t p) -> p t", p=P), allow_slow_non_contiguous=True).then_inc(col_loaded, 16)

        @block.scalar
        def _(act):
            for t in range(TT):
                act.wait_ge(x_loaded[t], 16)
                if t:
                    act.wait_ge(ss_done, t)
                nc.scalar.activation(sq[:, :], x[:, t, :], ACT.Square, accum_out=ss[:, t:t + 1]).then_inc(ss_done, 1)
            for n, (half, f) in enumerate(steps):
                act.wait_ge(h32_done, n + 1)
                nc.scalar.activation(h_hi[:, f, half * HALF:(half + 1) * HALF], h32[:, n % 4, :], ACT.Copy).then_inc(hi_done, 1)

        @block.gpsimd
        def _(pool):
            nc.gpsimd.memset(mhalf[:, :], -0.5).then_inc(half_done, 1)
            pool.wait_ge(half_done, 1)
            pool.wait_ge(ms_done, 1)
            nc.gpsimd.tensor_tensor(rstd[:, :], ms[:, :], mhalf[:, 0:1].broadcast_to([P, TT]), ALU.pow).then_inc(rstd_done, 1)
            for n, (half, f) in enumerate(steps):
                pool.wait_ge(h32_done, n + 1)
                pool.wait_ge(hi_done, n + 1)
                span = slice(half * HALF, (half + 1) * HALF)
                nc.gpsimd.tensor_tensor(h_lo[:, f, span], h32[:, n % 4, :], h_hi[:, f, span].bitcast(F32),
                                        ALU.subtract).then_inc(lo_done, 1)

        @block.vector
        def _(dve):
            dve.wait_ge(col_loaded, 48)
            nc.vector.scalar_tensor_tensor(gain[:, :], scale[:, :], 1.0, g[:, :], ALU.add, ALU.mult).then_inc(gain_done, 1)
            dve.wait_ge(gain_done, 1)
            dve.wait_ge(ss_done, TT)
            nc.vector.tensor_scalar(ms[:, :], ss[:, :], 1.0 / D, RMS_EPS, ALU.mult, ALU.add).then_inc(ms_done, 1)
            dve.wait_ge(rstd_done, 1)
            for t in range(TT):
                nc.vector.tensor_scalar(x[:, t, :], x[:, t, :], rstd[:, t:t + 1], None, ALU.mult).then_inc(xs_done, 1)
            for n, (half, f) in enumerate(steps):
                dve.wait_ge(turned, n + 1)
                if n >= 4:
                    dve.wait_ge(lo_done, n - 3)
                nc.vector.tensor_scalar(h32[:, n % 4, :], ps[:, n % 4, :], gain[:, f:f + 1], shift[:, f:f + 1],
                                        ALU.mult, ALU.add).then_inc(h32_done, 1)

        @block.tensor
        def _(pe):
            for n, (half, f) in enumerate(steps):
                pe.wait_ge(xs_done, 4 * (half + 1))
                if n >= 4:
                    pe.wait_ge(h32_done, n - 3)
                for t in range(4):
                    ins = nc.tensor.transpose(ps[:, n % 4, t * P:(t + 1) * P], x[:, 4 * half + t, f * P:(f + 1) * P], ident[:, :])
                ins.then_inc(turned, 1)


def split_products(nc, out, a_hi, a_lo, b_hi, b_lo, first, last):
    nc.tensor.matmul(out, a_hi, b_hi, start=first, stop=False)
    nc.tensor.matmul(out, a_hi, b_lo, start=False, stop=False)
    return nc.tensor.matmul(out, a_lo, b_hi, start=False, stop=last)


def project_qkv(nc, mix_in, h_hi, h_lo, consts, rope_cos, rope_sin, qk_d, v_d):
    ident = consts["ident"]
    NC = 3
    w_v = mix_in[0].rearrange("(t p) n -> t p n", p=P)
    with ExitStack() as ctx:
        s = Scope(nc, ctx, "qkv")
        R = 4
        w_raw = s.sb("w_raw", [P, R, WA])
        w_hi = s.sb("w_hi", [P, 2, KT, WA], F32R)
        w_lo = s.sb("w_lo", [P, 2, KT, WA], F32R)
        cos = s.sb("cos", [P, TT, HD])
        sin = s.sb("sin", [P, TT, HD])
        rc = s.sb("rc", [P, 2, WA])
        rs = s.sb("rs", [P, 2, WA])
        rot = s.sb("rot", [P, 2, WA])
        stage = s.sb("stage", [P, 2, WA])
        ps = s.ps("ps", [P, 4, WA])
        pt = s.ps("pt", [P, 2, WA])
        raw_loaded = [s.sem(f"raw_loaded{j}") for j in range(R)]
        tab_loaded, hi_done, lo_done = s.sem("tab_loaded"), s.sem("hi_done"), s.sem("lo_done")
        mm_done, rc_done, rs_done, rot_done = s.sem("mm_done"), s.sem("rc_done"), s.sem("rs_done"), s.sem("rot_done")
        turned, staged = s.sem("turned"), s.sem("staged")
        stored = [s.sem(f"stored{j}") for j in range(2)]
        block = s.block()

        @block.sync
        def _(sp):
            sp.dma_start(cos[:, :, :], rope_cos.rearrange("(t p) e -> p t e", p=P)).then_inc(tab_loaded, 16)
            sp.dma_start(sin[:, :, :], rope_sin.rearrange("(t p) e -> p t e", p=P)).then_inc(tab_loaded, 16)
            for n in range(NC * KT):
                cb, k = divmod(n, KT)
                if n >= R:
                    sp.wait_ge(lo_done, n - R + 1)
                sp.dma_start(w_raw[:, n % R, :], w_v[k, :, 4 * WA + cb * WA:4 * WA + (cb + 1) * WA]).then_inc(raw_loaded[n % R], 16)

        @block.scalar
        def _(act):
            def split(cb):
                if cb >= 2:
                    act.wait_ge(mm_done, TT * (cb - 1))
                for k in range(KT):
                    n = cb * KT + k
                    act.wait_ge(raw_loaded[n % R], 16 * (n // R + 1))
                    nc.scalar.activation(w_hi[:, cb % 2, k, :], w_raw[:, n % R, :], ACT.Copy).then_inc(hi_done, 1)

            def stage_out(cb, t):
                n = cb * TT + t
                if n >= 2:
                    act.wait_ge(stored[n % 2], 16 * (n // 2))
                if cb < 2:
                    act.wait_ge(turned, n + 1)
                    nc.scalar.activation(stage[:, n % 2, :], pt[:, n % 2, :], ACT.Copy).then_inc(staged, 1)
                    act.wait_ge(staged, n + 1)
                    dst = qk_d[cb].rearrange("(f p) s -> p f s", p=P)[:, :, t * P:(t + 1) * P]
                    act.dma_start(dst, stage[:, n % 2, :].rearrange("p (f s) -> p f s", f=4)).then_inc(stored[n % 2], 16)
                else:
                    act.wait_ge(mm_done, n + 1)
                    nc.scalar.activation(stage[:, n % 2, :], ps[:, n % 4, :], ACT.Copy).then_inc(staged, 1)
                    act.wait_ge(staged, n + 1)
                    act.dma_start(v_d[t * P:(t + 1) * P, :], stage[:, n % 2, :]).then_inc(stored[n % 2], 16)

            split(0)
            split(1)
            for cb in range(NC):
                for t in range(TT):
                    stage_out(cb, t)
                if cb + 2 < NC:
                    split(cb + 2)
            for j in range(2):
                act.wait_ge(stored[j], 16 * NC * TT // 2)

        @block.gpsimd
        def _(pool):
            def split(cb):
                for k in range(KT):
                    n = cb * KT + k
                    pool.wait_ge(hi_done, n + 1)
                    nc.gpsimd.tensor_tensor(w_lo[:, cb % 2, k, :], w_raw[:, n % R, :], w_hi[:, cb % 2, k, :].bitcast(F32),
                                            ALU.subtract).then_inc(lo_done, 1)

            for cb in range(NC):
                split(cb)

        @block.vector
        def _(dve):
            dve.wait_ge(tab_loaded, 32)
            for cb in range(2):
                for t in range(TT):
                    n = cb * TT + t
                    src = ps[:, n % 4, :].rearrange("p (h e) -> p h e", h=NH)
                    c = rc[:, n % 2, :].rearrange("p (h e) -> p h e", h=NH)
                    z = rs[:, n % 2, :].rearrange("p (h e) -> p h e", h=NH)
                    cb_t = cos[:, t:t + 1, :].broadcast_to([P, NH, HD])
                    lo_t = sin[:, t:t + 1, 0:HD // 2].broadcast_to([P, NH, HD // 2])
                    hi_t = sin[:, t:t + 1, HD // 2:HD].broadcast_to([P, NH, HD // 2])
                    dve.wait_ge(mm_done, n + 1)
                    nc.vector.tensor_tensor(c, src, cb_t, ALU.mult).then_inc(rc_done, 1)
                    nc.vector.tensor_tensor(z[:, :, 0:HD // 2], src[:, :, HD // 2:HD], lo_t, ALU.mult)
                    nc.vector.tensor_tensor(z[:, :, HD // 2:HD], src[:, :, 0:HD // 2], hi_t, ALU.mult).then_inc(rs_done, 1)
                    dve.wait_ge(rc_done, n + 1)
                    dve.wait_ge(rs_done, n + 1)
                    if n >= 2:
                        dve.wait_ge(turned, n - 1)
                    nc.vector.tensor_tensor(rot[:, n % 2, :], rc[:, n % 2, :], rs[:, n % 2, :], ALU.add).then_inc(rot_done, 1)

        @block.tensor
        def _(pe):
            def turn(n):
                pe.wait_ge(rot_done, n + 1)
                if n >= 2:
                    pe.wait_ge(staged, n - 1)
                for f in range(4):
                    ins = nc.tensor.transpose(pt[:, n % 2, f * P:(f + 1) * P], rot[:, n % 2, f * P:(f + 1) * P], ident[:, :])
                ins.then_inc(turned, 1)

            for cb in range(NC):
                pe.wait_ge(lo_done, KT * (cb + 1))
                for t in range(TT):
                    n = cb * TT + t
                    if n >= 4:
                        if n - 4 < 2 * TT:
                            pe.wait_ge(rs_done, n - 3)
                        else:
                            pe.wait_ge(staged, n - 3)
                    for k in range(KT):
                        ins = split_products(nc, ps[:, n % 4, :], h_hi[:, k, t * P:(t + 1) * P], h_lo[:, k, t * P:(t + 1) * P],
                                             w_hi[:, cb % 2, k, :], w_lo[:, cb % 2, k, :], k == 0, k == KT - 1)
                    ins.then_inc(mm_done, 1)
                    if 1 <= n <= 2 * TT:
                        turn(n - 1)


def load_columns(nc, groups, consts):
    ident = consts["ident"]
    with ExitStack() as ctx:
        s = Scope(nc, ctx, "cols")
        n_max = max(src.shape[0] for src, _ in groups)
        rows = s.sb("rows", [n_max, len(groups), P])
        ps = s.ps("ps", [P, len(groups), 64])
        loaded = [s.sem(f"loaded{i}") for i in range(len(groups))]
        turned, copied = s.sem("turned"), s.sem("copied")
        block = s.block()

        @block.sync
        def _(sp):
            for i, (src, _) in enumerate(groups):
                sp.dma_start(rows[0:src.shape[0], i, :], src).then_inc(loaded[i], 16)

        @block.tensor
        def _(pe):
            for i, (src, _) in enumerate(groups):
                n = src.shape[0]
                pe.wait_ge(loaded[i], 16)
                nc.tensor.transpose(ps[:, i, 0:n], rows[0:n, i, :], ident[0:n, 0:n]).then_inc(turned, 1)

        @block.vector
        def _(dve):
            dve.wait_ge(turned, len(groups))
            for i, (src, dst) in enumerate(groups):
                nc.vector.tensor_copy(dst, ps[:, i, 0:src.shape[0]]).then_inc(copied, 1)
            dve.wait_ge(copied, len(groups))


def make_constants(nc, consts):
    with ExitStack() as ctx:
        s = Scope(nc, ctx, "const")
        zeroed, selected = s.sem("zeroed"), s.sem("selected")
        heads_zeroed, heads_set = s.sem("heads_zeroed"), s.sem("heads_set")
        ident, heads = consts["ident"], consts["heads"]
        block = s.block()

        @block.gpsimd
        def _(pool):
            nc.gpsimd.memset(ident[:, :], 0.0).then_inc(zeroed, 1)
            pool.wait_ge(zeroed, 1)
            nc.gpsimd.affine_select(out=ident[:, :], in_=ident[:, :], compare_op=ALU.not_equal, fill=1.0, base=0,
                                    pattern=[[-1, P]], channel_multiplier=1).then_inc(selected, 1)

        @block.vector
        def _(dve):
            nc.vector.memset(heads[:, :], 0.0).then_inc(heads_zeroed, 1)
            dve.wait_ge(heads_zeroed, 1)
            nc.vector.memset(heads[0:HD, 0:HD], 1.0)
            nc.vector.memset(heads[HD:P, HD:P], 1.0).then_inc(heads_set, 1)
            dve.wait_ge(heads_set, 1)


def project_convolved(nc, mix_in, conv_cols, h_hi, h_lo, z_d):
    M = 4 * WA // P
    B = 4
    w_v = mix_in[0].rearrange("(t p) (m c) -> m p t c", p=P, c=P)
    with ExitStack() as ctx:
        s = Scope(nc, ctx, "za")
        w_raw = s.sb("w_raw", [P, B, KT, P])
        w_hi = s.sb("w_hi", [P, 2, KT, P], F32R)
        w_lo = s.sb("w_lo", [P, 2, KT, P], F32R)
        z = s.sb("z", [P, 2, S])
        ps = s.ps("ps", [P, 2, S])
        raw_loaded = [s.sem(f"raw_loaded{j}") for j in range(B)]
        stored = [s.sem(f"stored{j}") for j in range(2)]
        hi_done, lo_done, mm_done = s.sem("hi_done"), s.sem("lo_done"), s.sem("mm_done")
        mid_done, left_done, conv_done = s.sem("mid_done"), s.sem("left_done"), s.sem("conv_done")
        block = s.block()

        @block.sync
        def _(sp):
            def load(n, j):
                sp.dma_start(w_raw[:, j], w_v[bass.ds(n, 1)].rearrange("o p t c -> p (o t) c")).then_inc(raw_loaded[j], 16)

            def store(n, j):
                sp.wait_ge(conv_done, n + 3)
                sp.dma_start(z_d[bass.ds(n, 1)].rearrange("o p s -> p (o s)"), z[:, j % 2, :]).then_inc(stored[j % 2], 16)

            for j in range(2):
                sp.sem_inc(stored[j], 16)
            for j in range(B):
                load(j, j)
            with sp.Fori(0, M // B - 1) as i:
                for j in range(B):
                    store(i * B + j, j)
                    sp.wait_ge(lo_done, i * B + (j + 1))
                    load(i * B + (j + B), j)
            for j in range(B):
                store(M - B + j, j)
            for j in range(2):
                sp.wait_ge(stored[j], 16 + 16 * M // 2)

        @block.scalar
        def _(act):
            def split(i, j):
                act.wait_ge(raw_loaded[j], i * 16 + 16)
                act.wait_ge(mm_done, i * B + (j + 1))
                nc.scalar.activation(w_hi[:, j % 2], w_raw[:, j], ACT.Copy).then_inc(hi_done, 1)

            with act.Fori(0, M // B) as i:
                for j in range(B):
                    split(i, j)
                    act.wait_ge(mm_done, i * B + (j + 3))
                    act.wait_ge(stored[j % 2], i * (16 * B // 2) + 16 * (j // 2) + 16)
                    nc.scalar.activation(z[:, j % 2, :], ps[:, j % 2, :], ACT.Copy,
                                         scale=conv_cols[:, 1, bass.ds(i * B + j, 1)]).then_inc(mid_done, 1)

        @block.gpsimd
        def _(pool):
            with pool.Fori(0, M // B) as i:
                for j in range(B):
                    pool.wait_ge(hi_done, i * B + (j + 1))
                    nc.gpsimd.tensor_tensor(w_lo[:, j % 2], w_raw[:, j], w_hi[:, j % 2].bitcast(F32), ALU.subtract).then_inc(lo_done, 1)

        @block.vector
        def _(dve):
            dve.sem_inc(conv_done, 2)
            with dve.Fori(0, M // B) as i:
                for j in range(B):
                    dve.wait_ge(mid_done, i * B + (j + 1))
                    nc.vector.scalar_tensor_tensor(z[:, j % 2, 1:S], ps[:, j % 2, 0:S - 1], conv_cols[:, 0, bass.ds(i * B + j, 1)],
                                                   z[:, j % 2, 1:S], ALU.mult, ALU.add).then_inc(left_done, 1)
                    dve.wait_ge(left_done, i * B + (j + 1))
                    nc.vector.scalar_tensor_tensor(z[:, j % 2, 0:S - 1], ps[:, j % 2, 1:S], conv_cols[:, 2, bass.ds(i * B + j, 1)],
                                                   z[:, j % 2, 0:S - 1], ALU.mult, ALU.add).then_inc(conv_done, 1)

        @block.tensor
        def _(pe):
            pe.sem_inc(mm_done, 2)
            with pe.Fori(0, M // B) as i:
                for j in range(B):
                    pe.wait_ge(lo_done, i * B + (j + 1))
                    pe.wait_ge(conv_done, i * B + (j + 1))
                    for half in range(2):
                        span = slice(half * HALF, (half + 1) * HALF)
                        for k in range(KT):
                            ins = split_products(nc, ps[:, j % 2, span], w_hi[:, j % 2, k, :], w_lo[:, j % 2, k, :],
                                                 h_hi[:, k, span], h_lo[:, k, span], k == 0, k == KT - 1)
                    ins.then_inc(mm_done, 1)


def dilated_attention(nc, qk_d, v_d, bias_table, consts, yb_d):
    ident = consts["ident"]
    HB = 4
    NS = HB * TT
    OFF = S - P
    with ExitStack() as ctx:
        s = Scope(nc, ctx, "att")
        bias = s.sb("bias", [P, 2 * S - P])
        qT = s.sb("qT", [HD, HB, S])
        kT = s.sb("kT", [HD, HB, S])
        v = s.sb("v", [P, HB, TT, HD])
        sc = s.sb("sc", [P, 2, S])
        pr = s.sb("pr", [P, 2, S])
        prT = s.sb("prT", [P, 2, S])
        lowest = s.sb("lowest", [P, NS])
        den = s.sb("den", [P, NS])
        rden = s.sb("rden", [P, NS])
        y = s.sb("y", [P, 2, TT, HD])
        ps_s = s.ps("s", [P, 2, S])
        ps_t = s.ps("t", [P, S])
        ps_o = s.ps("o", [P, 2, 512])
        q_loaded = [s.sem(f"q_loaded{j}") for j in range(HB)]
        stored = [s.sem(f"stored{j}") for j in range(2)]
        begun, bias_loaded = s.sem("begun"), s.sem("bias_loaded")
        score_done, biased, exp_done, turned = s.sem("score_done"), s.sem("biased"), s.sem("exp_done"), s.sem("turned")
        copied_lo, copied_hi, out_done, rden_done, y_done = (
            s.sem("copied_lo"), s.sem("copied_hi"), s.sem("out_done"), s.sem("rden_done"), s.sem("y_done"))
        block = s.block()

        @block.sync
        def _(sp):
            sp.dma_start(bias[:, :], bias_table).then_inc(bias_loaded, 16)
            for j in range(2):
                sp.sem_inc(stored[j], 16)
            with sp.Fori(0, NH // HB) as i:
                for j in range(HB):
                    sp.wait_ge(out_done, i * NS + 2)
                    h = i * HB + j
                    sp.dma_start(qT[:, j, :], qk_d[0].rearrange("(h e) s -> h e s", e=HD)[bass.ds(h, 1)].rearrange("o e s -> (o e) s")).then_inc(q_loaded[j], 16)
                    sp.dma_start(kT[:, j, :], qk_d[1].rearrange("(h e) s -> h e s", e=HD)[bass.ds(h, 1)].rearrange("o e s -> (o e) s")).then_inc(q_loaded[j], 16)
                    sp.dma_start(v[:, j], v_d.rearrange("(t p) (h e) -> h p t e", p=P, e=HD)[bass.ds(h, 1)].rearrange("o p t e -> p (o t) e")).then_inc(q_loaded[j], 16)
                for j in range(HB):
                    h = i * HB + j
                    sp.wait_ge(y_done, i * NS + (TT * (j + 1) + 2))
                    sp.dma_start(yb_d.rearrange("(t p) (h e) -> h p t e", p=P, e=HD)[bass.ds(h, 1)].rearrange("o p t e -> p (o t) e"), y[:, j % 2]).then_inc(stored[j % 2], 16)
            for j in range(2):
                sp.wait_ge(stored[j], 16 + 16 * NH // 2)

        @block.tensor
        def _(pe):
            pe.sem_inc(out_done, 2)
            pe.sem_inc(turned, 2)
            with pe.Fori(0, NH // HB) as i:
                def scores(n):
                    j, t = divmod(n, TT)
                    if t == 0:
                        pe.wait_ge(q_loaded[j], i * 48 + 48)
                    pe.wait_ge(biased, i * NS + (n + 1))
                    for half in range(2):
                        ins = nc.tensor.matmul(ps_s[:, n % 2, half * HALF:(half + 1) * HALF], qT[:, j, t * P:(t + 1) * P],
                                               kT[:, j, half * HALF:(half + 1) * HALF], start=True, stop=True)
                    ins.then_inc(score_done, 1)

                def turn(n):
                    pe.wait_ge(exp_done, i * NS + (n + 3))
                    pe.wait_ge(copied_lo, i * NS + (n + 1))
                    pe.wait_ge(copied_hi, i * NS + (n + 1))
                    for k in range(TT):
                        ins = nc.tensor.transpose(ps_t[:, k * P:(k + 1) * P], pr[:, n % 2, k * P:(k + 1) * P], ident[:, :])
                    ins.then_inc(turned, 1)

                def weigh(n):
                    j, t = divmod(n, TT)
                    pe.wait_ge(copied_lo, i * NS + (n + 2))
                    pe.wait_ge(copied_hi, i * NS + (n + 2))
                    pe.wait_ge(y_done, i * NS + (n + 1))
                    for k in range(TT):
                        ins = nc.tensor.matmul(ps_o[:, n % 2, 0:HD], prT[:, n % 2, k * P:(k + 1) * P], v[:, j, k, :],
                                               start=(k == 0), stop=(k == TT - 1))
                    ins.then_inc(out_done, 1)

                scores(0)
                for n in range(NS):
                    if n + 1 < NS:
                        scores(n + 1)
                    if n >= 1:
                        weigh(n - 1)
                    turn(n)
                weigh(NS - 1)

        @block.vector
        def _(dve):
            dve.wait_ge(bias_loaded, 16)
            dve.sem_inc(biased, 2)
            dve.sem_inc(copied_lo, 1)
            dve.sem_inc(y_done, 2)
            with dve.Fori(0, NH // HB) as i:
                def bias_step(n):
                    t = n % TT
                    dve.wait_ge(score_done, i * NS + (n + 1))
                    dve.wait_ge(exp_done, i * NS + (n + 1))
                    dve.sem_inc(begun, 1)
                    nc.vector.tensor_tensor_reduce(out=sc[:, n % 2, :], in0=ps_s[:, n % 2, :], in1=bias[:, OFF - t * P:OFF - t * P + S],
                                                   scale=-1.0 / 8, scalar=3.0e38, op0=ALU.add, op1=ALU.min,
                                                   accum_out=lowest[:, n:n + 1]).then_inc(biased, 1)

                def copy_step(n):
                    dve.wait_ge(turned, i * NS + (n + 3))
                    dve.wait_ge(out_done, i * NS + (n + 1))
                    nc.vector.tensor_copy(prT[:, n % 2, 0:HALF], ps_t[:, 0:HALF]).then_inc(copied_lo, 1)

                def out_step(n):
                    j, t = divmod(n, TT)
                    dve.wait_ge(exp_done, i * NS + (n + 3))
                    nc.vector.reciprocal(rden[:, n:n + 1], den[:, n:n + 1]).then_inc(rden_done, 1)
                    dve.wait_ge(rden_done, i * NS + (n + 1))
                    dve.wait_ge(out_done, i * NS + (n + 3))
                    if t == 0:
                        dve.wait_ge(stored[j % 2], i * (16 * HB // 2) + 16 * (j // 2) + 16)
                    nc.vector.tensor_scalar(y[:, j % 2, t, :], ps_o[:, n % 2, 0:HD], rden[:, n:n + 1], None, ALU.mult).then_inc(y_done, 1)

                bias_step(0)
                for n in range(NS):
                    if n + 1 < NS:
                        bias_step(n + 1)
                    if n >= 1:
                        out_step(n - 1)
                    copy_step(n)
                out_step(NS - 1)

        @block.scalar
        def _(act):
            act.sem_inc(exp_done, 2)
            act.sem_inc(copied_hi, 1)
            with act.Fori(0, NH // HB) as i:
                def exp_step(n):
                    act.wait_ge(biased, i * NS + (n + 3))
                    act.wait_ge(turned, i * NS + (n + 1))
                    nc.scalar.activation(pr[:, n % 2, :], sc[:, n % 2, :], ACT.Exp, bias=lowest[:, n:n + 1], scale=-1.0,
                                         accum_out=den[:, n:n + 1]).then_inc(exp_done, 1)

                def copy_step(n):
                    act.wait_ge(turned, i * NS + (n + 3))
                    act.wait_ge(out_done, i * NS + (n + 1))
                    nc.scalar.activation(prT[:, n % 2, HALF:S], ps_t[:, HALF:S], ACT.Copy).then_inc(copied_hi, 1)

                exp_step(0)
                for n in range(NS):
                    if n + 1 < NS:
                        exp_step(n + 1)
                    copy_step(n)


def lora_hidden(nc, z_d, w1, a1, g1, tw, ta, tg):
    KU = WA // P
    with ExitStack() as ctx:
        s = Scope(nc, ctx, "lora")
        u = s.sb("u", [P, KU, S])
        w = s.sb("w", [P, 3, KU, P])
        ps = s.ps("ps", [P, 3, S])
        u_loaded, w_loaded, mm_done, out_done = s.sem("u_loaded"), s.sem("w_loaded"), s.sem("mm_done"), s.sem("out_done")
        block = s.block()

        @block.sync
        def _(sp):
            for d in range(2):
                for i, net in enumerate((w1, a1)):
                    sp.dma_start(w[:, i, :, d * 64:(d + 1) * 64], net[0, d].rearrange("(t p) e -> p t e", p=P)).then_inc(w_loaded, 16)
            sp.dma_start(w[:, 2], g1[0].rearrange("(t p) e -> p t e", p=P)).then_inc(w_loaded, 16)
            sp.dma_start(u[:, :, :], z_d[3 * KU:4 * KU].rearrange("t p s -> p t s")).then_inc(u_loaded, 16)

        @block.tensor
        def _(pe):
            pe.wait_ge(w_loaded, 80)
            pe.wait_ge(u_loaded, 16)
            for i in range(3):
                for half in range(2):
                    span = slice(half * HALF, (half + 1) * HALF)
                    for k in range(KU):
                        ins = nc.tensor.matmul(ps[:, i, span], w[:, i, k, :], u[:, k, span], start=(k == 0), stop=(k == KU - 1))
                ins.then_inc(mm_done, 1)

        @block.scalar
        def _(act):
            for i, (dst, f) in enumerate(((tw, ACT.Tanh), (ta, ACT.Copy), (tg, ACT.Sigmoid))):
                act.wait_ge(mm_done, i + 1)
                nc.scalar.activation(dst[:, :], ps[:, i, :], f).then_inc(out_done, 1)
            act.wait_ge(out_done, 3)


LEVELS = (2, 4, 8, 16, 32, 64)
ALPHA, RHO, NBETA, KAPPA, VAL = range(5)


def recurrent_mixer(nc, z_d, w2, a2, g2, tab, consts, tw, ta, tg, ya_d):
    KU = WA // P
    NCH = S // P
    M = NCH // 2
    vec, heads, ident = consts["vec"], consts["heads"], consts["ident"]
    W0, A0, K_K, K_A, R_K, LNW, LNB = 0, 2, 4, 5, 6, 7, 8
    with ExitStack() as ctx:
        s = Scope(nc, ctx, "rw")
        r, k, v, kk = s.sb("r", [P, S]), s.sb("k", [P, S]), s.sb("v", [P, S]), s.sb("kk", [P, S])
        w2s, a2s, g2s = s.sb("w2s", [P, P]), s.sb("a2s", [P, P]), s.sb("g2s", [P, P])
        vc = s.sb("vc", [P, 10])
        reset_row = s.sb("reset_row", [P, 2, S])
        lw = s.sb("lw", [P, 2, S])
        aa = s.sb("aa", [P, 2, S])
        cc = s.sb("cc", [P, 2, S])
        ep = s.sb("ep", [P, 2, S])
        kd = s.sb("kd", [P, 2, S])
        sqb = s.sb("sqb", [P, S])
        bon = s.sb("bon", [P, S])
        gate = s.sb("gate", [P, S])
        mids = s.sb("mids", [P, 2, NCH])
        emid = s.sb("emid", [P, 2, NCH])
        ff = s.sb("ff", [P, 2, NCH])
        ysum = s.sb("ysum", [P, 2, NCH, P])
        stat = s.sb("stat", [P, 4, 2 * NCH])
        mhalf = s.sb("mhalf", [P, 1])
        pred = s.sb("pred", [P, 2, 4 * P], U32)
        first = s.sb("first", [P, 2, 2, P], U32)
        lvl = s.sb("lvl", [P, 2, len(LEVELS), 64])
        st = [s.sb(f"st{g}", [P, 5, 2 * P]) for g in range(2)]
        rho2 = [s.sb(f"rho2{g}", [P, 2, P]) for g in range(2)]
        tok = [s.sb(f"tok{g}", [P, 4, 2, P]) for g in range(2)]
        qm = [s.sb(f"qm{g}", [P, 4, 4 * P]) for g in range(2)]
        T = [s.sb(f"T{g}", [P, 4, P]) for g in range(2)]
        U = [s.sb(f"U{g}", [P, 4, P]) for g in range(2)]
        xf = [[s.sb(f"xf{g}{i}", [P, 4, P]) for i in range(len(LEVELS))] for g in range(2)]
        mv = [s.sb(f"mv{g}", [P, 4, HD]) for g in range(2)]
        wt = [s.sb(f"wt{g}", [P, 4, P]) for g in range(2)]
        rt = [s.sb(f"rt{g}", [P, 2, P]) for g in range(2)]
        gt = [s.sb(f"gt{g}", [P, 2, HD]) for g in range(2)]
        es = [s.sb(f"es{g}", [P, 2, HD]) for g in range(2)]
        esf = [s.sb(f"esf{g}", [P, HD]) for g in range(2)]
        pb = s.ps("pb", [P, 8, 512])

        def both(name):
            return [s.sem(f"{name}{g}") for g in range(2)]

        (tab_loaded, in_loaded, vec_ready, kk_in, sq_done, ss_done, ssb_done, lora_mm, sig_done, root_done, kk_ready,
         vlink, centred, exps_done, kd_in, kd_done, cleared, ones_set) = (s.sem(n) for n in (
             "tab_loaded", "in_loaded", "vec_ready", "kk_in", "sq_done", "ss_done", "ssb_done", "lora_mm", "sig_done",
             "root_done", "kk_ready", "vlink", "centred", "exps_done", "kd_in", "kd_done", "cleared", "ones_set"))
        (kds_done, kdr_done, bonus_in, bonus_mm, bon_ready, factors, mean_out, sq2_done, pow_in, pow_done, yn_done,
         y_turned, y_scaled, y_plus, y_out, stored) = (s.sem(n) for n in (
             "kds_done", "kdr_done", "bonus_in", "bonus_mm", "bon_ready", "factors", "mean_out", "sq2_done",
             "pow_in", "pow_done", "yn_done", "y_turned", "y_scaled", "y_plus", "y_out", "stored"))
        staged, rho_done, tok_t, tok_c, q_done, qm_done, l_done, unit, tu_done = (both(n) for n in (
            "staged", "rho_done", "tok_t", "tok_c", "q_done", "qm_done", "l_done", "unit", "tu_done"))
        mv_done, mv_c, x_done, xf_done, tx_done, lev_done, w_done, w_c, rg_done, rt_done = (both(n) for n in (
            "mv_done", "mv_c", "x_done", "xf_done", "tx_done", "lev_done", "w_done", "w_c", "rg_done", "rt_done"))
        ph_done, es_done, esf_done, py_done, y_c = (both(n) for n in ("ph_done", "es_done", "esf_done", "py_done", "y_c"))
        settled = s.sem("settled")

        def settle(eng):
            eng.sem_inc(settled, 1)

        block = s.block()
        NL = len(LEVELS)
        ES = 1 + 2 * M

        def cols(t, u, g, b, which):
            return t[:, u, :].rearrange("p (q two b) -> p q two b", two=2, b=b)[:, :, which ^ g, :]

        def cols4(t, g, b, which):
            return t[:, :, :].rearrange("p u (q two b) -> p u q two b", two=2, b=b)[:, :, :, which ^ g, :]

        def quarter(bank, at, b):
            return pb[:, bank, at:at + 256].rearrange("p (u q b) -> p u q b", u=4, b=b)

        def y_bank(g, hh):
            return 2 * g + 1 if hh == 0 else 4 + 2 * g

        def tokens_of(g, m):
            return bass.ds(m * (2 * P), 2 * P) if g == 0 else bass.ds((M - 1 - m) * (2 * P), 2 * P)

        def chunks_of(g, m):
            return bass.ds(m * 2, 2) if g == 0 else bass.ds((M - 1 - m) * 2, 2)

        @block.sync
        def _(sp):
            sp.dma_start(pred[:, :, :], tab["rwkv_pred"].rearrange("g p n -> p g n")).then_inc(tab_loaded, 16)
            sp.dma_start(first[:, :, :, :], tab["rwkv_first"].rearrange("g a p n -> p g a n")).then_inc(tab_loaded, 16)
            sp.dma_start(lvl[:, :, :, :], tab["rwkv_level"].rearrange("g l p n -> p g l n")).then_inc(tab_loaded, 16)
            sp.sem_inc(stored, 16)
            with sp.Fori(0, KU) as f:
                sp.wait_ge(y_out, f + 1)
                for dst, j in ((r, 0), (k, 1), (v, 2)):
                    sp.dma_start(dst[:, :], z_d[bass.ds(f + j * KU, 1)].rearrange("o p s -> p (o s)")).then_inc(in_loaded, 16)
                for d in range(2):
                    rows = slice(d * 64, (d + 1) * 64)
                    sp.dma_start(w2s[rows, :], w2[0, d].rearrange("e (m c) -> m e c", c=P)[bass.ds(f, 1)].rearrange("o e c -> (o e) c")).then_inc(in_loaded, 16)
                    sp.dma_start(a2s[rows, :], a2[0, d].rearrange("e (m c) -> m e c", c=P)[bass.ds(f, 1)].rearrange("o e c -> (o e) c")).then_inc(in_loaded, 16)
                sp.dma_start(g2s[:, :], g2[0].rearrange("e (m c) -> m e c", c=P)[bass.ds(f, 1)].rearrange("o e c -> (o e) c")).then_inc(in_loaded, 16)
                sp.wait_ge(y_out, f + 2)
                sp.dma_start(ya_d.rearrange("(m p) s -> m p s", p=P)[bass.ds(f, 1)].rearrange("o p s -> (o p) s"), sqb[:, :]).then_inc(stored, 16)
            sp.wait_ge(stored, 16 + 16 * KU)

        @block.scalar
        def _(act):
            A = nc.scalar.activation
            for g in range(2):
                act.sem_inc(y_c[g], 1)
            with act.Fori(0, KU) as f:
                act.wait_ge(vec_ready, f + 1)
                for n, (dst, bank, bias) in enumerate(((lw[:, 0, :], 2, W0), (aa[:, 0, :], 4, A0), (lw[:, 1, :], 6, W0 + 1),
                                                       (aa[:, 1, :], 0, A0 + 1))):
                    act.wait_ge(lora_mm, f * 5 + (n + 1))
                    A(dst, pb[:, bank:bank + 2, :].rearrange("p a n -> p (a n)"), ACT.Sigmoid, bias=vc[:, bias:bias + 1]).then_inc(sig_done, 1)
                act.wait_ge(lora_mm, f * 5 + 5)
                A(gate[:, :], pb[:, 2:4, :].rearrange("p a n -> p (a n)"), ACT.Copy).then_inc(sig_done, 1)
                act.wait_ge(ssb_done, f + 1)
                A(sqb[:, :], sqb[:, :], ACT.Sqrt).then_inc(root_done, 1)
                for d in range(2):
                    act.wait_ge(centred, f * 2 + (d + 1))
                    A(emid[:, d, :], mids[:, d, :], ACT.Exp)
                    A(ep[:, d, :], cc[:, d, :], ACT.Exp)
                    A(lw[:, d, :], lw[:, d, :], ACT.Exp)
                    A(cc[:, d, :], cc[:, d, :], ACT.Exp, scale=-1.0).then_inc(exps_done, 1)
                with act.Fori(0, M) as m:
                    it = f * M + m
                    for g in range(2):
                        act.wait_ge(tok_t[g], it + 1)
                        A(tok[g][:, :, :, :].rearrange("p a c e -> p (a c e)"),
                          pb[:, 2 * g:2 * g + 2, :].rearrange("p a n -> p (a n)"), ACT.Copy).then_inc(tok_c[g], 1)
                    for g in range(2):
                        act.wait_ge(mv_done[g], it + 1)
                        A(mv[g][:, :, :].rearrange("p u e -> p (u e)"), pb[:, 5 + 2 * g, 0:256], ACT.Copy).then_inc(mv_c[g], 1)
                    for g in range(2):
                        act.wait_ge(w_done[g], it + 2)
                        A(wt[g][:, :, :].rearrange("p u e -> p (u e)"), pb[:, 4 + 2 * g, :], ACT.Copy).then_inc(w_c[g], 1)
                    for g in range(2):
                        act.wait_ge(py_done[g], it + 1)
                        act.wait_ge(y_turned, f + 1)
                        for hh in range(2):
                            src = pb[:, y_bank(g, hh), 0:2 * HD].rearrange("p (c e) -> p c e", c=2)
                            if g == 1:
                                src = src[:, ::-1, :]
                            ins = A(ysum[:, g, chunks_of(g, m), hh * HD:(hh + 1) * HD], src, ACT.Copy)
                        ins.then_inc(y_c[g], 1)
                act.wait_ge(y_turned, f + 2)
                A(sqb[:, :], pb[:, 6:8, :].rearrange("p a n -> p (a n)"), ACT.Identity, scale=vc[:, LNW:LNW + 1],
                  bias=vc[:, LNB:LNB + 1]).then_inc(y_scaled, 1)

        @block.gpsimd
        def _(pool):
            G = nc.gpsimd
            G.memset(mhalf[:, :], -0.5)
            for g in range(2):
                G.memset(qm[g][:, :, :], 0.0)
                for x in xf[g]:
                    G.memset(x[:, :, :], 0.0)
            G.memset(reset_row[:, :, :], 1.0).then_inc(ones_set, 1)
            pool.wait_ge(ones_set, 1)
            G.memset(reset_row[:, 0, :].rearrange("p (c t) -> p c t", t=P)[:, :, 0:1], 0.0)
            G.memset(reset_row[:, 1, :].rearrange("p (c t) -> p c t", t=P)[:, :, P - 1:P], 0.0).then_inc(cleared, 1)
            pool.sem_inc(y_out, 1)
            for g in range(2):
                pool.sem_inc(rho_done[g], 1)
            with pool.Fori(0, KU) as f:
                pool.wait_ge(kk_in, f + 1)
                pool.wait_ge(stored, f * 16 + 16)
                G.tensor_tensor(sqb[:, :], kk[:, :], kk[:, :], ALU.mult).then_inc(sq_done, 1)
                for d in range(2):
                    pool.wait_ge(kd_in, f * 2 + (d + 1))
                    G.tensor_tensor(kd[:, d, :], kd[:, d, :], k[:, :], ALU.mult).then_inc(kd_done, 1)
                pool.wait_ge(kd_done, f * 2 + 2)
                G.tensor_tensor(bon[:, :], kd[:, 0, :], kd[:, 1, :], ALU.add).then_inc(kds_done, 1)
                pool.wait_ge(kds_done, f + 1)
                G.tensor_tensor(bon[:, :], bon[:, :], r[:, :], ALU.mult).then_inc(kdr_done, 1)
                pool.wait_ge(exps_done, f * 2 + 2)
                pool.wait_ge(factors, f + 1)
                settle(pool)
                with pool.Fori(0, M) as m:
                    it = f * M + m
                    for g in range(2):
                        pool.wait_ge(l_done[g], it + 1)
                        pool.wait_ge(rho_done[g], it + 1)
                        settle(pool)
                        span = tokens_of(g, m)
                        for i, (x, y) in enumerate(((kk[:, span], lw[:, g, span]), (r[:, span], ep[:, g, span]),
                                                    (aa[:, g, span], cc[:, g, span]), (kd[:, g, span], cc[:, g, span]))):
                            G.tensor_tensor(st[g][:, i, :], x, y, ALU.mult)
                        G.tensor_copy(st[g][:, VAL, :], v[:, span]).then_inc(staged[g], 1)
                    for g in range(2):
                        pool.wait_ge(w_done[g], it + 1)
                        settle(pool)
                        for c in range(4):
                            G.tensor_copy(T[g][:, c, :], ident[:, :])
                            ins = G.tensor_copy(U[g][:, c, :], ident[:, :])
                        ins.then_inc(unit[g], 1)
                    for g in range(2):
                        pool.wait_ge(staged[g], it + 1)
                        pool.wait_ge(rt_done[g], it + 1)
                        settle(pool)
                        src = st[g][:, RHO, :].rearrange("p (c t) -> p c t", c=2)
                        if g == 1:
                            src = src[:, ::-1, :]
                        G.tensor_copy(rho2[g][:, :, :], src).then_inc(rho_done[g], 1)
                pool.wait_ge(mean_out, f + 1)
                G.tensor_tensor(ysum[:, 1], ysum[:, 0], ysum[:, 0], ALU.mult).then_inc(sq2_done, 1)
                pool.wait_ge(pow_in, f + 1)
                G.tensor_tensor(stat[:, 3, :], stat[:, 2, :], mhalf[:, 0:1].broadcast_to([P, 2 * NCH]), ALU.pow).then_inc(pow_done, 1)
                pool.wait_ge(bon_ready, f + 1)
                pool.wait_ge(y_scaled, f + 1)
                G.tensor_tensor(sqb[:, :], sqb[:, :], bon[:, :], ALU.add).then_inc(y_plus, 1)
                pool.wait_ge(y_plus, f + 1)
                G.tensor_tensor(sqb[:, :], sqb[:, :], gate[:, :], ALU.mult).then_inc(y_out, 1)

        VLINKS = 2 + 1 + 2 * 6 + 4

        @block.vector
        def _(dve):
            V = nc.vector
            ch = Chain(dve, vlink)
            dve.wait_ge(tab_loaded, 48)
            dve.wait_ge(cleared, 1)
            for g in range(2):
                dve.sem_inc(rt_done[g], 1)
            with dve.Fori(0, KU) as f:
                ch.turn(f, VLINKS)
                dve.wait_ge(in_loaded, f * 128 + 128)
                ch.link(V.tensor_copy(vc[:, 0:9], vec[:, :, bass.ds(f, 1)].rearrange("p a o -> p (a o)")))
                V.tensor_scalar(vc[:, 9:10], vc[:, K_A:K_A + 1], -1.0, 1.0, ALU.mult, ALU.add).then_inc(vec_ready, 1)
                dve.wait_ge(vec_ready, f + 1)
                V.tensor_scalar(kk[:, :], k[:, :], vc[:, K_K:K_K + 1], None, ALU.mult).then_inc(kk_in, 1)
                dve.wait_ge(ss_done, f + 1)
                V.tensor_scalar(sqb[:, :], pb[:, 0:2, :].rearrange("p a n -> p (a n)"), L2_EPS, None, ALU.add).then_inc(ssb_done, 1)
                for d in range(2):
                    dve.wait_ge(sig_done, f * 5 + (2 * d + 2))
                    V.tensor_scalar(kd[:, d, :], aa[:, d, :], vc[:, K_A:K_A + 1], vc[:, 9:10], ALU.mult, ALU.add).then_inc(kd_in, 1)
                    ch.link(V.tensor_scalar(lw[:, d, :], lw[:, d, :], DECAY, None, ALU.mult))
                    o = slice(None) if d == 0 else slice(None, None, -1)
                    ch.link(V.tensor_tensor_scan(cc[:, d, o], reset_row[:, d, o], lw[:, d, o], 0.0, ALU.mult, ALU.add))
                    c3 = cc[:, d, :].rearrange("p (c t) -> p c t", t=P)
                    ch.link(V.tensor_copy(mids[:, d, :], c3[:, :, P // 2]))
                    ch.link(V.tensor_tensor(c3, c3, mids[:, d, :].unsqueeze(2).broadcast_to([P, NCH, P]), ALU.subtract))
                    V.tensor_tensor(lw[:, d, :], cc[:, d, :], lw[:, d, :], ALU.subtract).then_inc(centred, 1)
                dve.wait_ge(root_done, f + 1)
                ch.link(V.reciprocal(sqb[:, :], sqb[:, :]))
                dve.wait_ge(sq_done, f + 1)
                V.tensor_tensor(kk[:, :], kk[:, :], sqb[:, :], ALU.mult).then_inc(kk_ready, 1)
                dve.wait_ge(kk_ready, f + 1)
                for d in range(2):
                    dve.wait_ge(kd_in, f * 2 + (d + 1))
                    ch.link(V.scalar_tensor_tensor(aa[:, d, :], kk[:, :], -1.0, aa[:, d, :], ALU.mult, ALU.mult))
                dve.wait_ge(kdr_done, f + 1)
                V.tensor_scalar(bon[:, :], bon[:, :], vc[:, R_K:R_K + 1], None, ALU.mult).then_inc(bonus_in, 1)
                dve.wait_ge(exps_done, f * 2 + 2)
                e0 = ep[:, 0, :].rearrange("p (c t) -> p c t", t=P)[:, :, P - 1]
                e1 = ep[:, 1, :].rearrange("p (c t) -> p c t", t=P)[:, ::-1, 0]
                m1 = emid[:, 1, ::-1]
                ch.link(V.tensor_tensor(ff[:, 0, 0:NCH - 1], e0[:, 0:NCH - 1], emid[:, 0, 1:NCH], ALU.mult))
                ch.link(V.tensor_copy(ff[:, 0, NCH - 1:NCH], e0[:, NCH - 1:NCH]))
                ch.link(V.tensor_tensor(ff[:, 1, 0:NCH - 1], e1[:, 0:NCH - 1], m1[:, 1:NCH], ALU.mult))
                V.tensor_copy(ff[:, 1, NCH - 1:NCH], e1[:, NCH - 1:NCH]).then_inc(factors, 1)
                for g in range(2):
                    V.memset(es[g][:, 0, :], 0.0).then_inc(es_done[g], 1)
                dve.wait_ge(bonus_mm, f + 1)
                V.tensor_tensor(bon[:, :], pb[:, 4:6, :].rearrange("p a n -> p (a n)"), v[:, :], ALU.mult).then_inc(bon_ready, 1)
                dve.wait_ge(factors, f + 1)
                settle(dve)
                with dve.Fori(0, M) as m:
                    it = f * M + m
                    for p in range(2):
                        for g in range(2):
                            dve.wait_ge(q_done[g], it * 2 + (p + 1))
                            settle(dve)
                            V.copy_predicated(qm[g][:, 2 * p:2 * p + 2, :], pred[:, g:g + 1, :].broadcast_to([P, 2, 4 * P]),
                                              pb[:, 2 * g:2 * g + 2, :]).then_inc(qm_done[g], 1)
                    for g in range(2):
                        dve.wait_ge(unit[g], it + 1)
                        dve.wait_ge(qm_done[g], it * 2 + 2)
                        dve.wait_ge(l_done[g], it + 2)
                        settle(dve)
                        for hh in range(2):
                            V.copy_predicated(T[g][:, hh::2, :], first[:, g, 0:1, :].broadcast_to([P, 2, P]),
                                              pb[:, 4 + 2 * g + hh, 0:2 * P].rearrange("p (c n) -> p c n", c=2))
                        V.copy_predicated(U[g][:, :, :], first[:, g, 1:2, :].broadcast_to([P, 4, P]),
                                          qm[g][:, :, 0:P]).then_inc(tu_done[g], 1)
                    for i, b in enumerate(LEVELS):
                        for g in range(2):
                            dve.wait_ge(x_done[g], it * NL + (i + 1))
                            mask = lvl[:, g, i, :].rearrange("p (u q b) -> p u q b", u=1, b=b).broadcast_to([P, 4, 64 // b, b])
                            V.tensor_tensor(cols4(xf[g][i], g, b, 0), quarter(4 + 2 * g, 0, b), mask, ALU.mult).then_inc(xf_done[g], 1)
                        for g in range(2):
                            dve.wait_ge(tx_done[g], it * NL + (i + 1))
                            if i < NL - 1:
                                tv = cols4(T[g], g, b, 0)
                                V.tensor_tensor(tv, quarter(4 + 2 * g, 256, b), tv, ALU.add)
                            uv = cols4(U[g], g, b, 1)
                            V.tensor_tensor(uv, quarter(5 + 2 * g, 0, b), uv, ALU.add).then_inc(lev_done[g], 1)
                    for g in range(2):
                        dve.wait_ge(rho_done[g], it + 2)
                        dve.wait_ge(rg_done[g], it + 1)
                        V.tensor_tensor(rt[g][:, :, :].rearrange("p c t -> p (c t)"), pb[:, 5 + 2 * g, 0:256],
                                        rho2[g][:, :, :].rearrange("p c t -> p (c t)"), ALU.add)
                        V.tensor_copy(gt[g][:, :, :].rearrange("p c t -> p (c t)"), pb[:, 5 + 2 * g, 256:384]).then_inc(rt_done[g], 1)
                    for c in range(2):
                        for g in range(2):
                            step = bass.ds(m * 2 + c, 1)
                            dve.wait_ge(es_done[g], f * ES + m * 2 + (c + 1))
                            V.tensor_scalar(esf[g][:, :], es[g][:, c, :], ff[:, g, step], None, ALU.mult).then_inc(esf_done[g], 1)
                            dve.wait_ge(esf_done[g], it * 2 + (c + 1))
                            dve.wait_ge(ph_done[g], it * 2 + (c + 1))
                            V.scalar_tensor_tensor(es[g][:, 1 - c, :], pb[:, 2 * g, c * HD:(c + 1) * HD], ff[:, g, step],
                                                   esf[g][:, :], ALU.mult, ALU.add).then_inc(es_done[g], 1)
                for g in range(2):
                    dve.wait_ge(y_c[g], f * M + (M + 1))
                y0 = ysum[:, 0].rearrange("p c (h e) -> p (c h) e", h=2)
                y1 = ysum[:, 1].rearrange("p c (h e) -> p (c h) e", h=2)
                ch.link(V.tensor_tensor(y0, y0, y1, ALU.add))
                ch.link(V.tensor_reduce(stat[:, 0, :], y0, AX.X, ALU.add))
                ch.link(V.tensor_scalar(stat[:, 0, :], stat[:, 0, :], 1.0 / HD, None, ALU.mult))
                V.tensor_tensor(y0, y0, stat[:, 0, :].unsqueeze(2).broadcast_to([P, 2 * NCH, HD]), ALU.subtract).then_inc(mean_out, 1)
                dve.wait_ge(sq2_done, f + 1)
                ch.link(V.tensor_reduce(stat[:, 1, :], y1, AX.X, ALU.add))
                V.tensor_scalar(stat[:, 2, :], stat[:, 1, :], 1.0 / HD, LNX_EPS, ALU.mult, ALU.add).then_inc(pow_in, 1)
                dve.wait_ge(pow_done, f + 1)
                V.tensor_tensor(y0, y0, stat[:, 3, :].unsqueeze(2).broadcast_to([P, 2 * NCH, HD]), ALU.mult).then_inc(yn_done, 1)
                assert ch.n == VLINKS, ch.n

        @block.tensor
        def _(pe):
            mm = nc.tensor.matmul
            for g in range(2):
                pe.sem_inc(l_done[g], 1)
                pe.sem_inc(w_done[g], 1)
            pe.sem_inc(y_turned, 1)

            def wide(bank, lhs, rhs):
                for half in range(2):
                    ins = mm(pb[:, bank + half, :], lhs, rhs[:, half * HALF:(half + 1) * HALF], start=True, stop=True)
                return ins

            with pe.Fori(0, KU) as f:
                pe.wait_ge(in_loaded, f * 128 + 128)
                wide(2, w2s[0:64, :], tw[0:64, :]).then_inc(lora_mm, 1)
                wide(4, a2s[0:64, :], ta[0:64, :]).then_inc(lora_mm, 1)
                wide(6, w2s[64:P, :], tw[64:P, :]).then_inc(lora_mm, 1)
                pe.wait_ge(sq_done, f + 1)
                wide(0, heads[:, :], sqb[:, :]).then_inc(ss_done, 1)
                pe.wait_ge(ssb_done, f + 1)
                wide(0, a2s[64:P, :], ta[64:P, :]).then_inc(lora_mm, 1)
                pe.wait_ge(sig_done, f * 5 + 1)
                wide(2, g2s[:, :], tg[:, :]).then_inc(lora_mm, 1)
                pe.wait_ge(bonus_in, f + 1)
                wide(4, heads[:, :], bon[:, :]).then_inc(bonus_mm, 1)
                pe.wait_ge(sig_done, f * 5 + 5)
                pe.wait_ge(bon_ready, f + 1)
                settle(pe)
                with pe.Fori(0, M) as m:
                    it = f * M + m

                    def head_rows(u):
                        return slice((u % 2) * HD, (u % 2 + 1) * HD)

                    def staged_cols(g, c):
                        return slice((c ^ g) * P, ((c ^ g) + 1) * P)

                    for g in range(2):
                        pe.wait_ge(staged[g], it + 1)
                        pe.wait_ge(y_c[g], it + 1)
                        pe.wait_ge(es_done[g], f * ES + m * 2 + 1)
                        for a, i in enumerate((ALPHA, NBETA, KAPPA, VAL)):
                            for c in range(2):
                                n = a * 2 + c
                                ins = nc.tensor.transpose(pb[:, 2 * g + n // 4, (n % 4) * P:(n % 4 + 1) * P],
                                                          st[g][:, i, staged_cols(g, c)], ident[:, :])
                        ins.then_inc(tok_t[g], 1)
                    for p in range(2):
                        for g in range(2):
                            if p == 0:
                                pe.wait_ge(tok_c[g], it + 1)
                            else:
                                pe.wait_ge(qm_done[g], it * 2 + 1)
                            for hh in range(2):
                                u = 2 * p + hh
                                rows, c = head_rows(u), staged_cols(g, p)
                                moving = st[g][rows, ALPHA:RHO + 1, c]
                                mm(pb[:, 2 * g + hh, 0:2 * P], st[g][rows, NBETA, c], moving, start=True, stop=True)
                                ins = mm(pb[:, 2 * g + hh, 2 * P:4 * P], st[g][rows, KAPPA, c], moving, start=True, stop=True)
                            ins.then_inc(q_done[g], 1)
                    for g in range(2):
                        for u in range(4):
                            rows, c = head_rows(u), staged_cols(g, u // 2)
                            ins = mm(pb[:, 4 + 2 * g + u % 2, u // 2 * P:(u // 2 + 1) * P], st[g][rows, ALPHA, c], st[g][rows, NBETA, c],
                                     start=True, stop=True)
                        ins.then_inc(l_done[g], 1)
                    for g in range(2):
                        pe.wait_ge(qm_done[g], it * 2 + 2)
                        pe.wait_ge(tu_done[g], it + 1)
                        for u in range(4):
                            ins = mm(pb[:, 5 + 2 * g, u * HD:(u + 1) * HD], qm[g][:, u, 2 * P:3 * P],
                                     tok[g][:, 3, u // 2, head_rows(u)], start=True, stop=True)
                        ins.then_inc(mv_done[g], 1)
                    for i, b in enumerate(LEVELS):
                        for g in range(2):
                            if i == 0:
                                pe.wait_ge(tu_done[g], it + 1)
                            else:
                                pe.wait_ge(lev_done[g], it * NL + i)
                            for u in range(4):
                                ins = mm(pb[:, 4 + 2 * g, u * 64:(u + 1) * 64], qm[g][:, u, 0:P], cols(T[g], u, g, b, 0), start=True, stop=True)
                            ins.then_inc(x_done[g], 1)
                        for g in range(2):
                            if i == 0:
                                pe.wait_ge(mv_c[g], it + 1)
                            pe.wait_ge(xf_done[g], it * NL + (i + 1))
                            for u in range(4):
                                if i < NL - 1:
                                    mm(pb[:, 4 + 2 * g, 256 + u * 64:256 + (u + 1) * 64], U[g][:, u, :], cols(xf[g][i], u, g, b, 0), start=True, stop=True)
                                ins = mm(pb[:, 5 + 2 * g, u * 64:(u + 1) * 64], xf[g][i][:, u, :], cols(U[g], u, g, b, 1), start=True, stop=True)
                            ins.then_inc(tx_done[g], 1)
                    for g in range(2):
                        pe.wait_ge(lev_done[g], it * NL + NL)
                        for u in range(4):
                            mm(pb[:, 4 + 2 * g, u * P:u * P + HD], U[g][:, u, :], tok[g][:, 0, u // 2, head_rows(u)], start=True, stop=True)
                            ins = mm(pb[:, 4 + 2 * g, u * P + HD:(u + 1) * P], U[g][:, u, :], mv[g][:, u, :], start=True, stop=True)
                        ins.then_inc(w_done[g], 1)
                    for g in range(2):
                        pe.wait_ge(w_c[g], it + 1)
                        for u in range(4):
                            rows, c = head_rows(u), u // 2
                            mm(pb[rows, 5 + 2 * g, c * P:(c + 1) * P], wt[g][:, u, 0:HD], qm[g][:, u, P:2 * P], start=True, stop=True)
                            ins = mm(pb[rows, 5 + 2 * g, 256 + c * HD:256 + (c + 1) * HD], wt[g][:, u, 0:HD], tok[g][:, 1, c, rows], start=True, stop=True)
                        ins.then_inc(rg_done[g], 1)
                    for c in range(2):
                        for g in range(2):
                            pe.wait_ge(rt_done[g], it + 2)
                            pe.wait_ge(es_done[g], f * ES + m * 2 + (c + 1))
                            for hh in range(2):
                                u = 2 * c + hh
                                rows = head_rows(u)
                                o = pb[rows, 2 * g, c * HD:(c + 1) * HD]
                                mm(o, tok[g][:, 2, c, rows], tok[g][:, 3, c, rows], start=True, stop=False)
                                mm(o, tok[g][:, 1, c, rows], wt[g][:, u, HD:P], start=False, stop=False)
                                ins = mm(o, gt[g][rows, c, :], es[g][rows, c, :], start=False, stop=True)
                            ins.then_inc(ph_done[g], 1)
                        for g in range(2):
                            for hh in range(2):
                                u = 2 * c + hh
                                rows = head_rows(u)
                                o = pb[:, y_bank(g, hh), c * HD:(c + 1) * HD]
                                mm(o, qm[g][:, u, 3 * P:4 * P], tok[g][:, 3, c, rows], start=True, stop=False)
                                mm(o, qm[g][:, u, P:2 * P], wt[g][:, u, HD:P], start=False, stop=False)
                                ins = mm(o, rt[g][rows, c, :], es[g][rows, c, :], start=False, stop=True)
                            if c == 1:
                                ins.then_inc(py_done[g], 1)
                pe.wait_ge(yn_done, f + 1)
                for c in range(NCH):
                    ins = nc.tensor.transpose(pb[:, 6 + c // 4, (c % 4) * P:(c % 4 + 1) * P], ysum[:, 0, c, :], ident[:, :])
                ins.then_inc(y_turned, 1)


def gather_mixed(nc, ya_d, yb_d, consts, y_hi, y_lo):
    ident = consts["ident"]
    KU = WA // P
    with ExitStack() as ctx:
        s = Scope(nc, ctx, "gather")
        ya = s.sb("ya", [P, KU, S])
        yb = s.sb("yb", [P, TT, WA])
        y32 = s.sb("y32", [P, KU, S])
        ps = s.ps("ps", [P, 4, HALF])
        a_loaded, b_loaded, turned, copied, hi_done, lo_done = (s.sem(n) for n in (
            "a_loaded", "b_loaded", "turned", "copied", "hi_done", "lo_done"))
        block = s.block()

        @block.sync
        def _(sp):
            sp.dma_start(yb[:, :, :], yb_d.rearrange("(t p) n -> p t n", p=P)).then_inc(b_loaded, 16)
            sp.dma_start(ya[:, :, :], ya_d.rearrange("(t p) s -> p t s", p=P)).then_inc(a_loaded, 16)

        @block.tensor
        def _(pe):
            pe.wait_ge(b_loaded, 16)
            for n in range(2 * KU):
                f, half = divmod(n, 2)
                if n >= 4:
                    pe.wait_ge(copied, n - 3)
                for t in range(4):
                    ins = nc.tensor.transpose(ps[:, n % 4, t * P:(t + 1) * P], yb[:, half * 4 + t, f * P:(f + 1) * P], ident[:, :])
                ins.then_inc(turned, 1)

        @block.vector
        def _(dve):
            for n in range(2 * KU):
                f, half = divmod(n, 2)
                dve.wait_ge(turned, n + 1)
                nc.vector.tensor_copy(y32[:, f, half * HALF:(half + 1) * HALF], ps[:, n % 4, :]).then_inc(copied, 1)

        @block.scalar
        def _(act):
            act.wait_ge(a_loaded, 16)
            for f in range(KU):
                nc.scalar.activation(y_hi[:, f, :], ya[:, f, :], ACT.Copy).then_inc(hi_done, 1)
            for f in range(KU):
                act.wait_ge(copied, 2 * f + 2)
                nc.scalar.activation(y_hi[:, KU + f, :], y32[:, f, :], ACT.Copy).then_inc(hi_done, 1)

        @block.gpsimd
        def _(pool):
            for f in range(2 * KU):
                pool.wait_ge(hi_done, f + 1)
                src = ya[:, f, :] if f < KU else y32[:, f - KU, :]
                nc.gpsimd.tensor_tensor(y_lo[:, f, :], src, y_hi[:, f, :].bitcast(F32), ALU.subtract).then_inc(lo_done, 1)


def output_product(nc, name, w_rows, a_hi, a_lo, y):
    w_v = w_rows.rearrange("(t p) n -> t p n", p=P)
    with ExitStack() as ctx:
        s = Scope(nc, ctx, name)
        w_raw = s.sb("w_raw", [P, 3, D])
        w_hi = s.sb("w_hi", [P, KT, D], F32R)
        w_lo = s.sb("w_lo", [P, KT, D], F32R)
        ps = s.ps("ps", [P, 4, HALF])
        raw_loaded = [s.sem(f"raw_loaded{j}") for j in range(3)]
        hi_done, lo_done, mm_done, y_done = s.sem("hi_done"), s.sem("lo_done"), s.sem("mm_done"), s.sem("y_done")
        block = s.block()

        @block.sync
        def _(sp):
            for k in range(KT):
                if k >= 3:
                    sp.wait_ge(lo_done, k - 2)
                sp.dma_start(w_raw[:, k % 3, :], w_v[k]).then_inc(raw_loaded[k % 3], 16)

        @block.scalar
        def _(act):
            for k in range(KT):
                act.wait_ge(raw_loaded[k % 3], 16 * (k // 3 + 1))
                nc.scalar.activation(w_hi[:, k, :], w_raw[:, k % 3, :], ACT.Copy).then_inc(hi_done, 1)

        @block.gpsimd
        def _(pool):
            for k in range(KT):
                pool.wait_ge(hi_done, k + 1)
                nc.gpsimd.tensor_tensor(w_lo[:, k, :], w_raw[:, k % 3, :], w_hi[:, k, :].bitcast(F32), ALU.subtract).then_inc(lo_done, 1)

        @block.vector
        def _(dve):
            for n in range(2 * TT):
                t, half = divmod(n, 2)
                dve.wait_ge(mm_done, n + 1)
                nc.vector.tensor_copy(y[:, t, half * HALF:(half + 1) * HALF], ps[:, n % 4, :]).then_inc(y_done, 1)

        @block.tensor
        def _(pe):
            for n in range(2 * TT):
                t, half = divmod(n, 2)
                span = slice(half * HALF, (half + 1) * HALF)
                if n >= 4:
                    pe.wait_ge(y_done, n - 3)
                for k in range(KT):
                    if n == 0:
                        pe.wait_ge(lo_done, k + 1)
                    ins = split_products(nc, ps[:, n % 4, :], a_hi[:, k, t * P:(t + 1) * P], a_lo[:, k, t * P:(t + 1) * P],
                                         w_hi[:, k, span], w_lo[:, k, span], k == 0, k == KT - 1)
                ins.then_inc(mm_done, 1)


def residual(nc, name, y, x_src, gate_row, norm_row, x_dst):
    with ExitStack() as ctx:
        s = Scope(nc, ctx, name)
        x = s.sb("x", [P, TT, D])
        sq = s.sb("sq", [P, D])
        gate = s.sb("gate", [P, D])
        norm = s.sb("norm", [P, D])
        ss = s.sb("ss", [P, TT])
        ms = s.sb("ms", [P, TT])
        rstd = s.sb("rstd", [P, TT])
        mhalf = s.sb("mhalf", [P, 1])
        x_loaded = [s.sem(f"x_loaded{t}") for t in range(TT)]
        row_loaded, gain_done, half_done, ss_done, ms_done, rstd_done, scaled, x_done, stored = (s.sem(n) for n in (
            "row_loaded", "gain_done", "half_done", "ss_done", "ms_done", "rstd_done", "scaled", "x_done", "stored"))
        block = s.block()

        @block.sync
        def _(sp):
            sp.dma_start(gate[:, :], gate_row.rearrange("(o n) -> o n", o=1).broadcast_to([P, D])).then_inc(row_loaded, 16)
            sp.dma_start(norm[:, :], norm_row.rearrange("(o n) -> o n", o=1).broadcast_to([P, D])).then_inc(row_loaded, 16)
            for t in range(TT):
                sp.dma_start(x[:, t, :], x_src[t * P:(t + 1) * P, :]).then_inc(x_loaded[t], 16)
            for t in range(TT):
                sp.wait_ge(x_done, t + 1)
                sp.dma_start(x_dst[t * P:(t + 1) * P, :], x[:, t, :]).then_inc(stored, 16)
            sp.wait_ge(stored, 16 * TT)

        @block.scalar
        def _(act):
            for t in range(TT):
                if t:
                    act.wait_ge(ss_done, t)
                nc.scalar.activation(sq[:, :], y[:, t, :], ACT.Square, accum_out=ss[:, t:t + 1]).then_inc(ss_done, 1)

        @block.gpsimd
        def _(pool):
            nc.gpsimd.memset(mhalf[:, :], -0.5).then_inc(half_done, 1)
            pool.wait_ge(half_done, 1)
            for q in range(2):
                span = slice(4 * q, 4 * q + 4)
                pool.wait_ge(ms_done, q + 1)
                nc.gpsimd.tensor_tensor(rstd[:, span], ms[:, span], mhalf[:, 0:1].broadcast_to([P, 4]), ALU.pow).then_inc(rstd_done, 1)
            for t in range(TT):
                pool.wait_ge(scaled, t + 1)
                pool.wait_ge(x_loaded[t], 16)
                nc.gpsimd.tensor_tensor(x[:, t, :], x[:, t, :], y[:, t, :], ALU.add).then_inc(x_done, 1)

        @block.vector
        def _(dve):
            dve.wait_ge(row_loaded, 32)
            nc.vector.tensor_tensor(gate[:, :], gate[:, :], norm[:, :], ALU.mult).then_inc(gain_done, 1)
            for q in range(2):
                span = slice(4 * q, 4 * q + 4)
                dve.wait_ge(ss_done, 4 * q + 4)
                nc.vector.tensor_scalar(ms[:, span], ss[:, span], 1.0 / D, RMS_EPS, ALU.mult, ALU.add).then_inc(ms_done, 1)
            dve.wait_ge(gain_done, 1)
            for t in range(TT):
                dve.wait_ge(rstd_done, t // 4 + 1)
                nc.vector.scalar_tensor_tensor(y[:, t, :], y[:, t, :], rstd[:, t:t + 1], gate[:, :], ALU.mult, ALU.mult).then_inc(scaled, 1)


def conv_glu(nc, name, l, up_w, down_w, conv_cols, h_hi, h_lo, y):
    NG = FT // 2
    up_v = up_w.rearrange("(t p) (m c) -> m p t c", p=P, c=P)
    down_v = down_w.rearrange("(m p) n -> m p n", p=P)
    with ExitStack() as ctx:
        s = Scope(nc, ctx, name)
        u_raw = s.sb("u_raw", [P, 4, KT, P])
        u_hi = s.sb("u_hi", [P, 2, KT, P], F32R)
        u_lo = s.sb("u_lo", [P, 2, KT, P], F32R)
        d_raw = s.sb("d_raw", [P, 2, D])
        d_hi = s.sb("d_hi", [P, 2, D], F32R)
        d_lo = s.sb("d_lo", [P, 2, D], F32R)
        z = s.sb("z", [P, 4, S])
        a_hi = s.sb("a_hi", [P, 2, S], F32R)
        a_lo = s.sb("a_lo", [P, 2, S], F32R)
        ps_u = s.ps("ps_u", [P, 2, S])
        ps_d = s.ps("ps_d", [P, 4, HALF])
        u_loaded = [s.sem(f"u_loaded{j}") for j in range(4)]
        d_loaded = [s.sem(f"d_loaded{j}") for j in range(2)]
        (uhi_done, ulo_done, umm_done, mid_done, left_done, conv_done, gelu_done, glu_done, ahi_done, alo_done, dhi_done,
         dlo_done, share_done, added, zeroed) = (s.sem(n) for n in (
             "uhi_done", "ulo_done", "umm_done", "mid_done", "left_done", "conv_done", "gelu_done", "glu_done", "ahi_done",
             "alo_done", "dhi_done", "dlo_done", "share_done", "added", "zeroed"))
        block = s.block()

        def tile_of(g, j):
            return g * 2 + (j // 2 + (j % 2) * FT)

        @block.sync
        def _(sp):
            def load_up(g, j):
                sp.dma_start(u_raw[:, j], up_v[bass.ds(tile_of(g, j), 1)].rearrange("o p t c -> p (o t) c")).then_inc(u_loaded[j], 16)

            def load_down(g, j):
                sp.dma_start(d_raw[:, j, :], down_v[bass.ds(g * 2 + j, 1)].rearrange("o p n -> p (o n)")).then_inc(d_loaded[j], 16)

            for j in range(4):
                load_up(0, j)
            for j in range(2):
                load_down(0, j)
            with sp.Fori(0, NG - 1) as g:
                for j in range(4):
                    sp.wait_ge(ulo_done, g * 4 + (j + 1))
                    load_up(g + 1, j)
                for j in range(2):
                    sp.wait_ge(dlo_done, g * 2 + (j + 1))
                    load_down(g + 1, j)

        @block.scalar
        def _(act):
            A = nc.scalar.activation

            def split(g, j):
                act.wait_ge(u_loaded[j], g * 16 + 16)
                act.wait_ge(umm_done, g * 4 + (j + 1))
                A(u_hi[:, j % 2], u_raw[:, j], ACT.Copy).then_inc(uhi_done, 1)

            def split_down(g):
                act.wait_ge(share_done, g * (2 * TT) + 1)
                for j in range(2):
                    act.wait_ge(d_loaded[j], g * 16 + 16)
                    A(d_hi[:, j, :], d_raw[:, j, :], ACT.Copy).then_inc(dhi_done, 1)

            def middle(g, j):
                act.wait_ge(umm_done, g * 4 + (j + 3))
                act.wait_ge(alo_done, g * 2 + (j // 2 + 1))
                A(z[:, j, :], ps_u[:, j % 2, :], ACT.Copy, scale=conv_cols[:, 1, bass.ds(tile_of(g, j), 1)]).then_inc(mid_done, 1)

            def gelu(g, p):
                act.wait_ge(conv_done, g * 4 + (2 * p + 3))
                A(z[:, 2 * p, :], z[:, 2 * p, :], ACT.Gelu_apprx_tanh).then_inc(gelu_done, 1)
                act.wait_ge(glu_done, g * 2 + (p + 1))
                act.wait_ge(share_done, g * (2 * TT) + 1)
                A(a_hi[:, p, :], z[:, 2 * p, :], ACT.Copy).then_inc(ahi_done, 1)

            def turn(g, last):
                split(g, 1)
                middle(g, 0)
                split(g, 2)
                middle(g, 1)
                gelu(g, 0)
                split_down(g)
                split(g, 3)
                middle(g, 2)
                if not last:
                    split(g + 1, 0)
                middle(g, 3)
                gelu(g, 1)

            split(0, 0)
            with act.Fori(0, NG - 1) as g:
                turn(g, False)
            turn(NG - 1, True)

        @block.gpsimd
        def _(pool):
            G = nc.gpsimd

            def split(g, j):
                pool.wait_ge(uhi_done, g * 4 + (j + 1))
                G.tensor_tensor(u_lo[:, j % 2], u_raw[:, j], u_hi[:, j % 2].bitcast(F32), ALU.subtract).then_inc(ulo_done, 1)

            def split_down(g):
                for j in range(2):
                    pool.wait_ge(dhi_done, g * 2 + (j + 1))
                    G.tensor_tensor(d_lo[:, j, :], d_raw[:, j, :], d_hi[:, j, :].bitcast(F32), ALU.subtract).then_inc(dlo_done, 1)

            def split_product(g, p):
                pool.wait_ge(ahi_done, g * 2 + (p + 1))
                G.tensor_tensor(a_lo[:, p, :], z[:, 2 * p, :], a_hi[:, p, :].bitcast(F32), ALU.subtract).then_inc(alo_done, 1)

            def turn(g, last):
                split(g, 1)
                split(g, 2)
                split_product(g, 0)
                split_down(g)
                split(g, 3)
                if not last:
                    split(g + 1, 0)
                split_product(g, 1)

            pool.sem_inc(alo_done, 2)
            split(0, 0)
            with pool.Fori(0, NG - 1) as g:
                turn(g, False)
            turn(NG - 1, True)

        @block.vector
        def _(dve):
            V = nc.vector

            def convolve(g, j):
                dve.wait_ge(mid_done, g * 4 + (j + 1))
                V.scalar_tensor_tensor(z[:, j, 1:S], ps_u[:, j % 2, 0:S - 1], conv_cols[:, 0, bass.ds(tile_of(g, j), 1)],
                                       z[:, j, 1:S], ALU.mult, ALU.add).then_inc(left_done, 1)
                dve.wait_ge(left_done, g * 4 + (j + 1))
                V.scalar_tensor_tensor(z[:, j, 0:S - 1], ps_u[:, j % 2, 1:S], conv_cols[:, 2, bass.ds(tile_of(g, j), 1)],
                                       z[:, j, 0:S - 1], ALU.mult, ALU.add).then_inc(conv_done, 1)

            def product(g, p):
                dve.wait_ge(conv_done, g * 4 + (2 * p + 4))
                dve.wait_ge(gelu_done, g * 2 + (p + 1))
                V.tensor_tensor(z[:, 2 * p, :], z[:, 2 * p, :], z[:, 2 * p + 1, :], ALU.mult).then_inc(glu_done, 1)

            def add_share(g):
                for n in range(2 * TT):
                    t, half = divmod(n, 2)
                    dst = y[:, t, half * HALF:(half + 1) * HALF]
                    dve.wait_ge(share_done, g * (2 * TT) + (n + 2))
                    V.tensor_tensor(dst, ps_d[:, n % 4, :], dst, ALU.add).then_inc(added, 1)

            def rest(g):
                convolve(g, 1)
                product(g, 0)
                convolve(g, 2)
                convolve(g, 3)
                product(g, 1)

            V.memset(y[:, :, :], 0.0).then_inc(zeroed, 1)
            dve.sem_inc(conv_done, 2)
            dve.sem_inc(added, 4)
            dve.wait_ge(zeroed, 1)
            convolve(0, 0)
            with dve.Fori(0, NG - 1) as g:
                rest(g)
                convolve(g + 1, 0)
                add_share(g)
            rest(NG - 1)
            add_share(NG - 1)

        @block.tensor
        def _(pe):
            def up(g, j):
                pe.wait_ge(ulo_done, g * 4 + (j + 1))
                pe.wait_ge(conv_done, g * 4 + (j + 1))
                for half in range(2):
                    span = slice(half * HALF, (half + 1) * HALF)
                    for k in range(KT):
                        ins = split_products(nc, ps_u[:, j % 2, span], u_hi[:, j % 2, k, :], u_lo[:, j % 2, k, :],
                                             h_hi[:, k, span], h_lo[:, k, span], k == 0, k == KT - 1)
                ins.then_inc(umm_done, 1)

            def share(g):
                pe.wait_ge(dlo_done, g * 2 + 2)
                pe.wait_ge(alo_done, g * 2 + 4)
                for n in range(2 * TT):
                    t, half = divmod(n, 2)
                    span = slice(half * HALF, (half + 1) * HALF)
                    pe.wait_ge(added, g * (2 * TT) + (n + 1))
                    for p in range(2):
                        ins = split_products(nc, ps_d[:, n % 4, :], a_hi[:, p, t * P:(t + 1) * P], a_lo[:, p, t * P:(t + 1) * P],
                                             d_hi[:, p, span], d_lo[:, p, span], p == 0, p == 1)
                    ins.then_inc(share_done, 1)

            pe.sem_inc(umm_done, 2)
            pe.sem_inc(share_done, 1)
            up(0, 0)
            with pe.Fori(0, NG - 1) as g:
                for j in range(1, 4):
                    up(g, j)
                up(g + 1, 0)
                share(g)
            for j in range(1, 4):
                up(NG - 1, j)
            share(NG - 1)


def fourier(nc, tab, h_hi, h_lo):
    GR = KT
    H = S // 2
    with ExitStack() as ctx:
        s = Scope(nc, ctx, "fft")
        raw = s.sb("raw", [P, 4, H])
        fe_raw = s.sb("fe_raw", [P, 2 * P])
        al_raw = s.sb("al_raw", [P, TT, 2])
        fe_hi, fe_lo = s.sb("fe_hi", [P, 2 * P], F32R), s.sb("fe_lo", [P, 2 * P], F32R)
        al_hi, al_lo = s.sb("al_hi", [P, TT, 2], F32R), s.sb("al_lo", [P, TT, 2], F32R)
        tk_hi, tk_lo = s.sb("tk_hi", [P, 2, TT, H], F32R), s.sb("tk_lo", [P, 2, TT, H], F32R)
        uv_hi, uv_lo = s.sb("uv_hi", [P, 2, TT, 2, P], F32R), s.sb("uv_lo", [P, 2, TT, 2, P], F32R)
        e = s.sb("e", [P, H + 2])
        f32 = s.sb("f32", [P, S])
        ps_uv = s.ps("uv", [P, TT // 2, 512])
        ps_e, ps_o, ps_m = s.ps("pe", [P, H]), s.ps("po", [P, H]), s.ps("pm", [P, 512])
        NR = 2 * TT
        small_loaded, small_hi, small_lo = s.sem("small_loaded"), s.sem("small_hi"), s.sem("small_lo")
        raw_loaded = [s.sem(f"raw_loaded{j}") for j in range(4)]
        tk_hi_done, tk_lo_done, uv_mm, uv_hi_done, uv_lo_done = (s.sem(n) for n in (
            "tk_hi_done", "tk_lo_done", "uv_mm", "uv_hi_done", "uv_lo_done"))
        e_mm, o_mm, e_copied, f_done, f_hi_done, f_lo_done = (s.sem(n) for n in (
            "e_mm", "o_mm", "e_copied", "f_done", "f_hi_done", "f_lo_done"))
        block = s.block()
        tok_v = tab["fft_tokens"].rearrange("a (t p) k -> a t p k", p=P)

        @block.sync
        def _(sp):
            sp.dma_start(fe_raw[:, :], tab["fft_features"]).then_inc(small_loaded, 16)
            sp.dma_start(al_raw[:, :, :], tab["fft_middle"].rearrange("(t p) k -> p t k", p=P)).then_inc(small_loaded, 16)
            for n in range(NR):
                a, t = divmod(n, TT)
                if n >= 4:
                    sp.wait_ge(tk_lo_done, n - 3)
                sp.dma_start(raw[:, n % 4, :], tok_v[a, t]).then_inc(raw_loaded[n % 4], 16)

        @block.scalar
        def _(act):
            A = nc.scalar.activation
            act.wait_ge(small_loaded, 32)
            A(fe_hi[:, :], fe_raw[:, :], ACT.Copy)
            A(al_hi[:, :, :], al_raw[:, :, :], ACT.Copy).then_inc(small_hi, 1)

            def split_tables(lo, hi):
                for n in range(lo, hi):
                    a, t = divmod(n, TT)
                    act.wait_ge(raw_loaded[n % 4], 16 * (n // 4 + 1))
                    A(tk_hi[:, a, t, :], raw[:, n % 4, :], ACT.Copy).then_inc(tk_hi_done, 1)

            def split_uv(g):
                for q in range(TT // 2):
                    act.wait_ge(uv_mm, g * (TT // 2) + q + 1)
                    dst = uv_hi[:, g % 2, 2 * q:2 * q + 2].rearrange("p t a e -> p (t a e)")
                    A(dst, ps_uv[:, q, :], ACT.Copy).then_inc(uv_hi_done, 1)

            split_tables(0, TT)
            split_uv(0)
            split_tables(TT, NR)
            for g in range(GR):
                act.wait_ge(e_mm, g + 1)
                if g:
                    act.wait_ge(f_done, g)
                A(e[:, 0:H], ps_e[:, :], ACT.Copy)
                A(e[:, H:H + 2], ps_m[:, 0:2], ACT.Copy).then_inc(e_copied, 1)
                if g + 1 < GR:
                    split_uv(g + 1)
                act.wait_ge(f_done, g + 1)
                A(h_hi[:, g, :], f32[:, :], ACT.Copy).then_inc(f_hi_done, 1)

        @block.gpsimd
        def _(pool):
            G = nc.gpsimd
            pool.wait_ge(small_hi, 1)
            G.tensor_tensor(fe_lo[:, :], fe_raw[:, :], fe_hi[:, :].bitcast(F32), ALU.subtract)
            G.tensor_tensor(al_lo[:, :, :], al_raw[:, :, :], al_hi[:, :, :].bitcast(F32), ALU.subtract).then_inc(small_lo, 1)
            for n in range(NR):
                a, t = divmod(n, TT)
                pool.wait_ge(tk_hi_done, n + 1)
                G.tensor_tensor(tk_lo[:, a, t, :], raw[:, n % 4, :], tk_hi[:, a, t, :].bitcast(F32), ALU.subtract).then_inc(tk_lo_done, 1)
            for g in range(GR):
                pool.wait_ge(f_hi_done, g + 1)
                G.tensor_tensor(h_lo[:, g, :], f32[:, :], h_hi[:, g, :].bitcast(F32), ALU.subtract).then_inc(f_lo_done, 1)

        @block.vector
        def _(dve):
            V = nc.vector

            def split_uv(g):
                for q in range(TT // 2):
                    n = g * (TT // 2) + q
                    dve.wait_ge(uv_hi_done, n + 1)
                    hi = uv_hi[:, g % 2, 2 * q:2 * q + 2].rearrange("p t a e -> p (t a e)")
                    lo = uv_lo[:, g % 2, 2 * q:2 * q + 2].rearrange("p t a e -> p (t a e)")
                    V.tensor_tensor(lo, ps_uv[:, q, :], hi.bitcast(F32), ALU.subtract).then_inc(uv_lo_done, 1)

            split_uv(0)
            for g in range(GR):
                if g + 1 < GR:
                    split_uv(g + 1)
                dve.wait_ge(o_mm, g + 1)
                dve.wait_ge(e_copied, g + 1)
                if g:
                    dve.wait_ge(f_lo_done, g)
                V.tensor_tensor(f32[:, 0:H], e[:, 0:H], ps_o[:, :], ALU.subtract)
                V.tensor_tensor(f32[:, :H:-1], e[:, 1:H], ps_o[:, 1:H], ALU.add)
                V.tensor_copy(f32[:, H:H + 1], e[:, H:H + 1]).then_inc(f_done, 1)

        @block.tensor
        def _(pe):
            def over_features(g):
                for t in range(TT):
                    if t % 2 == 0 and g:
                        pe.wait_ge(uv_lo_done, (g - 1) * (TT // 2) + t // 2 + 1)
                    out = ps_uv[:, t // 2, (t % 2) * 2 * P:(t % 2 + 1) * 2 * P]
                    ins = split_products(nc, out, h_hi[:, g, t * P:(t + 1) * P], h_lo[:, g, t * P:(t + 1) * P], fe_hi[:, :], fe_lo[:, :], True, True)
                    if t % 2 == 1:
                        ins.then_inc(uv_mm, 1)

            def over_tokens(g, a, out):
                for t in range(TT):
                    if g == 0:
                        pe.wait_ge(tk_lo_done, a * TT + t + 1)
                    ins = split_products(nc, out, uv_hi[:, g % 2, t, a, :], uv_lo[:, g % 2, t, a, :], tk_hi[:, a, t, :], tk_lo[:, a, t, :],
                                         t == 0, t == TT - 1)
                return ins

            pe.wait_ge(small_lo, 1)
            over_features(0)
            for g in range(GR):
                pe.wait_ge(uv_lo_done, (g + 1) * (TT // 2))
                if g:
                    pe.wait_ge(e_copied, g)
                over_tokens(g, 0, ps_e[:, :])
                for t in range(TT):
                    ins = split_products(nc, ps_m[:, 0:2], uv_hi[:, g % 2, t, 0, :], uv_lo[:, g % 2, t, 0, :], al_hi[:, t, :], al_lo[:, t, :],
                                         t == 0, t == TT - 1)
                ins.then_inc(e_mm, 1)
                if g + 1 < GR:
                    over_features(g + 1)
                if g:
                    pe.wait_ge(f_done, g)
                over_tokens(g, 1, ps_o[:, :]).then_inc(o_mm, 1)


SCRATCH = {
    "mod": (2, 6 * D),
    "qk": (2, WA, S),
    "v": (S, WA),
    "z": (4 * WA // P, P, S),
    "ya": (WA, S),
    "yb": (S, WA),
    "x1": (S, D),
    "x2": (S, D),
    "x3": (S, D),
}


def tables():
    half = HD // 2
    inv = (np.float32(10000.0) ** (-np.arange(half, dtype=np.float32) / np.float32(half))).astype(np.float32)
    ang = np.arange(S, dtype=np.float32)[:, None] * inv[None, :]
    cos, sin = np.cos(ang), np.sin(ang)
    away = np.arange(2 * S - P)[None, :] - np.arange(P)[:, None] - (S - P)
    n = (np.abs(away) <= 64) * 1 + ((np.abs(away) <= 256) & (away % 4 == 0)) + (away % 16 == 0)
    bias = np.where(n > 0, 8.0 * np.log(np.maximum(n, 1)), NEG_BIG).astype(np.float32)
    row, col = np.arange(P)[:, None], np.arange(P)[None, :]
    pred, first, level = [], [], []
    for g in range(2):
        before = (row < col) if g == 0 else (row > col)
        upto = before | (row == col)
        pred.append(np.concatenate([before, upto, before, upto], 1))
        pair = (row // 2 == col // 2)
        first.append(np.stack([pair & before.T, pair & before]))
        lv = []
        for b in LEVELS:
            c = np.arange(64)[None, :] // b
            lv.append((row // (2 * b) == c) & ((row // b) % 2 == 1 - g))
        level.append(np.stack(lv))
    k = np.arange(S)[:, None] * np.arange(S // 2)[None, :] % S * (2 * np.pi / S)
    q = np.arange(P)[:, None] * np.arange(P)[None, :] % P * (2 * np.pi / P)
    features = np.concatenate([np.cos(q), np.sin(q)], 1) / np.sqrt(float(S * P))
    middle = np.repeat(np.where(np.arange(S) % 2 == 0, 1.0, -1.0)[:, None], 2, 1)
    return {
        "fft_tokens": np.stack([np.cos(k), np.sin(k)]).astype(np.float32),
        "fft_features": features.astype(np.float32),
        "fft_middle": middle.astype(np.float32),
        "att_bias": bias,
        "rwkv_pred": np.stack(pred).astype(np.uint32),
        "rwkv_first": np.stack(first).astype(np.uint32),
        "rwkv_level": np.stack(level).astype(np.float32),
        "rope_cos": np.concatenate([cos, cos], 1).astype(np.float32),
        "rope_sin": np.concatenate([-sin, sin], 1).astype(np.float32),
    }


def glu_layer(nc, l, a, mod, consts, x_src, x_dst, y):
    with ExitStack() as ctx:
        hs = Scope(nc, ctx, f"g{l}")
        h_hi, h_lo = hs.sb("hi", [P, KT, S], F32R), hs.sb("lo", [P, KT, S], F32R)
        norm_to_features(nc, f"ng{l}", x_src, a["norm_g"][l, 2], mod[l], 3 * D, consts, h_hi, h_lo)
        conv_glu(nc, f"cg{l}", l, a["ffn_up"][l], a["ffn_down"][l], consts["conv_f"][:, l], h_hi, h_lo, y)
    residual(nc, f"rg{l}", y, x_src, mod[l, 5 * D:6 * D], a["norm_g"][l, 3], x_dst)


def build(nc, a, tab, out, dbg=()):
    scr = {n: nc.dram_tensor(f"scr_{n}", shape, F32, kind="ExternalOutput" if n in dbg else "Internal").ap()
           for n, shape in SCRATCH.items()}
    x0 = a["x"][0]
    with ExitStack() as ctx:
        top = Scope(nc, ctx, "top")
        consts = {
            "ident": top.sb("ident", [P, P]),
            "heads": top.sb("heads", [P, P]),
            "conv_a": top.sb("conv_a", [P, 3, 4 * WA // P]),
            "conv_f": top.sb("conv_f", [P, 2, 3, 2 * FT]),
            "vec": top.sb("vec", [P, 9, 4]),
        }
        make_constants(nc, consts)
        groups = [(a["mix_conv"][0].rearrange("w (m p) -> (w m) p", p=P), consts["conv_a"][:, :, :].rearrange("p w m -> p (w m)"))]
        for l in range(2):
            for w in range(3):
                groups.append((a["ffn_conv"][l, w].rearrange("(m p) -> m p", p=P), consts["conv_f"][:, l, w, :]))
        vecs = [a["rwkv_w0"][0, 0], a["rwkv_w0"][0, 1], a["rwkv_a0"][0, 0], a["rwkv_a0"][0, 1], a["rwkv_k_k"][0], a["rwkv_k_a"][0],
                a["rwkv_r_k"][0].rearrange("h e -> (h e)"), a["rwkv_lnx_w"][0], a["rwkv_lnx_b"][0]]
        for i, v in enumerate(vecs):
            groups.append((v.rearrange("(m p) -> m p", p=P), consts["vec"][:, i, :]))
        load_columns(nc, groups, consts)
        modulation(nc, a["c"], a["ada_w"], a["ada_b"], scr["mod"])
        with ExitStack() as hctx:
            hs = Scope(nc, hctx, "h0")
            h_hi, h_lo = hs.sb("hi", [P, KT, S], F32R), hs.sb("lo", [P, KT, S], F32R)
            norm_to_features(nc, "n0", x0, a["norm_g"][0, 0], scr["mod"][0], 0, consts, h_hi, h_lo)
            project_qkv(nc, a["mix_in"], h_hi, h_lo, consts, tab["rope_cos"], tab["rope_sin"], scr["qk"], scr["v"])
            project_convolved(nc, a["mix_in"], consts["conv_a"], h_hi, h_lo, scr["z"])
        with ExitStack() as actx:
            dilated_attention(nc, scr["qk"], scr["v"], tab["att_bias"], consts, scr["yb"])
        with ExitStack() as rctx:
            rs = Scope(nc, rctx, "lt")
            tw, ta, tg = (rs.sb(n, [P, S]) for n in ("tw", "ta", "tg"))
            lora_hidden(nc, scr["z"], a["rwkv_w1"], a["rwkv_a1"], a["rwkv_g1"], tw, ta, tg)
            recurrent_mixer(nc, scr["z"], a["rwkv_w2"], a["rwkv_a2"], a["rwkv_g2"], tab, consts, tw, ta, tg, scr["ya"])
        mod = scr["mod"]

        def gate(l, i):
            return mod[l, i * D:(i + 1) * D]

        with ExitStack() as yctx:
            y = Scope(nc, yctx, "y0").sb("y", [P, TT, D])
            with ExitStack() as hctx:
                hs = Scope(nc, hctx, "m0")
                m_hi, m_lo = hs.sb("hi", [P, KT, S], F32R), hs.sb("lo", [P, KT, S], F32R)
                gather_mixed(nc, scr["ya"], scr["yb"], consts, m_hi, m_lo)
                output_product(nc, "mo", a["mix_out"][0], m_hi, m_lo, y)
            residual(nc, "r0", y, x0, gate(0, 2), a["norm_g"][0, 1], scr["x1"])
            glu_layer(nc, 0, a, mod, consts, scr["x1"], scr["x2"], y)
        with ExitStack() as hctx:
            hs = Scope(nc, hctx, "f1")
            h_hi, h_lo = hs.sb("hi", [P, KT, S], F32R), hs.sb("lo", [P, KT, S], F32R)
            norm_to_features(nc, "n2", scr["x2"], a["norm_g"][1, 0], mod[1], 0, consts, h_hi, h_lo)
            fourier(nc, tab, h_hi, h_lo)
            y = hs.sb("y", [P, TT, D])
            output_product(nc, "fo", a["fnet_w"][0], h_hi, h_lo, y)
            residual(nc, "r2", y, scr["x2"], gate(1, 2), a["norm_g"][1, 1], scr["x3"])
        with ExitStack() as yctx:
            y = Scope(nc, yctx, "y1").sb("y", [P, TT, D])
            glu_layer(nc, 1, a, mod, consts, scr["x3"], out[0], y)


def kernel(**inputs):
    import numpy as _np
    import concourse.bacc as _bacc
    from concourse import mybir as _mybir
    from concourse.bass_utils import run_bass_kernel_spmd as _run

    nc = _bacc.Bacc("TRN2", target_bir_lowering=False, num_devices=1)
    arrays = {f"in_{n}": _np.ascontiguousarray(a) for n, a in inputs.items()}
    arrays.update({f"table_{n}": a for n, a in tables().items()})
    aps = {n: nc.dram_tensor(n, a.shape, _mybir.dt.from_np(a.dtype), kind="ExternalInput").ap() for n, a in arrays.items()}
    out = nc.dram_tensor("out_0", (1, S, D), F32, kind="ExternalOutput").ap()
    build(nc, {n[3:]: a for n, a in aps.items() if n.startswith("in_")},
          {n[6:]: a for n, a in aps.items() if n.startswith("table_")}, out)
    r = _run(nc, [arrays], core_ids=[0])
    return r.results[0]["out_0"]
```

```python
from contextlib import ExitStack
import math

import numpy as np
import concourse.bass as bass
from concourse import mybir

F32 = mybir.dt.float32
F32R = mybir.dt.float32r
U32 = mybir.dt.uint32
ALU = mybir.AluOpType
ACT = mybir.ActivationFunctionType
AX = mybir.AxisListType

P = 128
D = 1024
S = 1024
KT = D // P
TT = S // P
HALF = 512
HD = 64
NH = 8
WA = NH * HD
DFF = ((8 * D // 3 + 127) // 128) * 128
FT = DFF // P
CHUNK = 512
RMS_EPS = 1e-6
LNX_EPS = 64e-5
L2_EPS = 1e-12
DECAY = -math.exp(-0.5)
NEG_BIG = -1e30


class Scope:

    def __init__(self, nc, ctx, name):
        self.nc, self.ctx, self.name = nc, ctx, name
        self.sems = []

    def sb(self, name, shape, dt=F32):
        return self.ctx.enter_context(self.nc.sbuf_tensor(f"{self.name}_{name}", shape, dt))

    def ps(self, name, shape, dt=F32):
        return self.ctx.enter_context(self.nc.psum_tensor(f"{self.name}_{name}", shape, dt))

    def sem(self, name):
        self.sems.append(self.nc.alloc_semaphore(f"{self.name}_{name}"))
        return self.sems[-1]

    def block(self):
        def end():
            self.nc.clear_and_free_semaphores(self.sems)
            self.nc.all_engine_barrier()

        self.ctx.callback(end)
        return self.ctx.enter_context(self.nc.Block())


class Chain:

    def __init__(self, eng, sem):
        self.eng, self.sem, self.n, self.base = eng, sem, 0, 0

    def link(self, ins):
        self.n += 1
        ins.then_inc(self.sem, 1)
        self.eng.wait_ge(self.sem, self.base + self.n)

    def turn(self, i, steps):
        self.base, self.n = i * steps, 0


def modulation(nc, c, ada_w, ada_b, mod_d):
    L = ada_w.shape[0]
    per = 6 * D // CHUNK
    R = 4
    with ExitStack() as ctx:
        s = Scope(nc, ctx, "mod")
        w = s.sb("w", [P, R, KT, CHUNK])
        acc = s.sb("acc", [P, R, CHUNK])
        ccol = s.sb("ccol", [P, KT])
        sig = s.sb("sig", [P, KT])
        sc = s.sb("sc", [P, KT])
        brow = s.sb("brow", [1, R, CHUNK])
        row = s.sb("row", [1, R, CHUNK])
        ones = s.sb("ones", [P, 1])
        ps = s.ps("ps", [P, R, CHUNK])
        c_loaded, sig_done, sc_done, ones_done = s.sem("c_loaded"), s.sem("sig_done"), s.sem("sc_done"), s.sem("ones_done")
        w_loaded = [s.sem(f"w_loaded{j}") for j in range(R)]
        b_loaded = [s.sem(f"b_loaded{j}") for j in range(R)]
        row_stored = [s.sem(f"row_stored{j}") for j in range(R)]
        acc_done, sum_done, row_done, link = s.sem("acc_done"), s.sem("sum_done"), s.sem("row_done"), s.sem("link")
        settled = s.sem("settled")
        block = s.block()
        NB = per // R

        def chunk(vector, e):
            return vector.rearrange("(e n) -> e n", n=CHUNK)[bass.ds(e, 1)]

        @block.sync
        def _(sp):
            sp.dma_start(ccol[:, :], c.rearrange("o (t p) -> p (o t)", p=P), allow_slow_non_contiguous=True).then_inc(c_loaded, 16)
            for l in range(L):
                with sp.Fori(0, NB) as i:
                    for j in range(R):
                        n = l * per + i * R + j
                        sp.wait_ge(acc_done, n + 1)
                        sp.sem_inc(settled, 1)
                        src = ada_w[l].rearrange("(t p) (e n) -> e p t n", p=P, n=CHUNK)[bass.ds(i * R + j, 1)]
                        sp.dma_start(w[:, j], src.rearrange("o p t n -> p (o t) n")).then_inc(w_loaded[j], 16)

        @block.gpsimd
        def _(pool):
            for l in range(L):
                with pool.Fori(0, NB) as i:
                    for j in range(R):
                        pool.wait_ge(sum_done, l * per + i * R + (j + 1))
                        pool.dma_start(brow[:, j, :], chunk(ada_b[l], i * R + j)).then_inc(b_loaded[j], 16)

        @block.scalar
        def _(act):
            act.wait_ge(c_loaded, 16)
            nc.scalar.activation(sig[:, :], ccol[:, :], ACT.Sigmoid).then_inc(sig_done, 1)
            for j in range(R):
                act.sem_inc(row_stored[j], 16)
            act.sem_inc(row_done, R)
            for l in range(L):
                with act.Fori(0, NB) as i:
                    for j in range(R):
                        n = l * per + i * R + j
                        act.wait_ge(sum_done, n + (R + 1))
                        act.wait_ge(row_stored[j], (i + l * NB) * 16 + 16)
                        nc.scalar.activation(row[:, j, :], ps[0:1, j, :], ACT.Copy).then_inc(row_done, 1)
                        act.wait_ge(row_done, n + (R + 1))
                        act.dma_start(chunk(mod_d[l], i * R + j), row[:, j, :]).then_inc(row_stored[j], 16)
            for j in range(R):
                act.wait_ge(row_stored[j], 16 + 16 * L * NB)

        @block.vector
        def _(dve):
            V = nc.vector
            V.memset(ones[:, :], 1.0).then_inc(ones_done, 1)
            dve.wait_ge(sig_done, 1)
            V.tensor_tensor(sc[:, :], ccol[:, :], sig[:, :], ALU.mult).then_inc(sc_done, 1)
            dve.wait_ge(sc_done, 1)
            dve.sem_inc(acc_done, R)
            links = 2 * (KT - 1)
            for l in range(L):
                with dve.Fori(0, NB) as i:
                    body = i + l * NB
                    for pair in range(R // 2):
                        for t in range(KT):
                            for q in range(2):
                                j = pair * 2 + q
                                if t == 0:
                                    dve.wait_ge(w_loaded[j], body * 16 + 16)
                                    dve.wait_ge(sum_done, body * R + (j + 1))
                                    ins = V.tensor_scalar(acc[:, j, :], w[:, j, 0, :], sc[:, 0:1], None, ALU.mult)
                                else:
                                    dve.wait_ge(link, body * (R // 2 * links) + (pair * links + 2 * t + q - 1))
                                    ins = V.scalar_tensor_tensor(acc[:, j, :], w[:, j, t, :], sc[:, t:t + 1], acc[:, j, :],
                                                                 ALU.mult, ALU.add)
                                ins.then_inc(link if t < KT - 1 else acc_done, 1)

        @block.tensor
        def _(pe):
            pe.wait_ge(ones_done, 1)
            pe.sem_inc(sum_done, R)
            for l in range(L):
                with pe.Fori(0, NB) as i:
                    for j in range(R):
                        n = l * per + i * R + j
                        pe.wait_ge(acc_done, n + (R + 1))
                        pe.wait_ge(b_loaded[j], (i + l * NB) * 16 + 16)
                        pe.wait_ge(row_done, n + 1)
                        nc.tensor.matmul(ps[0:1, j, :], ones[:, :], acc[:, j, :], start=True, stop=False)
                        nc.tensor.matmul(ps[0:1, j, :], ones[0:1, :], brow[:, j, :], start=False, stop=True).then_inc(sum_done, 1)


def norm_to_features(nc, name, x_src, norm_row, mod_row, at, consts, h_hi, h_lo):
    ident = consts["ident"]
    with ExitStack() as ctx:
        s = Scope(nc, ctx, name)
        x = s.sb("x", [P, TT, D])
        sq = s.sb("sq", [P, D])
        ss = s.sb("ss", [P, TT])
        ms = s.sb("ms", [P, TT])
        rstd = s.sb("rstd", [P, TT])
        mhalf = s.sb("mhalf", [P, 1])
        g = s.sb("g", [P, KT])
        scale = s.sb("scale", [P, KT])
        shift = s.sb("shift", [P, KT])
        gain = s.sb("gain", [P, KT])
        h32 = s.sb("h32", [P, 4, HALF])
        ps = s.ps("ps", [P, 4, HALF])
        x_loaded = [s.sem(f"x_loaded{t}") for t in range(TT)]
        col_loaded, gain_done, half_done = s.sem("col_loaded"), s.sem("gain_done"), s.sem("half_done")
        ss_done, ms_done, rstd_done, xs_done = s.sem("ss_done"), s.sem("ms_done"), s.sem("rstd_done"), s.sem("xs_done")
        turned, h32_done, hi_done = s.sem("turned"), s.sem("h32_done"), s.sem("hi_done")
        pool_lo, dve_lo = s.sem("pool_lo"), s.sem("dve_lo")
        link_sem = s.sem("link")
        block = s.block()
        steps = [(half, f) for half in range(2) for f in range(KT)]

        @block.sync
        def _(sp):
            for t in range(TT):
                sp.dma_start(x[:, t, :], x_src[t * P:(t + 1) * P, :]).then_inc(x_loaded[t], 16)
            sp.dma_start(g[:, :], norm_row.rearrange("(t p) -> p t", p=P), allow_slow_non_contiguous=True).then_inc(col_loaded, 16)
            sp.dma_start(shift[:, :], mod_row[at:at + D].rearrange("(t p) -> p t", p=P), allow_slow_non_contiguous=True).then_inc(col_loaded, 16)
            sp.dma_start(scale[:, :], mod_row[at + D:at + 2 * D].rearrange("(t p) -> p t", p=P), allow_slow_non_contiguous=True).then_inc(col_loaded, 16)

        @block.scalar
        def _(act):
            for t in range(TT):
                act.wait_ge(x_loaded[t], 16)
                if t:
                    act.wait_ge(ss_done, t)
                nc.scalar.activation(sq[:, :], x[:, t, :], ACT.Square, accum_out=ss[:, t:t + 1]).then_inc(ss_done, 1)
            for n, (half, f) in enumerate(steps):
                act.wait_ge(h32_done, n + 1)
                nc.scalar.activation(h_hi[:, f, half * HALF:(half + 1) * HALF], h32[:, n % 4, :], ACT.Copy).then_inc(hi_done, 1)

        @block.gpsimd
        def _(pool):
            nc.gpsimd.memset(mhalf[:, :], -0.5).then_inc(half_done, 1)
            pool.wait_ge(half_done, 1)
            pool.wait_ge(ms_done, 1)
            nc.gpsimd.tensor_tensor(rstd[:, :], ms[:, :], mhalf[:, 0:1].broadcast_to([P, TT]), ALU.pow).then_inc(rstd_done, 1)
            for n, (half, f) in enumerate(steps):
                if n % 4 == 3:
                    continue
                pool.wait_ge(h32_done, n + 1)
                pool.wait_ge(hi_done, n + 1)
                span = slice(half * HALF, (half + 1) * HALF)
                nc.gpsimd.tensor_tensor(h_lo[:, f, span], h32[:, n % 4, :], h_hi[:, f, span].bitcast(F32),
                                        ALU.subtract).then_inc(pool_lo, 1)

        @block.vector
        def _(dve):
            def low_part(n):
                half, f = steps[n]
                span = slice(half * HALF, (half + 1) * HALF)
                dve.wait_ge(hi_done, n + 1)
                nc.vector.tensor_tensor(h_lo[:, f, span], h32[:, n % 4, :], h_hi[:, f, span].bitcast(F32),
                                        ALU.subtract).then_inc(dve_lo, 1)

            dve.wait_ge(col_loaded, 48)
            nc.vector.scalar_tensor_tensor(gain[:, :], scale[:, :], 1.0, g[:, :], ALU.add, ALU.mult).then_inc(gain_done, 1)
            dve.wait_ge(gain_done, 1)
            dve.wait_ge(ss_done, TT)
            nc.vector.tensor_scalar(ms[:, :], ss[:, :], 1.0 / D, RMS_EPS, ALU.mult, ALU.add).then_inc(ms_done, 1)
            dve.wait_ge(rstd_done, 1)
            for t in range(TT):
                nc.vector.tensor_scalar(x[:, t, :], x[:, t, :], rstd[:, t:t + 1], None, ALU.mult).then_inc(xs_done, 1)
            for n, (half, f) in enumerate(steps):
                dve.wait_ge(turned, n + 1)
                if n >= 4:
                    if n % 4 == 3:
                        dve.wait_ge(dve_lo, n // 4)
                    else:
                        dve.wait_ge(pool_lo, 3 * (n // 4 - 1) + n % 4 + 1)
                nc.vector.tensor_scalar(h32[:, n % 4, :], ps[:, n % 4, :], gain[:, f:f + 1], shift[:, f:f + 1],
                                        ALU.mult, ALU.add).then_inc(h32_done, 1)
                if n % 4 == 1 and n > 4:
                    low_part(n - 2)
            low_part(len(steps) - 1)

        @block.tensor
        def _(pe):
            for n, (half, f) in enumerate(steps):
                pe.wait_ge(xs_done, 4 * (half + 1))
                if n >= 4:
                    pe.wait_ge(h32_done, n - 3)
                for t in range(4):
                    ins = nc.tensor.transpose(ps[:, n % 4, t * P:(t + 1) * P], x[:, 4 * half + t, f * P:(f + 1) * P], ident[:, :])
                ins.then_inc(turned, 1)


def split_products(nc, out, a_hi, a_lo, b_hi, b_lo, first, last):
    nc.tensor.matmul(out, a_hi, b_hi, start=first, stop=False)
    nc.tensor.matmul(out, a_hi, b_lo, start=False, stop=False)
    return nc.tensor.matmul(out, a_lo, b_hi, start=False, stop=last)


def project_qkv(nc, mix_in, h_hi, h_lo, consts, rope_cos, rope_sin, qk_d, v_d):
    ident = consts["ident"]
    NC = 3
    w_v = mix_in[0].rearrange("(t p) n -> t p n", p=P)
    with ExitStack() as ctx:
        s = Scope(nc, ctx, "qkv")
        R = 4
        w_raw = s.sb("w_raw", [P, R, WA])
        w_hi = s.sb("w_hi", [P, 2, KT, WA], F32R)
        w_lo = s.sb("w_lo", [P, 2, KT, WA], F32R)
        cos = s.sb("cos", [P, TT, HD])
        sin = s.sb("sin", [P, TT, HD])
        rc = s.sb("rc", [P, 2, WA])
        rs = s.sb("rs", [P, 2, WA])
        rot = s.sb("rot", [P, 2, WA])
        stage = s.sb("stage", [P, 2, WA])
        ps = s.ps("ps", [P, 4, WA])
        pt = s.ps("pt", [P, 2, WA])
        raw_loaded = [s.sem(f"raw_loaded{j}") for j in range(R)]
        tab_loaded, hi_done, lo_done = s.sem("tab_loaded"), s.sem("hi_done"), s.sem("lo_done")
        mm_done, rc_done, rs_done, rot_done = s.sem("mm_done"), s.sem("rc_done"), s.sem("rs_done"), s.sem("rot_done")
        turned, staged = s.sem("turned"), s.sem("staged")
        stored = [s.sem(f"stored{j}") for j in range(2)]
        block = s.block()

        @block.sync
        def _(sp):
            sp.dma_start(cos[:, :, :], rope_cos.rearrange("(t p) e -> p t e", p=P)).then_inc(tab_loaded, 16)
            sp.dma_start(sin[:, :, :], rope_sin.rearrange("(t p) e -> p t e", p=P)).then_inc(tab_loaded, 16)
            for n in range(NC * KT):
                cb, k = divmod(n, KT)
                if n >= R:
                    sp.wait_ge(lo_done, n - R + 1)
                sp.dma_start(w_raw[:, n % R, :], w_v[k, :, 4 * WA + cb * WA:4 * WA + (cb + 1) * WA]).then_inc(raw_loaded[n % R], 16)

        @block.scalar
        def _(act):
            def split(cb):
                if cb >= 2:
                    act.wait_ge(mm_done, TT * (cb - 1))
                for k in range(KT):
                    n = cb * KT + k
                    act.wait_ge(raw_loaded[n % R], 16 * (n // R + 1))
                    nc.scalar.activation(w_hi[:, cb % 2, k, :], w_raw[:, n % R, :], ACT.Copy).then_inc(hi_done, 1)

            def stage_out(cb, t):
                n = cb * TT + t
                if n >= 2:
                    act.wait_ge(stored[n % 2], 16 * (n // 2))
                if cb < 2:
                    act.wait_ge(turned, n + 1)
                    nc.scalar.activation(stage[:, n % 2, :], pt[:, n % 2, :], ACT.Copy).then_inc(staged, 1)
                    act.wait_ge(staged, n + 1)
                    dst = qk_d[cb].rearrange("(f p) s -> p f s", p=P)[:, :, t * P:(t + 1) * P]
                    act.dma_start(dst, stage[:, n % 2, :].rearrange("p (f s) -> p f s", f=4)).then_inc(stored[n % 2], 16)
                else:
                    act.wait_ge(mm_done, n + 1)
                    nc.scalar.activation(stage[:, n % 2, :], ps[:, n % 4, :], ACT.Copy).then_inc(staged, 1)
                    act.wait_ge(staged, n + 1)
                    act.dma_start(v_d[t * P:(t + 1) * P, :], stage[:, n % 2, :]).then_inc(stored[n % 2], 16)

            split(0)
            split(1)
            for cb in range(NC):
                for t in range(TT):
                    stage_out(cb, t)
                if cb + 2 < NC:
                    split(cb + 2)
            for j in range(2):
                act.wait_ge(stored[j], 16 * NC * TT // 2)

        @block.gpsimd
        def _(pool):
            def split(cb):
                for k in range(KT):
                    n = cb * KT + k
                    pool.wait_ge(hi_done, n + 1)
                    nc.gpsimd.tensor_tensor(w_lo[:, cb % 2, k, :], w_raw[:, n % R, :], w_hi[:, cb % 2, k, :].bitcast(F32),
                                            ALU.subtract).then_inc(lo_done, 1)

            for cb in range(NC):
                split(cb)

        @block.vector
        def _(dve):
            dve.wait_ge(tab_loaded, 32)
            for cb in range(2):
                for t in range(TT):
                    n = cb * TT + t
                    src = ps[:, n % 4, :].rearrange("p (h e) -> p h e", h=NH)
                    c = rc[:, n % 2, :].rearrange("p (h e) -> p h e", h=NH)
                    z = rs[:, n % 2, :].rearrange("p (h e) -> p h e", h=NH)
                    cb_t = cos[:, t:t + 1, :].broadcast_to([P, NH, HD])
                    lo_t = sin[:, t:t + 1, 0:HD // 2].broadcast_to([P, NH, HD // 2])
                    hi_t = sin[:, t:t + 1, HD // 2:HD].broadcast_to([P, NH, HD // 2])
                    dve.wait_ge(mm_done, n + 1)
                    nc.vector.tensor_tensor(c, src, cb_t, ALU.mult).then_inc(rc_done, 1)
                    nc.vector.tensor_tensor(z[:, :, 0:HD // 2], src[:, :, HD // 2:HD], lo_t, ALU.mult)
                    nc.vector.tensor_tensor(z[:, :, HD // 2:HD], src[:, :, 0:HD // 2], hi_t, ALU.mult).then_inc(rs_done, 1)
                    dve.wait_ge(rc_done, n + 1)
                    dve.wait_ge(rs_done, n + 1)
                    if n >= 2:
                        dve.wait_ge(turned, n - 1)
                    nc.vector.tensor_tensor(rot[:, n % 2, :], rc[:, n % 2, :], rs[:, n % 2, :], ALU.add).then_inc(rot_done, 1)

        @block.tensor
        def _(pe):
            def turn(n):
                pe.wait_ge(rot_done, n + 1)
                if n >= 2:
                    pe.wait_ge(staged, n - 1)
                for f in range(4):
                    ins = nc.tensor.transpose(pt[:, n % 2, f * P:(f + 1) * P], rot[:, n % 2, f * P:(f + 1) * P], ident[:, :])
                ins.then_inc(turned, 1)

            for cb in range(NC):
                pe.wait_ge(lo_done, KT * (cb + 1))
                for t in range(TT):
                    n = cb * TT + t
                    if n >= 4:
                        if n - 4 < 2 * TT:
                            pe.wait_ge(rs_done, n - 3)
                        else:
                            pe.wait_ge(staged, n - 3)
                    for k in range(KT):
                        ins = split_products(nc, ps[:, n % 4, :], h_hi[:, k, t * P:(t + 1) * P], h_lo[:, k, t * P:(t + 1) * P],
                                             w_hi[:, cb % 2, k, :], w_lo[:, cb % 2, k, :], k == 0, k == KT - 1)
                    ins.then_inc(mm_done, 1)
                    if 1 <= n <= 2 * TT:
                        turn(n - 1)


def load_columns(nc, groups, consts):
    ident = consts["ident"]
    with ExitStack() as ctx:
        s = Scope(nc, ctx, "cols")
        n_max = max(src.shape[0] for src, _ in groups)
        rows = s.sb("rows", [n_max, len(groups), P])
        ps = s.ps("ps", [P, len(groups), 64])
        loaded = [s.sem(f"loaded{i}") for i in range(len(groups))]
        turned, copied = s.sem("turned"), s.sem("copied")
        block = s.block()

        @block.sync
        def _(sp):
            for i, (src, _) in enumerate(groups):
                sp.dma_start(rows[0:src.shape[0], i, :], src).then_inc(loaded[i], 16)

        @block.tensor
        def _(pe):
            for i, (src, _) in enumerate(groups):
                n = src.shape[0]
                pe.wait_ge(loaded[i], 16)
                nc.tensor.transpose(ps[:, i, 0:n], rows[0:n, i, :], ident[0:n, 0:n]).then_inc(turned, 1)

        @block.vector
        def _(dve):
            dve.wait_ge(turned, len(groups))
            for i, (src, dst) in enumerate(groups):
                nc.vector.tensor_copy(dst, ps[:, i, 0:src.shape[0]]).then_inc(copied, 1)
            dve.wait_ge(copied, len(groups))


def make_constants(nc, consts):
    with ExitStack() as ctx:
        s = Scope(nc, ctx, "const")
        zeroed, selected = s.sem("zeroed"), s.sem("selected")
        heads_zeroed, heads_set = s.sem("heads_zeroed"), s.sem("heads_set")
        ident, heads = consts["ident"], consts["heads"]
        block = s.block()

        @block.gpsimd
        def _(pool):
            nc.gpsimd.memset(ident[:, :], 0.0).then_inc(zeroed, 1)
            pool.wait_ge(zeroed, 1)
            nc.gpsimd.affine_select(out=ident[:, :], in_=ident[:, :], compare_op=ALU.not_equal, fill=1.0, base=0,
                                    pattern=[[-1, P]], channel_multiplier=1).then_inc(selected, 1)

        @block.vector
        def _(dve):
            nc.vector.memset(heads[:, :], 0.0).then_inc(heads_zeroed, 1)
            dve.wait_ge(heads_zeroed, 1)
            nc.vector.memset(heads[0:HD, 0:HD], 1.0)
            nc.vector.memset(heads[HD:P, HD:P], 1.0).then_inc(heads_set, 1)
            dve.wait_ge(heads_set, 1)


def project_convolved(nc, mix_in, conv_cols, h_hi, h_lo, z_d):
    M = 4 * WA // P
    B = 4
    w_v = mix_in[0].rearrange("(t p) (m c) -> m p t c", p=P, c=P)
    with ExitStack() as ctx:
        s = Scope(nc, ctx, "za")
        w_raw = s.sb("w_raw", [P, B, KT, P])
        w_hi = s.sb("w_hi", [P, 2, KT, P], F32R)
        w_lo = s.sb("w_lo", [P, 2, KT, P], F32R)
        z = s.sb("z", [P, 2, S])
        ps = s.ps("ps", [P, 2, S])
        raw_loaded = [s.sem(f"raw_loaded{j}") for j in range(B)]
        stored = [s.sem(f"stored{j}") for j in range(2)]
        hi_done, lo_done, mm_done = s.sem("hi_done"), s.sem("lo_done"), s.sem("mm_done")
        mid_done, left_done, conv_done = s.sem("mid_done"), s.sem("left_done"), s.sem("conv_done")
        block = s.block()

        @block.sync
        def _(sp):
            def load(n, j):
                sp.dma_start(w_raw[:, j], w_v[bass.ds(n, 1)].rearrange("o p t c -> p (o t) c")).then_inc(raw_loaded[j], 16)

            def store(n, j):
                sp.wait_ge(conv_done, n + 3)
                sp.dma_start(z_d[bass.ds(n, 1)].rearrange("o p s -> p (o s)"), z[:, j % 2, :]).then_inc(stored[j % 2], 16)

            for j in range(2):
                sp.sem_inc(stored[j], 16)
            for j in range(B):
                load(j, j)
            with sp.Fori(0, M // B - 1) as i:
                for j in range(B):
                    store(i * B + j, j)
                    sp.wait_ge(lo_done, i * B + (j + 1))
                    load(i * B + (j + B), j)
            for j in range(B):
                store(M - B + j, j)
            for j in range(2):
                sp.wait_ge(stored[j], 16 + 16 * M // 2)

        @block.scalar
        def _(act):
            def split(i, j):
                act.wait_ge(raw_loaded[j], i * 16 + 16)
                act.wait_ge(mm_done, i * B + (j + 1))
                nc.scalar.activation(w_hi[:, j % 2], w_raw[:, j], ACT.Copy).then_inc(hi_done, 1)

            def middle(i, j):
                act.wait_ge(mm_done, i * B + (j + 3))
                act.wait_ge(stored[j % 2], i * (16 * B // 2) + 16 * (j // 2) + 16)
                nc.scalar.activation(z[:, j % 2, :], ps[:, j % 2, :], ACT.Copy,
                                     scale=conv_cols[:, 1, bass.ds(i * B + j, 1)]).then_inc(mid_done, 1)

            def turn(i, last):
                for j in range(B):
                    if j + 1 < B:
                        split(i, j + 1)
                    elif not last:
                        split(i + 1, 0)
                    middle(i, j)

            split(0, 0)
            with act.Fori(0, M // B - 1) as i:
                turn(i, False)
            turn(M // B - 1, True)

        @block.gpsimd
        def _(pool):
            with pool.Fori(0, M // B) as i:
                for j in range(B):
                    pool.wait_ge(hi_done, i * B + (j + 1))
                    nc.gpsimd.tensor_tensor(w_lo[:, j % 2], w_raw[:, j], w_hi[:, j % 2].bitcast(F32), ALU.subtract).then_inc(lo_done, 1)

        @block.vector
        def _(dve):
            dve.sem_inc(conv_done, 2)
            with dve.Fori(0, M // B) as i:
                for j in range(B):
                    dve.wait_ge(mid_done, i * B + (j + 1))
                    nc.vector.scalar_tensor_tensor(z[:, j % 2, 1:S], ps[:, j % 2, 0:S - 1], conv_cols[:, 0, bass.ds(i * B + j, 1)],
                                                   z[:, j % 2, 1:S], ALU.mult, ALU.add).then_inc(left_done, 1)
                    dve.wait_ge(left_done, i * B + (j + 1))
                    nc.vector.scalar_tensor_tensor(z[:, j % 2, 0:S - 1], ps[:, j % 2, 1:S], conv_cols[:, 2, bass.ds(i * B + j, 1)],
                                                   z[:, j % 2, 0:S - 1], ALU.mult, ALU.add).then_inc(conv_done, 1)

        @block.tensor
        def _(pe):
            pe.sem_inc(mm_done, 2)
            with pe.Fori(0, M // B) as i:
                for j in range(B):
                    pe.wait_ge(lo_done, i * B + (j + 1))
                    pe.wait_ge(conv_done, i * B + (j + 1))
                    for half in range(2):
                        span = slice(half * HALF, (half + 1) * HALF)
                        for k in range(KT):
                            ins = split_products(nc, ps[:, j % 2, span], w_hi[:, j % 2, k, :], w_lo[:, j % 2, k, :],
                                                 h_hi[:, k, span], h_lo[:, k, span], k == 0, k == KT - 1)
                    ins.then_inc(mm_done, 1)


def dilated_attention(nc, qk_d, v_d, bias_table, consts, yb_d):
    ident = consts["ident"]
    HB = 2
    NB = NH // HB
    NS = HB * TT
    OFF = S - P
    with ExitStack() as ctx:
        s = Scope(nc, ctx, "att")
        bias = s.sb("bias", [P, 2 * S - P])
        q_raw = s.sb("q_raw", [P, HB, S])
        k_raw = s.sb("k_raw", [P, HB, S])
        q2 = s.sb("q2", [P, HB, S], F32R)
        k2 = s.sb("k2", [P, HB, S], F32R)
        k_lo = s.sb("k_lo", [P, HB, S], F32R)
        v = s.sb("v", [P, HB, TT, HD])
        sc = s.sb("sc", [P, 2, S])
        pr = s.sb("pr", [P, 2, S])
        prT = s.sb("prT", [P, 2, S])
        lowest = s.sb("lowest", [P, NS])
        den = s.sb("den", [P, NS])
        rden = s.sb("rden", [P, NS])
        y = s.sb("y", [P, 2, TT, HD])
        ps_s = s.ps("s", [P, 2, S])
        ps_t = s.ps("t", [P, S])
        ps_o = s.ps("o", [P, 2, 512])
        q_loaded = [s.sem(f"q_loaded{j}") for j in range(HB)]
        stored = [s.sem(f"stored{j}") for j in range(2)]
        begun, settled, bias_loaded, hi_done, lo_done = s.sem("begun"), s.sem("settled"), s.sem("bias_loaded"), s.sem("hi_done"), s.sem("lo_done")
        score_done, biased, exp_done, turned = s.sem("score_done"), s.sem("biased"), s.sem("exp_done"), s.sem("turned")
        copied_lo, copied_hi, out_done, rden_done, y_done = (
            s.sem("copied_lo"), s.sem("copied_hi"), s.sem("out_done"), s.sem("rden_done"), s.sem("y_done"))
        block = s.block()

        @block.sync
        def _(sp):
            sp.dma_start(bias[:, :], bias_table).then_inc(bias_loaded, 16)
            for j in range(2):
                sp.sem_inc(stored[j], 16)
            def load(i, j):
                h = i * HB + j
                for raw, at in ((q_raw, 0), (k_raw, 1)):
                    for rows in (slice(0, HD), slice(HD, P)):
                        sp.dma_start(raw[rows, j, :], qk_d[at].rearrange("(h e) s -> h e s", e=HD)[bass.ds(h, 1)].rearrange("o e s -> (o e) s")).then_inc(q_loaded[j], 16)
                sp.dma_start(v[:, j], v_d.rearrange("(t p) (h e) -> h p t e", p=P, e=HD)[bass.ds(h, 1)].rearrange("o p t e -> p (o t) e")).then_inc(q_loaded[j], 16)

            def store(i, j):
                sp.wait_ge(y_done, i * NS + (TT * (j + 1) + 2))
                sp.sem_inc(settled, 1)
                sp.dma_start(yb_d.rearrange("(t p) (h e) -> h p t e", p=P, e=HD)[bass.ds(i * HB + j, 1)].rearrange("o p t e -> p (o t) e"), y[:, j]).then_inc(stored[j], 16)

            for j in range(HB):
                load(0, j)
            with sp.Fori(0, NB - 1) as i:
                for j in range(HB):
                    sp.wait_ge(lo_done, i * (2 * HB) + (2 * j + 3))
                    sp.sem_inc(settled, 1)
                    sp.wait_ge(out_done, i * NS + (TT * (j + 1) + 2))
                    sp.sem_inc(settled, 1)
                    load(i + 1, j)
                    store(i, j)
            for j in range(HB):
                store(NB - 1, j)
            for j in range(2):
                sp.wait_ge(stored[j], 16 + 16 * NH // 2)

        @block.tensor
        def _(pe):
            pe.sem_inc(out_done, 2)
            pe.sem_inc(turned, 2)
            def scores(i, n):
                j, t = divmod(n, TT)
                if t == 0:
                    pe.wait_ge(lo_done, i * (2 * HB) + (2 * j + 3))
                pe.wait_ge(biased, i * NS + (n + 1))
                for half in range(2):
                    out, span = ps_s[:, n % 2, half * HALF:(half + 1) * HALF], slice(half * HALF, (half + 1) * HALF)
                    queries = slice(t * P, (t + 1) * P)
                    nc.tensor.matmul(out, q2[:, j, queries], k2[:, j, span], start=True, stop=False)
                    ins = nc.tensor.matmul(out, q2[:, j, queries], k_lo[:, j, span], start=False, stop=True)
                ins.then_inc(score_done, 1)

            def turn(i, n):
                pe.wait_ge(exp_done, i * NS + (n + 3))
                pe.wait_ge(copied_lo, i * NS + (n + 1))
                pe.wait_ge(copied_hi, i * NS + (n + 1))
                for k in range(TT):
                    ins = nc.tensor.transpose(ps_t[:, k * P:(k + 1) * P], pr[:, n % 2, k * P:(k + 1) * P], ident[:, :])
                ins.then_inc(turned, 1)

            def weigh(i, n):
                j, t = divmod(n, TT)
                pe.wait_ge(copied_lo, i * NS + (n + 2))
                pe.wait_ge(copied_hi, i * NS + (n + 2))
                pe.wait_ge(y_done, i * NS + (n + 1))
                for k in range(TT):
                    ins = nc.tensor.matmul(ps_o[:, n % 2, 0:HD], prT[:, n % 2, k * P:(k + 1) * P], v[:, j, k, :],
                                           start=(k == 0), stop=(k == TT - 1))
                ins.then_inc(out_done, 1)

            def body(i, last):
                for n in range(NS):
                    if n + 1 < NS:
                        scores(i, n + 1)
                    elif not last:
                        scores(i + 1, 0)
                    if n >= 1:
                        weigh(i, n - 1)
                    turn(i, n)
                weigh(i, NS - 1)

            scores(0, 0)
            with pe.Fori(0, NB - 1) as i:
                body(i, False)
            body(NB - 1, True)

        @block.gpsimd
        def _(pool):
            pool.sem_inc(lo_done, 1)
            with pool.Fori(0, NB) as i:
                for j in range(HB):
                    pool.wait_ge(lo_done, i * (2 * HB) + (2 * j + 1))
                    pool.wait_ge(hi_done, i * (2 * HB) + (2 * j + 1))
                    nc.gpsimd.tensor_tensor(q2[HD:P, j, :], q_raw[HD:P, j, :], q2[HD:P, j, :].bitcast(F32), ALU.subtract).then_inc(lo_done, 1)
                    pool.wait_ge(lo_done, i * (2 * HB) + (2 * j + 2))
                    pool.wait_ge(hi_done, i * (2 * HB) + (2 * j + 2))
                    nc.gpsimd.tensor_tensor(k_lo[:, j, :], k_raw[:, j, :], k2[:, j, :].bitcast(F32), ALU.subtract).then_inc(lo_done, 1)

        @block.vector
        def _(dve):
            dve.wait_ge(bias_loaded, 16)
            dve.sem_inc(biased, 2)
            dve.sem_inc(copied_lo, 1)
            dve.sem_inc(y_done, 2)
            def bias_step(i, n):
                t = n % TT
                dve.wait_ge(score_done, i * NS + (n + 1))
                dve.wait_ge(exp_done, i * NS + (n + 1))
                dve.sem_inc(begun, 1)
                nc.vector.tensor_tensor_reduce(out=sc[:, n % 2, :], in0=ps_s[:, n % 2, :], in1=bias[:, OFF - t * P:OFF - t * P + S],
                                               scale=-1.0 / 8, scalar=3.0e38, op0=ALU.add, op1=ALU.min,
                                               accum_out=lowest[:, n:n + 1]).then_inc(biased, 1)

            def copy_step(i, n):
                dve.wait_ge(turned, i * NS + (n + 3))
                dve.wait_ge(out_done, i * NS + (n + 1))
                nc.vector.tensor_copy(prT[:, n % 2, 0:HALF], ps_t[:, 0:HALF]).then_inc(copied_lo, 1)

            def out_step(i, n):
                j, t = divmod(n, TT)
                dve.wait_ge(exp_done, i * NS + (n + 3))
                nc.vector.reciprocal(rden[:, n:n + 1], den[:, n:n + 1]).then_inc(rden_done, 1)
                dve.wait_ge(rden_done, i * NS + (n + 1))
                dve.wait_ge(out_done, i * NS + (n + 3))
                if t == 0:
                    dve.wait_ge(stored[j % 2], i * (16 * HB // 2) + 16 * (j // 2) + 16)
                nc.vector.tensor_scalar(y[:, j % 2, t, :], ps_o[:, n % 2, 0:HD], rden[:, n:n + 1], None, ALU.mult).then_inc(y_done, 1)

            def body(i, last):
                for n in range(NS):
                    if n + 1 < NS:
                        bias_step(i, n + 1)
                    elif not last:
                        bias_step(i + 1, 0)
                    if n >= 1:
                        out_step(i, n - 1)
                    copy_step(i, n)
                out_step(i, NS - 1)

            bias_step(0, 0)
            with dve.Fori(0, NB - 1) as i:
                body(i, False)
            body(NB - 1, True)

        @block.scalar
        def _(act):
            act.sem_inc(exp_done, 2)
            act.sem_inc(copied_hi, 1)
            def split(i, j, raw, hi):
                act.wait_ge(q_loaded[j], i * 80 + 80)
                nc.scalar.activation(hi[:, j, :], raw[:, j, :], ACT.Copy).then_inc(hi_done, 1)

            def exp_step(i, n):
                act.wait_ge(biased, i * NS + (n + 3))
                act.wait_ge(turned, i * NS + (n + 1))
                nc.scalar.activation(pr[:, n % 2, :], sc[:, n % 2, :], ACT.Exp, bias=lowest[:, n:n + 1], scale=-1.0,
                                     accum_out=den[:, n:n + 1]).then_inc(exp_done, 1)

            def copy_step(i, n):
                act.wait_ge(turned, i * NS + (n + 3))
                act.wait_ge(out_done, i * NS + (n + 1))
                nc.scalar.activation(prT[:, n % 2, HALF:S], ps_t[:, HALF:S], ACT.Copy).then_inc(copied_hi, 1)

            def body(i, last):
                for n in range(NS):
                    if n + 1 < NS:
                        exp_step(i, n + 1)
                    elif not last:
                        exp_step(i + 1, 0)
                    copy_step(i, n)
                    if n == TT // 2:
                        act.wait_ge(score_done, i * NS + 1)
                        split(i, 1, q_raw, q2)
                    if n == TT // 2 + 1:
                        split(i, 1, k_raw, k2)
                    if not last and n == TT + TT // 2:
                        act.wait_ge(score_done, i * NS + TT)
                        split(i + 1, 0, q_raw, q2)
                    if not last and n == TT + TT // 2 + 1:
                        split(i + 1, 0, k_raw, k2)

            split(0, 0, q_raw, q2)
            split(0, 0, k_raw, k2)
            exp_step(0, 0)
            with act.Fori(0, NB - 1) as i:
                body(i, False)
            body(NB - 1, True)


def lora_hidden(nc, z_d, w1, a1, g1, tw, ta, tg):
    KU = WA // P
    with ExitStack() as ctx:
        s = Scope(nc, ctx, "lora")
        u = s.sb("u", [P, KU, S])
        w = s.sb("w", [P, 3, KU, P])
        ps = s.ps("ps", [P, 3, S])
        u_loaded, w_loaded, mm_done, out_done = s.sem("u_loaded"), s.sem("w_loaded"), s.sem("mm_done"), s.sem("out_done")
        block = s.block()

        @block.sync
        def _(sp):
            for d in range(2):
                for i, net in enumerate((w1, a1)):
                    sp.dma_start(w[:, i, :, d * 64:(d + 1) * 64], net[0, d].rearrange("(t p) e -> p t e", p=P)).then_inc(w_loaded, 16)
            sp.dma_start(w[:, 2], g1[0].rearrange("(t p) e -> p t e", p=P)).then_inc(w_loaded, 16)
            sp.dma_start(u[:, :, :], z_d[3 * KU:4 * KU].rearrange("t p s -> p t s")).then_inc(u_loaded, 16)

        @block.tensor
        def _(pe):
            pe.wait_ge(w_loaded, 80)
            pe.wait_ge(u_loaded, 16)
            for i in range(3):
                for half in range(2):
                    span = slice(half * HALF, (half + 1) * HALF)
                    for k in range(KU):
                        ins = nc.tensor.matmul(ps[:, i, span], w[:, i, k, :], u[:, k, span], start=(k == 0), stop=(k == KU - 1))
                ins.then_inc(mm_done, 1)

        @block.scalar
        def _(act):
            for i, (dst, f) in enumerate(((tw, ACT.Tanh), (ta, ACT.Copy), (tg, ACT.Sigmoid))):
                act.wait_ge(mm_done, i + 1)
                nc.scalar.activation(dst[:, :], ps[:, i, :], f).then_inc(out_done, 1)
            act.wait_ge(out_done, 3)


LEVELS = (2, 4, 8, 16, 32, 64)
ALPHA, RHO, NBETA, KAPPA, VAL = range(5)


def prepare_recurrence(nc, z_d, w2, a2, g2, consts, tw, ta, tg, ff, bon, gate, st_d):
    KU = WA // P
    NCH = S // P
    M = NCH // 2
    vec, heads = consts["vec"], consts["heads"]
    W0, A0, K_K, K_A, R_K = 0, 2, 4, 5, 6
    LORA_D0, RATE_D0, SQUARES, LORA_D1, RATE_D1, GATE, BONUS = range(7)
    NP = 7
    with ExitStack() as ctx:
        s = Scope(nc, ctx, "rp")

        def pair(name, shape):
            return [s.sb(f"{name}{j}", shape) for j in range(2)]

        r, k, v, kk = pair("r", [P, S]), pair("k", [P, S]), pair("v", [P, S]), pair("kk", [P, S])
        w2s, a2s, g2s, vc = pair("w2s", [P, P]), pair("a2s", [P, P]), pair("g2s", [P, P]), pair("vc", [P, 10])
        lw = pair("lw", [P, 2, S])
        aa = pair("aa", [P, 2, S])
        cc = pair("cc", [P, 2, S])
        ep = pair("ep", [P, 2, S])
        kd = pair("kd", [P, 2, S])
        sqb = pair("sqb", [P, S])
        mids, emid = pair("mids", [P, 2, NCH]), pair("emid", [P, 2, NCH])
        reset_row = s.sb("reset_row", [P, S])
        eps = s.sb("eps", [P, 1])
        pb = s.ps("pb", [P, 8, 512])
        in_loaded, stored = ([s.sem(f"{n}{j}") for j in range(2)] for n in ("in_loaded", "stored"))
        (ones_set, cleared, eps_set, vec_ready, kk_in, sq_done, mm_done, act_read, kd_in, kd_done, kds_done, centred,
         exps_done, kk_ready, bonus_in, bon_ready, factors, dve_out, pool_out, vlink) = (s.sem(n) for n in (
             "ones_set", "cleared", "eps_set", "vec_ready", "kk_in", "sq_done", "mm_done", "act_read", "kd_in", "kd_done",
             "kds_done", "centred", "exps_done", "kk_ready", "bonus_in", "bon_ready", "factors", "dve_out", "pool_out", "vlink"))
        settled = s.sem("settled")
        block = s.block()

        def result(j, n):
            at = 4 * j + 2 * (n % 2)
            return pb[:, at:at + 2, :].rearrange("p a n -> p (a n)")

        @block.sync
        def _(sp):
            for j in range(2):
                sp.sem_inc(stored[j], 16)
            with sp.Fori(0, KU // 2) as i:
                for j in range(2):
                    f = i * 2 + j
                    sp.wait_ge(stored[j], i * 128 + 16)
                    sp.wait_ge(bon_ready, i * 2 + 2)
                    for dst, q in ((k[j], 1), (r[j], 0), (v[j], 2)):
                        sp.dma_start(dst[:, :], z_d[bass.ds(f + q * KU, 1)].rearrange("o p s -> p (o s)")).then_inc(in_loaded[j], 16)
                    for d in range(2):
                        rows = slice(d * 64, (d + 1) * 64)
                        for dst, net in ((w2s[j], w2), (a2s[j], a2)):
                            sp.dma_start(dst[rows, :], net[0, d].rearrange("e (m c) -> m e c", c=P)[bass.ds(f, 1)].rearrange("o e c -> (o e) c")).then_inc(in_loaded[j], 16)
                    sp.dma_start(g2s[j][:, :], g2[0].rearrange("e (m c) -> m e c", c=P)[bass.ds(f, 1)].rearrange("o e c -> (o e) c")).then_inc(in_loaded[j], 16)
                for g in range(2):
                    for j in range(2):
                        made = i * 12 + (g * 6 + j * 3)
                        for q, src, sem, count in ((0, lw[j], dve_out, made + 1), (1, ep[j], pool_out, i * 4 + (g * 2 + j + 1)),
                                                   (2, aa[j], dve_out, made + 2), (3, kd[j], dve_out, made + 3)):
                            sp.wait_ge(sem, count)
                            sp.sem_inc(settled, 1)
                            sp.dma_start(st_d[g, bass.ds(i * (2 * M) + j * M, M), q].rearrange("m p t -> p m t"),
                                         src[:, g, :].rearrange("p (m t) -> p m t", m=M)).then_inc(stored[j], 16)
            for j in range(2):
                sp.wait_ge(stored[j], 16 + 128 * (KU // 2))

        @block.tensor
        def _(pe):
            with pe.Fori(0, KU // 2) as i:
                for n in range(NP):
                    for j in range(2):
                        if n == 0:
                            pe.wait_ge(in_loaded[j], i * 128 + 128)
                            pe.wait_ge(bon_ready, i * 2 + (j + 1))
                        elif n >= 2:
                            pe.wait_ge(act_read, i * 12 + ((n - 2) * 2 + j + 1))
                        if n == SQUARES:
                            pe.wait_ge(sq_done, i * 2 + (j + 1))
                        if n == BONUS:
                            pe.wait_ge(bonus_in, i * 2 + (j + 1))
                            pe.wait_ge(act_read, i * 12 + (GATE * 2 + j + 1))
                        d0, d1 = slice(0, 64), slice(64, P)
                        lhs, rhs = ((w2s[j][d0], tw[d0]), (a2s[j][d0], ta[d0]), (heads, sqb[j]), (w2s[j][d1], tw[d1]),
                                    (a2s[j][d1], ta[d1]), (g2s[j], tg), (heads, sqb[j]))[n]
                        for half in range(2):
                            span = slice(half * HALF, (half + 1) * HALF)
                            ins = nc.tensor.matmul(result(j, n)[:, span], lhs[:, :], rhs[:, span], start=True, stop=True)
                        ins.then_inc(mm_done, 1)

        @block.scalar
        def _(act):
            A = nc.scalar.activation
            with act.Fori(0, KU // 2) as i:
                def read(n, j, dst, f, **kw):
                    act.wait_ge(mm_done, i * 14 + (n * 2 + j + 1))
                    A(dst, result(j, n), f, **kw).then_inc(act_read, 1)

                def rate(d, j):
                    act.wait_ge(act_read, i * 12 + ((RATE_D0, RATE_D1)[d] * 2 + j + 1))
                    A(kd[j][:, d, :], aa[j][:, d, :], ACT.Identity, scale=vc[j][:, K_A:K_A + 1], bias=vc[j][:, 9:10]).then_inc(kd_in, 1)

                for j in range(2):
                    act.wait_ge(vec_ready, i * 2 + (j + 1))
                    A(kk[j][:, :], k[j][:, :], ACT.Copy, scale=vc[j][:, K_K:K_K + 1]).then_inc(kk_in, 1)
                for j in range(2):
                    read(LORA_D0, j, lw[j][:, 0, :], ACT.Sigmoid, bias=vc[j][:, W0:W0 + 1])
                for j in range(2):
                    read(RATE_D0, j, aa[j][:, 0, :], ACT.Sigmoid, bias=vc[j][:, A0:A0 + 1])
                act.wait_ge(eps_set, 1)
                for j in range(2):
                    read(SQUARES, j, sqb[j][:, :], ACT.Sqrt, bias=eps[:, 0:1])
                for j in range(2):
                    rate(0, j)
                for j in range(2):
                    read(LORA_D1, j, lw[j][:, 1, :], ACT.Sigmoid, bias=vc[j][:, W0 + 1:W0 + 2])
                for j in range(2):
                    read(RATE_D1, j, aa[j][:, 1, :], ACT.Sigmoid, bias=vc[j][:, A0 + 1:A0 + 2])
                for j in range(2):
                    rate(1, j)
                for j in range(2):
                    read(GATE, j, gate[:, bass.ds(i * 2 + j, 1), :].rearrange("p o s -> p (o s)"), ACT.Copy)
                for d in range(2):
                    for j in range(2):
                        act.wait_ge(centred, i * 4 + (d * 2 + j + 1))
                        A(emid[j][:, d, :], mids[j][:, d, :], ACT.Exp, scale=DECAY)
                        A(ep[j][:, d, :], cc[j][:, d, :], ACT.Exp, scale=DECAY)
                        A(lw[j][:, d, :], lw[j][:, d, :], ACT.Exp, scale=DECAY)
                        A(cc[j][:, d, :], cc[j][:, d, :], ACT.Exp, scale=-DECAY).then_inc(exps_done, 1)

        @block.gpsimd
        def _(pool):
            G = nc.gpsimd
            G.memset(eps[:, :], L2_EPS).then_inc(eps_set, 1)
            G.memset(reset_row[:, :], 1.0).then_inc(ones_set, 1)
            pool.wait_ge(ones_set, 1)
            G.memset(reset_row[:, :].rearrange("p (c t) -> p c t", t=P)[:, :, 0:1], 0.0).then_inc(cleared, 1)
            with pool.Fori(0, KU // 2) as i:
                for j in range(2):
                    pool.wait_ge(kk_in, i * 2 + (j + 1))
                    G.tensor_tensor(sqb[j][:, :], kk[j][:, :], kk[j][:, :], ALU.mult).then_inc(sq_done, 1)
                for d in range(2):
                    for j in range(2):
                        pool.wait_ge(kd_in, i * 4 + (d * 2 + j + 1))
                        G.tensor_tensor(kd[j][:, d, :], kd[j][:, d, :], k[j][:, :], ALU.mult).then_inc(kd_done, 1)
                for j in range(2):
                    pool.wait_ge(kd_done, i * 4 + (2 + j + 1))
                    pool.wait_ge(kk_ready, i * 2 + (j + 1))
                    G.tensor_tensor(sqb[j][:, :], kd[j][:, 0, :], kd[j][:, 1, :], ALU.add).then_inc(kds_done, 1)
                for g in range(2):
                    for j in range(2):
                        pool.wait_ge(exps_done, i * 4 + (g * 2 + j + 1))
                        pool.wait_ge(factors, i * 4 + (g * 2 + j + 1))
                        G.tensor_tensor(ep[j][:, g, :], r[j][:, :], ep[j][:, g, :], ALU.mult).then_inc(pool_out, 1)

        VLINKS = 2 + 4 * 3 + 2 + 4

        @block.vector
        def _(dve):
            V = nc.vector
            ch = Chain(dve, vlink)
            dve.wait_ge(cleared, 1)
            dve.sem_inc(bon_ready, 2)
            with dve.Fori(0, KU // 2) as i:
                ch.turn(i, VLINKS)

                def running(d, j):
                    dve.wait_ge(act_read, i * 12 + ((LORA_D0, LORA_D1)[d] * 2 + j + 1))
                    o = slice(None) if d == 0 else slice(None, None, -1)
                    c, w = cc[j][:, d, :], lw[j][:, d, :]
                    c3 = c.rearrange("p (c t) -> p c t", t=P)
                    ch.link(V.tensor_tensor_scan(cc[j][:, d, o], reset_row[:, :], lw[j][:, d, o], 0.0, ALU.mult, ALU.add))
                    ch.link(V.tensor_copy(mids[j][:, d, :], c3[:, :, P // 2]))
                    ch.link(V.tensor_tensor(c3, c3, mids[j][:, d, :].unsqueeze(2).broadcast_to([P, NCH, P]), ALU.subtract))
                    V.tensor_tensor(w, c, w, ALU.subtract).then_inc(centred, 1)

                for j in range(2):
                    dve.wait_ge(in_loaded[j], i * 128 + 128)
                    ch.link(V.tensor_copy(vc[j][:, 0:9], vec[:, :, bass.ds(i * 2 + j, 1)].rearrange("p a o -> p (a o)")))
                    V.tensor_scalar(vc[j][:, 9:10], vc[j][:, K_A:K_A + 1], -1.0, 1.0, ALU.mult, ALU.add).then_inc(vec_ready, 1)
                for j in range(2):
                    running(0, j)
                for j in range(2):
                    dve.wait_ge(act_read, i * 12 + (SQUARES * 2 + j + 1))
                    ch.link(V.reciprocal(sqb[j][:, :], sqb[j][:, :]))
                    V.tensor_tensor(kk[j][:, :], kk[j][:, :], sqb[j][:, :], ALU.mult).then_inc(kk_ready, 1)
                for j in range(2):
                    running(1, j)
                for d in range(2):
                    for j in range(2):
                        dve.wait_ge(kk_ready, i * 2 + (j + 1))
                        dve.wait_ge(kd_in, i * 4 + (d * 2 + j + 1))
                        ch.link(V.scalar_tensor_tensor(aa[j][:, d, :], kk[j][:, :], -1.0, aa[j][:, d, :], ALU.mult, ALU.mult))
                for j in range(2):
                    dve.wait_ge(kds_done, i * 2 + (j + 1))
                    V.scalar_tensor_tensor(sqb[j][:, :], sqb[j][:, :], vc[j][:, R_K:R_K + 1], r[j][:, :], ALU.mult, ALU.mult).then_inc(bonus_in, 1)
                for g in range(2):
                    for j in range(2):
                        dve.wait_ge(exps_done, i * 4 + (g * 2 + j + 1))
                        e3 = ep[j][:, g, :].rearrange("p (c t) -> p c t", t=P)
                        e = e3[:, :, P - 1] if g == 0 else e3[:, ::-1, 0]
                        m = emid[j][:, g, :] if g == 0 else emid[j][:, g, ::-1]
                        at = i * (2 * NCH) + j * NCH
                        V.tensor_copy(ff[:, g, bass.ds(at + (NCH - 1), 1)], e[:, NCH - 1:NCH])
                        V.tensor_tensor(ff[:, g, bass.ds(at, NCH - 1)], e[:, 0:NCH - 1], m[:, 1:NCH], ALU.mult).then_inc(factors, 1)
                        V.tensor_tensor(lw[j][:, g, :], kk[j][:, :], lw[j][:, g, :], ALU.mult).then_inc(dve_out, 1)
                        V.tensor_tensor(aa[j][:, g, :], aa[j][:, g, :], cc[j][:, g, :], ALU.mult).then_inc(dve_out, 1)
                        V.tensor_tensor(kd[j][:, g, :], kd[j][:, g, :], cc[j][:, g, :], ALU.mult).then_inc(dve_out, 1)
                for j in range(2):
                    dve.wait_ge(mm_done, i * 14 + (BONUS * 2 + j + 1))
                    V.tensor_tensor(bon[:, bass.ds(i * 2 + j, 1), :].rearrange("p o s -> p (o s)"), result(j, BONUS), v[j][:, :],
                                    ALU.mult).then_inc(bon_ready, 1)
                assert ch.n == VLINKS, ch.n


def recurrence(nc, z_d, st_d, tab, consts, ff, ysum):
    KU = WA // P
    NCH = S // P
    M = NCH // 2
    ident = consts["ident"]
    with ExitStack() as ctx:
        s = Scope(nc, ctx, "rw")
        pred = s.sb("pred", [P, 2, 4 * P], U32)
        first = s.sb("first", [P, 2, 2, P], U32)
        lvl = s.sb("lvl", [P, 2, len(LEVELS), 64])
        st = [s.sb(f"st{g}", [P, 5, 2 * P]) for g in range(2)]
        rho2 = [s.sb(f"rho2{g}", [P, 2, P]) for g in range(2)]
        tok = [s.sb(f"tok{g}", [P, 3, 2, P]) for g in range(2)]
        rhs = [s.sb(f"rhs{g}", [P, 4, P]) for g in range(2)]
        qm = [s.sb(f"qm{g}", [P, 4, 4 * P]) for g in range(2)]
        T = [s.sb(f"T{g}", [P, 4, P]) for g in range(2)]
        U = [s.sb(f"U{g}", [P, 4, P]) for g in range(2)]
        xc = [s.sb(f"xc{g}", [P, 4, 64]) for g in range(2)]
        wt = [s.sb(f"wt{g}", [P, 4, P]) for g in range(2)]
        rt = [s.sb(f"rt{g}", [P, 2, P]) for g in range(2)]
        gt = [s.sb(f"gt{g}", [P, 2, HD]) for g in range(2)]
        es = [s.sb(f"es{g}", [P, 2, HD]) for g in range(2)]
        esf = [s.sb(f"esf{g}", [P, HD]) for g in range(2)]
        pb = s.ps("pb", [P, 8, 512])

        def both(name):
            return [s.sem(f"{name}{g}") for g in range(2)]

        tab_loaded, cleared = s.sem("tab_loaded"), s.sem("cleared")
        staged, rho_done, tok_t, tok_c, q_done, qm_done, l_done, unit, tu_done = (both(n) for n in (
            "staged", "rho_done", "tok_t", "tok_c", "q_done", "qm_done", "l_done", "unit", "tu_done"))
        mv_done, mv_c, x_done, xc_done, tx_done, lev_done, flipped, u_done, w_done, w_c, rg_done, rt_done = (both(n) for n in (
            "mv_done", "mv_c", "x_done", "xc_done", "tx_done", "lev_done", "flipped", "u_done", "w_done", "w_c", "rg_done", "rt_done"))
        ph_done, es_done, esf_done, py_done, y_c = (both(n) for n in ("ph_done", "es_done", "esf_done", "py_done", "y_c"))
        settled = s.sem("settled")

        def settle(eng):
            eng.sem_inc(settled, 1)

        block = s.block()
        NL = len(LEVELS)
        ES = 1 + 2 * M

        def cols(t, u, g, b, which):
            return t[:, u, :].rearrange("p (q two b) -> p q two b", two=2, b=b)[:, :, which ^ g, :]

        def block_rows(g, which):
            return slice((which ^ g) * 64, ((which ^ g) + 1) * 64)

        def cols4(t, g, b, which):
            return t[:, :, :].rearrange("p u (q two b) -> p u q two b", two=2, b=b)[:, :, :, which ^ g, :]

        def quarter(bank, b):
            return pb[:, bank, 0:256].rearrange("p (u q b) -> p u q b", u=4, b=b)

        def half_of(bank, g, b, which):
            return pb[:, bank, :].rearrange("p (u q two b) -> p u q two b", u=4, two=2, b=b)[:, :, :, which ^ g, :]

        def y_bank(g, hh):
            return 2 * g + 1 if hh == 0 else 4 + 2 * g

        def tokens_of(g, m):
            return bass.ds(m * (2 * P), 2 * P) if g == 0 else bass.ds((M - 1 - m) * (2 * P), 2 * P)

        def chunks_of(g, f, m):
            return bass.ds(f * NCH + m * 2, 2) if g == 0 else bass.ds(f * NCH + (M - 1 - m) * 2, 2)

        @block.sync
        def _(sp):
            sp.dma_start(pred[:, :, :], tab["rwkv_pred"].rearrange("g p n -> p g n")).then_inc(tab_loaded, 16)
            sp.dma_start(first[:, :, :, :], tab["rwkv_first"].rearrange("g a p n -> p g a n")).then_inc(tab_loaded, 16)
            sp.dma_start(lvl[:, :, :, :], tab["rwkv_level"].rearrange("g l p n -> p g l n")).then_inc(tab_loaded, 16)
            with sp.Fori(0, KU) as f:
                with sp.Fori(0, M) as m:
                    it = f * M + m
                    for g in range(2):
                        sp.wait_ge(l_done[g], it + 1)
                        sp.wait_ge(rho_done[g], it + 1)
                        block_of = it if g == 0 else f * M + (M - 1) - m
                        sp.dma_start(st[g][:, 0:VAL, :], st_d[g, bass.ds(block_of, 1)].rearrange("o i p t -> p (o i) t")).then_inc(staged[g], 16)
                        sp.dma_start(st[g][:, VAL, :], z_d[bass.ds(f + 2 * KU, 1)].rearrange("o p s -> p (o s)")[:, tokens_of(g, m)]).then_inc(staged[g], 16)

        @block.scalar
        def _(act):
            A = nc.scalar.activation
            for g in range(2):
                act.sem_inc(y_c[g], 1)
            with act.Fori(0, KU) as f:
                with act.Fori(0, M) as m:
                    it = f * M + m
                    for g in range(2):
                        act.wait_ge(tok_t[g], it + 1)
                        turned = pb[:, 2 * g:2 * g + 2, :].rearrange("p a n -> p (a n)")
                        A(rhs[g][:, :, 0:HD], turned[:, 0:2 * P].rearrange("p (u e) -> p u e", e=HD), ACT.Copy)
                        A(tok[g][:, :, :, :].rearrange("p a c e -> p (a c e)"), turned[:, 2 * P:8 * P], ACT.Copy).then_inc(tok_c[g], 1)
                    for g in range(2):
                        act.wait_ge(mv_done[g], it + 1)
                        A(rhs[g][:, :, HD:P], pb[:, 5 + 2 * g, 0:256].rearrange("p (u e) -> p u e", e=HD), ACT.Copy).then_inc(mv_c[g], 1)
                    for i, b in enumerate(LEVELS[:-1]):
                        for g in range(2):
                            act.wait_ge(flipped[g], it * (NL - 1) + (i + 1))
                            A(cols4(U[g], g, b, 1), half_of(5 + 2 * g, g, b, 1), ACT.Copy).then_inc(u_done[g], 1)
                    for g in range(2):
                        act.wait_ge(w_done[g], it + 2)
                        A(wt[g][:, :, :].rearrange("p u e -> p (u e)"), pb[:, 4 + 2 * g, :], ACT.Copy).then_inc(w_c[g], 1)
                    for g in range(2):
                        act.wait_ge(py_done[g], it + 1)
                        for hh in range(2):
                            src = pb[:, y_bank(g, hh), 0:2 * HD].rearrange("p (c e) -> p c e", c=2)
                            if g == 1:
                                src = src[:, ::-1, :]
                            ins = A(ysum[:, g, chunks_of(g, f, m), hh * HD:(hh + 1) * HD], src, ACT.Copy)
                        ins.then_inc(y_c[g], 1)

        @block.gpsimd
        def _(pool):
            G = nc.gpsimd
            for g in range(2):
                ins = G.memset(qm[g][:, :, :], 0.0)
            ins.then_inc(cleared, 1)
            for g in range(2):
                pool.sem_inc(rho_done[g], 1)
            with pool.Fori(0, KU) as f:
                with pool.Fori(0, M) as m:
                    it = f * M + m
                    for g in range(2):
                        pool.wait_ge(w_done[g], it + 1)
                        settle(pool)
                        for c in range(4):
                            G.tensor_copy(T[g][:, c, :], ident[:, :])
                            ins = G.tensor_copy(U[g][:, c, :], ident[:, :])
                        ins.then_inc(unit[g], 1)
                    for g in range(2):
                        pool.wait_ge(staged[g], it * 32 + 32)
                        pool.wait_ge(rt_done[g], it + 1)
                        settle(pool)
                        src = st[g][:, RHO, :].rearrange("p (c t) -> p c t", c=2)
                        if g == 1:
                            src = src[:, ::-1, :]
                        G.tensor_copy(rho2[g][:, :, :], src).then_inc(rho_done[g], 1)

        @block.vector
        def _(dve):
            V = nc.vector
            dve.wait_ge(tab_loaded, 48)
            dve.wait_ge(cleared, 1)
            for g in range(2):
                dve.sem_inc(rt_done[g], 1)
            with dve.Fori(0, KU) as f:
                for g in range(2):
                    V.memset(es[g][:, 0, :], 0.0).then_inc(es_done[g], 1)
                with dve.Fori(0, M) as m:
                    it = f * M + m
                    for p in range(2):
                        for g in range(2):
                            dve.wait_ge(q_done[g], it * 2 + (p + 1))
                            settle(dve)
                            V.copy_predicated(qm[g][:, 2 * p:2 * p + 2, :], pred[:, g:g + 1, :].broadcast_to([P, 2, 4 * P]),
                                              pb[:, 2 * g:2 * g + 2, :]).then_inc(qm_done[g], 1)
                    for g in range(2):
                        dve.wait_ge(unit[g], it + 1)
                        dve.wait_ge(qm_done[g], it * 2 + 2)
                        dve.wait_ge(l_done[g], it + 2)
                        settle(dve)
                        for hh in range(2):
                            V.copy_predicated(T[g][:, hh::2, :], first[:, g, 0:1, :].broadcast_to([P, 2, P]),
                                              pb[:, 4 + 2 * g + hh, 0:2 * P].rearrange("p (c n) -> p c n", c=2))
                        V.copy_predicated(U[g][:, :, :], first[:, g, 1:2, :].broadcast_to([P, 4, P]),
                                          qm[g][:, :, 0:P]).then_inc(tu_done[g], 1)
                    for i, b in enumerate(LEVELS):
                        for g in range(2):
                            dve.wait_ge(x_done[g], it * NL + (i + 1))
                            mask = lvl[:, g, i, :].rearrange("p (u q b) -> p u q b", u=1, b=b).broadcast_to([P, 4, 64 // b, b])
                            V.tensor_tensor(xc[g][:, :, :].rearrange("p u (q b) -> p u q b", b=b), half_of(4 + 2 * g, g, b, 0), mask,
                                            ALU.mult).then_inc(xc_done[g], 1)
                        for g in range(2):
                            dve.wait_ge(tx_done[g], it * NL + (i + 1))
                            if i < NL - 1:
                                tv = cols4(T[g], g, b, 0)
                                V.tensor_tensor(tv, quarter(2 * g + 1, b), tv, ALU.add).then_inc(lev_done[g], 1)
                            else:
                                rows = block_rows(g, 0)
                                uv = U[g][rows, :, block_rows(g, 1)]
                                V.tensor_tensor(uv, pb[rows, 5 + 2 * g, 0:256].rearrange("p (u b) -> p u b", u=4), uv,
                                                ALU.add).then_inc(lev_done[g], 1)
                    for g in range(2):
                        dve.wait_ge(rho_done[g], it + 2)
                        dve.wait_ge(rg_done[g], it + 1)
                        V.tensor_tensor(rt[g][:, :, :].rearrange("p c t -> p (c t)"), pb[:, 5 + 2 * g, 0:256],
                                        rho2[g][:, :, :].rearrange("p c t -> p (c t)"), ALU.add)
                        V.tensor_copy(gt[g][:, :, :].rearrange("p c t -> p (c t)"), pb[:, 5 + 2 * g, 256:384]).then_inc(rt_done[g], 1)
                    for c in range(2):
                        for g in range(2):
                            step = bass.ds(it * 2 + c, 1)
                            dve.wait_ge(es_done[g], f * ES + m * 2 + (c + 1))
                            V.tensor_scalar(esf[g][:, :], es[g][:, c, :], ff[:, g, step], None, ALU.mult).then_inc(esf_done[g], 1)
                            dve.wait_ge(esf_done[g], it * 2 + (c + 1))
                            dve.wait_ge(ph_done[g], it * 2 + (c + 1))
                            V.scalar_tensor_tensor(es[g][:, 1 - c, :], pb[:, 2 * g, c * HD:(c + 1) * HD], ff[:, g, step],
                                                   esf[g][:, :], ALU.mult, ALU.add).then_inc(es_done[g], 1)
                for g in range(2):
                    dve.wait_ge(es_done[g], f * ES + ES)

        @block.tensor
        def _(pe):
            mm = nc.tensor.matmul
            for g in range(2):
                pe.sem_inc(l_done[g], 1)
                pe.sem_inc(w_done[g], 1)

            with pe.Fori(0, KU) as f:
                with pe.Fori(0, M) as m:
                    it = f * M + m

                    def head_rows(u):
                        return slice((u % 2) * HD, (u % 2 + 1) * HD)

                    def staged_cols(g, c):
                        return slice((c ^ g) * P, ((c ^ g) + 1) * P)

                    for g in range(2):
                        pe.wait_ge(staged[g], it * 32 + 32)
                        pe.wait_ge(y_c[g], it + 1)
                        pe.wait_ge(es_done[g], f * ES + m * 2 + 1)
                        for a, i in enumerate((ALPHA, NBETA, KAPPA, VAL)):
                            for c in range(2):
                                n = a * 2 + c
                                ins = nc.tensor.transpose(pb[:, 2 * g + n // 4, (n % 4) * P:(n % 4 + 1) * P],
                                                          st[g][:, i, staged_cols(g, c)], ident[:, :])
                        ins.then_inc(tok_t[g], 1)
                    for p in range(2):
                        for g in range(2):
                            if p == 0:
                                pe.wait_ge(tok_c[g], it + 1)
                            else:
                                pe.wait_ge(qm_done[g], it * 2 + 1)
                            for hh in range(2):
                                u = 2 * p + hh
                                rows, c = head_rows(u), staged_cols(g, p)
                                moving = st[g][rows, ALPHA:RHO + 1, c]
                                mm(pb[:, 2 * g + hh, 0:2 * P], st[g][rows, NBETA, c], moving, start=True, stop=True)
                                ins = mm(pb[:, 2 * g + hh, 2 * P:4 * P], st[g][rows, KAPPA, c], moving, start=True, stop=True)
                            ins.then_inc(q_done[g], 1)
                    for g in range(2):
                        for u in range(4):
                            rows, c = head_rows(u), staged_cols(g, u // 2)
                            ins = mm(pb[:, 4 + 2 * g + u % 2, u // 2 * P:(u // 2 + 1) * P], st[g][rows, ALPHA, c], st[g][rows, NBETA, c],
                                     start=True, stop=True)
                        ins.then_inc(l_done[g], 1)
                    for g in range(2):
                        pe.wait_ge(qm_done[g], it * 2 + 2)
                        pe.wait_ge(tu_done[g], it + 1)
                        for u in range(4):
                            ins = mm(pb[:, 5 + 2 * g, u * HD:(u + 1) * HD], qm[g][:, u, 2 * P:3 * P],
                                     tok[g][:, 2, u // 2, head_rows(u)], start=True, stop=True)
                        ins.then_inc(mv_done[g], 1)
                    for i, b in enumerate(LEVELS):
                        for g in range(2):
                            if i == 0:
                                pe.wait_ge(tu_done[g], it + 1)
                            else:
                                pe.wait_ge(lev_done[g], it * NL + i)
                            for u in range(4):
                                ins = mm(pb[:, 4 + 2 * g, u * P:(u + 1) * P], qm[g][:, u, 0:P], T[g][:, u, :], start=True, stop=True)
                            ins.then_inc(x_done[g], 1)
                            if i:
                                if i == 1:
                                    pe.wait_ge(mv_c[g], it + 1)
                                for u in range(4):
                                    ins = nc.tensor.transpose(pb[:, 5 + 2 * g, u * P:(u + 1) * P], T[g][:, u, :], ident[:, :])
                                ins.then_inc(flipped[g], 1)
                        for g in range(2):
                            if i:
                                pe.wait_ge(u_done[g], it * (NL - 1) + i)
                            pe.wait_ge(xc_done[g], it * NL + (i + 1))
                            for u in range(4):
                                if i < NL - 1:
                                    ins = mm(pb[:, 2 * g + 1, u * 64:(u + 1) * 64], U[g][:, u, :], xc[g][:, u, :], start=True, stop=True)
                                else:
                                    ins = mm(pb[block_rows(g, 0), 5 + 2 * g, u * 64:(u + 1) * 64], xc[g][:, u, :], cols(U[g], u, g, b, 1), start=True, stop=True)
                            ins.then_inc(tx_done[g], 1)
                    for g in range(2):
                        pe.wait_ge(lev_done[g], it * NL + NL)
                        pe.wait_ge(mv_c[g], it + 1)
                        for u in range(4):
                            ins = mm(pb[:, 4 + 2 * g, u * P:(u + 1) * P], U[g][:, u, :], rhs[g][:, u, :], start=True, stop=True)
                        ins.then_inc(w_done[g], 1)
                    for g in range(2):
                        pe.wait_ge(w_c[g], it + 1)
                        for u in range(4):
                            rows, c = head_rows(u), u // 2
                            mm(pb[rows, 5 + 2 * g, c * P:(c + 1) * P], wt[g][:, u, 0:HD], qm[g][:, u, P:2 * P], start=True, stop=True)
                            ins = mm(pb[rows, 5 + 2 * g, 256 + c * HD:256 + (c + 1) * HD], wt[g][:, u, 0:HD], tok[g][:, 0, c, rows], start=True, stop=True)
                        ins.then_inc(rg_done[g], 1)
                    for c in range(2):
                        for g in range(2):
                            pe.wait_ge(rt_done[g], it + 2)
                            pe.wait_ge(es_done[g], f * ES + m * 2 + (c + 1))
                            for hh in range(2):
                                u = 2 * c + hh
                                rows = head_rows(u)
                                o = pb[rows, 2 * g, c * HD:(c + 1) * HD]
                                mm(o, tok[g][:, 1, c, rows], tok[g][:, 2, c, rows], start=True, stop=False)
                                mm(o, tok[g][:, 0, c, rows], wt[g][:, u, HD:P], start=False, stop=False)
                                ins = mm(o, gt[g][rows, c, :], es[g][rows, c, :], start=False, stop=True)
                            ins.then_inc(ph_done[g], 1)
                        for g in range(2):
                            for hh in range(2):
                                u = 2 * c + hh
                                rows = head_rows(u)
                                o = pb[:, y_bank(g, hh), c * HD:(c + 1) * HD]
                                mm(o, qm[g][:, u, 3 * P:4 * P], tok[g][:, 2, c, rows], start=True, stop=False)
                                mm(o, qm[g][:, u, P:2 * P], wt[g][:, u, HD:P], start=False, stop=False)
                                ins = mm(o, rt[g][rows, c, :], es[g][rows, c, :], start=False, stop=True)
                            if c == 1:
                                ins.then_inc(py_done[g], 1)


def finish_recurrence(nc, consts, ysum, bon, gate, ya_d):
    KU = WA // P
    NCH = S // P
    NV = 2 * NCH
    vec, ident = consts["vec"], consts["ident"]
    LNW, LNB = 7, 8
    with ExitStack() as ctx:
        s = Scope(nc, ctx, "ry")
        sq = s.sb("sq", [P, 2, NCH * P])
        out = s.sb("out", [P, KU, S])
        mean, var, root = (s.sb(n, [P, KU, NV]) for n in ("mean", "var", "root"))
        eps = s.sb("eps", [P, 1])
        ps = s.ps("ps", [P, KU, S])
        (eps_set, summed, mean_in, mean_out, centred, sq_done, var_in, root_done, rstd_out, yn_done, turned, scaled,
         y_plus, y_out, stored) = (s.sem(n) for n in (
             "eps_set", "summed", "mean_in", "mean_out", "centred", "sq_done", "var_in", "root_done", "rstd_out", "yn_done",
             "turned", "scaled", "y_plus", "y_out", "stored"))
        block = s.block()

        def tile(f):
            return ysum[:, 0, f * NCH:(f + 1) * NCH, :]

        def heads_of(t):
            return t.rearrange("p c (h e) -> p (c h) e", h=2)

        def spread(t, f):
            return t[:, f, :].unsqueeze(2).broadcast_to([P, NV, HD])

        @block.gpsimd
        def _(pool):
            nc.gpsimd.memset(eps[:, :], LNX_EPS).then_inc(eps_set, 1)
            for f in range(KU):
                pool.wait_ge(scaled, f + 1)
                nc.gpsimd.tensor_tensor(out[:, f, :], out[:, f, :], bon[:, f, :], ALU.add).then_inc(y_plus, 1)

        @block.vector
        def _(dve):
            V = nc.vector
            for f in range(KU):
                V.tensor_tensor(tile(f), tile(f), ysum[:, 1, f * NCH:(f + 1) * NCH, :], ALU.add).then_inc(summed, 1)
            for f in range(KU):
                dve.wait_ge(summed, f + 1)
                V.tensor_reduce(mean[:, f, :], heads_of(tile(f)), AX.X, ALU.add).then_inc(mean_in, 1)
            for f in range(KU):
                dve.wait_ge(mean_in, f + 1)
                V.tensor_scalar(mean[:, f, :], mean[:, f, :], 1.0 / HD, None, ALU.mult).then_inc(mean_out, 1)
            for f in range(KU):
                dve.wait_ge(mean_out, f + 1)
                V.tensor_tensor(heads_of(tile(f)), heads_of(tile(f)), spread(mean, f), ALU.subtract).then_inc(centred, 1)
            for f in range(KU):
                dve.wait_ge(sq_done, f + 1)
                V.tensor_reduce(var[:, f, :], sq[:, f % 2, :].rearrange("p (v e) -> p v e", e=HD), AX.X, ALU.add).then_inc(var_in, 1)
            for f in range(KU):
                dve.wait_ge(root_done, f + 1)
                V.reciprocal(root[:, f, :], root[:, f, :]).then_inc(rstd_out, 1)
                dve.wait_ge(rstd_out, f + 1)
                V.tensor_tensor(heads_of(tile(f)), heads_of(tile(f)), spread(root, f), ALU.mult).then_inc(yn_done, 1)
            for f in range(KU):
                dve.wait_ge(y_plus, f + 1)
                V.tensor_tensor(out[:, f, :], out[:, f, :], gate[:, f, :], ALU.mult).then_inc(y_out, 1)

        @block.scalar
        def _(act):
            for f in range(KU):
                act.wait_ge(centred, f + 1)
                if f >= 2:
                    act.wait_ge(var_in, f - 1)
                nc.scalar.activation(sq[:, f % 2, :], tile(f).rearrange("p c n -> p (c n)"), ACT.Square).then_inc(sq_done, 1)
            act.wait_ge(eps_set, 1)
            for f in range(KU):
                act.wait_ge(var_in, f + 1)
                nc.scalar.activation(root[:, f, :], var[:, f, :], ACT.Sqrt, scale=1.0 / HD, bias=eps[:, 0:1]).then_inc(root_done, 1)
            for f in range(KU):
                act.wait_ge(turned, f + 1)
                nc.scalar.activation(out[:, f, :], ps[:, f, :], ACT.Identity, scale=vec[:, LNW, f:f + 1],
                                     bias=vec[:, LNB, f:f + 1]).then_inc(scaled, 1)

        @block.tensor
        def _(pe):
            for f in range(KU):
                pe.wait_ge(yn_done, f + 1)
                for c in range(NCH):
                    ins = nc.tensor.transpose(ps[:, f, c * P:(c + 1) * P], ysum[:, 0, f * NCH + c, :], ident[:, :])
                ins.then_inc(turned, 1)

        @block.sync
        def _(sp):
            for f in range(KU):
                sp.wait_ge(y_out, f + 1)
                sp.dma_start(ya_d[f * P:(f + 1) * P, :], out[:, f, :]).then_inc(stored, 16)
            sp.wait_ge(stored, 16 * KU)


def gather_mixed(nc, ya_d, yb_d, consts, y_hi, y_lo):
    ident = consts["ident"]
    KU = WA // P
    with ExitStack() as ctx:
        s = Scope(nc, ctx, "gather")
        ya = s.sb("ya", [P, KU, S])
        yb = s.sb("yb", [P, TT, WA])
        y32 = s.sb("y32", [P, KU, S])
        ps = s.ps("ps", [P, 4, HALF])
        a_loaded, b_loaded, turned, copied, hi_done, lo_done = (s.sem(n) for n in (
            "a_loaded", "b_loaded", "turned", "copied", "hi_done", "lo_done"))
        block = s.block()

        @block.sync
        def _(sp):
            sp.dma_start(yb[:, :, :], yb_d.rearrange("(t p) n -> p t n", p=P)).then_inc(b_loaded, 16)
            sp.dma_start(ya[:, :, :], ya_d.rearrange("(t p) s -> p t s", p=P)).then_inc(a_loaded, 16)

        @block.tensor
        def _(pe):
            pe.wait_ge(b_loaded, 16)
            for n in range(2 * KU):
                f, half = divmod(n, 2)
                if n >= 4:
                    pe.wait_ge(copied, n - 3)
                for t in range(4):
                    ins = nc.tensor.transpose(ps[:, n % 4, t * P:(t + 1) * P], yb[:, half * 4 + t, f * P:(f + 1) * P], ident[:, :])
                ins.then_inc(turned, 1)

        @block.vector
        def _(dve):
            for n in range(2 * KU):
                f, half = divmod(n, 2)
                dve.wait_ge(turned, n + 1)
                nc.vector.tensor_copy(y32[:, f, half * HALF:(half + 1) * HALF], ps[:, n % 4, :]).then_inc(copied, 1)

        @block.scalar
        def _(act):
            act.wait_ge(a_loaded, 16)
            for f in range(KU):
                nc.scalar.activation(y_hi[:, f, :], ya[:, f, :], ACT.Copy).then_inc(hi_done, 1)
            for f in range(KU):
                act.wait_ge(copied, 2 * f + 2)
                nc.scalar.activation(y_hi[:, KU + f, :], y32[:, f, :], ACT.Copy).then_inc(hi_done, 1)

        @block.gpsimd
        def _(pool):
            for f in range(2 * KU):
                pool.wait_ge(hi_done, f + 1)
                src = ya[:, f, :] if f < KU else y32[:, f - KU, :]
                nc.gpsimd.tensor_tensor(y_lo[:, f, :], src, y_hi[:, f, :].bitcast(F32), ALU.subtract).then_inc(lo_done, 1)


def output_product(nc, name, w_rows, a_hi, a_lo, y):
    w_v = w_rows.rearrange("(t p) n -> t p n", p=P)
    with ExitStack() as ctx:
        s = Scope(nc, ctx, name)
        w_raw = s.sb("w_raw", [P, 3, D])
        w_hi = s.sb("w_hi", [P, KT, D], F32R)
        w_lo = s.sb("w_lo", [P, KT, D], F32R)
        ps = s.ps("ps", [P, 4, HALF])
        raw_loaded = [s.sem(f"raw_loaded{j}") for j in range(3)]
        hi_done, lo_done, mm_done, y_done = s.sem("hi_done"), s.sem("lo_done"), s.sem("mm_done"), s.sem("y_done")
        block = s.block()

        @block.sync
        def _(sp):
            for k in range(KT):
                if k >= 3:
                    sp.wait_ge(lo_done, k - 2)
                sp.dma_start(w_raw[:, k % 3, :], w_v[k]).then_inc(raw_loaded[k % 3], 16)

        @block.scalar
        def _(act):
            for k in range(KT):
                act.wait_ge(raw_loaded[k % 3], 16 * (k // 3 + 1))
                nc.scalar.activation(w_hi[:, k, :], w_raw[:, k % 3, :], ACT.Copy).then_inc(hi_done, 1)

        @block.gpsimd
        def _(pool):
            for k in range(KT):
                pool.wait_ge(hi_done, k + 1)
                nc.gpsimd.tensor_tensor(w_lo[:, k, :], w_raw[:, k % 3, :], w_hi[:, k, :].bitcast(F32), ALU.subtract).then_inc(lo_done, 1)

        @block.vector
        def _(dve):
            for n in range(2 * TT):
                t, half = divmod(n, 2)
                dve.wait_ge(mm_done, n + 1)
                nc.vector.tensor_copy(y[:, t, half * HALF:(half + 1) * HALF], ps[:, n % 4, :]).then_inc(y_done, 1)

        @block.tensor
        def _(pe):
            for n in range(2 * TT):
                t, half = divmod(n, 2)
                span = slice(half * HALF, (half + 1) * HALF)
                if n >= 4:
                    pe.wait_ge(y_done, n - 3)
                for k in range(KT):
                    if n == 0:
                        pe.wait_ge(lo_done, k + 1)
                    ins = split_products(nc, ps[:, n % 4, :], a_hi[:, k, t * P:(t + 1) * P], a_lo[:, k, t * P:(t + 1) * P],
                                         w_hi[:, k, span], w_lo[:, k, span], k == 0, k == KT - 1)
                ins.then_inc(mm_done, 1)


def residual(nc, name, y, x_src, gate_row, norm_row, x_dst):
    with ExitStack() as ctx:
        s = Scope(nc, ctx, name)
        x = s.sb("x", [P, TT, D])
        sq = s.sb("sq", [P, D])
        gate = s.sb("gate", [P, D])
        norm = s.sb("norm", [P, D])
        ss = s.sb("ss", [P, TT])
        ms = s.sb("ms", [P, TT])
        rstd = s.sb("rstd", [P, TT])
        mhalf = s.sb("mhalf", [P, 1])
        x_loaded = [s.sem(f"x_loaded{t}") for t in range(TT)]
        row_loaded, gain_done, half_done, ss_done, ms_done, rstd_done, scaled, even_done, odd_done, stored = (s.sem(n) for n in (
            "row_loaded", "gain_done", "half_done", "ss_done", "ms_done", "rstd_done", "scaled", "even_done", "odd_done", "stored"))
        block = s.block()

        @block.sync
        def _(sp):
            sp.dma_start(gate[:, :], gate_row.rearrange("(o n) -> o n", o=1).broadcast_to([P, D])).then_inc(row_loaded, 16)
            sp.dma_start(norm[:, :], norm_row.rearrange("(o n) -> o n", o=1).broadcast_to([P, D])).then_inc(row_loaded, 16)
            for t in range(TT):
                sp.dma_start(x[:, t, :], x_src[t * P:(t + 1) * P, :]).then_inc(x_loaded[t], 16)
            for t in range(TT):
                sp.wait_ge((even_done, odd_done)[t % 2], t // 2 + 1)
                sp.dma_start(x_dst[t * P:(t + 1) * P, :], x[:, t, :]).then_inc(stored, 16)
            sp.wait_ge(stored, 16 * TT)

        @block.scalar
        def _(act):
            for t in range(TT):
                if t:
                    act.wait_ge(ss_done, t)
                nc.scalar.activation(sq[:, :], y[:, t, :], ACT.Square, accum_out=ss[:, t:t + 1]).then_inc(ss_done, 1)

        @block.gpsimd
        def _(pool):
            nc.gpsimd.memset(mhalf[:, :], -0.5).then_inc(half_done, 1)
            pool.wait_ge(half_done, 1)
            for q in range(2):
                span = slice(4 * q, 4 * q + 4)
                pool.wait_ge(ms_done, q + 1)
                nc.gpsimd.tensor_tensor(rstd[:, span], ms[:, span], mhalf[:, 0:1].broadcast_to([P, 4]), ALU.pow).then_inc(rstd_done, 1)
            for t in range(0, TT, 2):
                pool.wait_ge(scaled, t + 1)
                pool.wait_ge(x_loaded[t], 16)
                nc.gpsimd.tensor_tensor(x[:, t, :], x[:, t, :], y[:, t, :], ALU.add).then_inc(even_done, 1)

        @block.vector
        def _(dve):
            dve.wait_ge(row_loaded, 32)
            nc.vector.tensor_tensor(gate[:, :], gate[:, :], norm[:, :], ALU.mult).then_inc(gain_done, 1)
            for q in range(2):
                span = slice(4 * q, 4 * q + 4)
                dve.wait_ge(ss_done, 4 * q + 4)
                nc.vector.tensor_scalar(ms[:, span], ss[:, span], 1.0 / D, RMS_EPS, ALU.mult, ALU.add).then_inc(ms_done, 1)
            dve.wait_ge(gain_done, 1)
            for t in range(TT):
                dve.wait_ge(rstd_done, t // 4 + 1)
                nc.vector.scalar_tensor_tensor(y[:, t, :], y[:, t, :], rstd[:, t:t + 1], gate[:, :], ALU.mult, ALU.mult).then_inc(scaled, 1)
                if t % 2:
                    dve.wait_ge(scaled, t + 1)
                    dve.wait_ge(x_loaded[t], 16)
                    nc.vector.tensor_tensor(x[:, t, :], x[:, t, :], y[:, t, :], ALU.add).then_inc(odd_done, 1)


def conv_glu(nc, name, l, up_w, down_w, conv_cols, h_hi, h_lo, y):
    NG = FT // 2
    up_v = up_w.rearrange("(t p) (m c) -> m p t c", p=P, c=P)
    down_v = down_w.rearrange("(m p) n -> m p n", p=P)
    with ExitStack() as ctx:
        s = Scope(nc, ctx, name)
        u_raw = s.sb("u_raw", [P, 4, KT, P])
        u_hi = s.sb("u_hi", [P, 2, KT, P], F32R)
        u_lo = s.sb("u_lo", [P, 2, KT, P], F32R)
        d_raw = s.sb("d_raw", [P, 2, D])
        d_hi = s.sb("d_hi", [P, 2, D], F32R)
        d_lo = s.sb("d_lo", [P, 2, D], F32R)
        z = s.sb("z", [P, 4, S])
        a_hi = s.sb("a_hi", [P, 2, S], F32R)
        a_lo = s.sb("a_lo", [P, 2, S], F32R)
        ps_u = s.ps("ps_u", [P, 2, S])
        ps_d = s.ps("ps_d", [P, 4, HALF])
        u_loaded = [s.sem(f"u_loaded{j}") for j in range(4)]
        d_loaded = [s.sem(f"d_loaded{j}") for j in range(2)]
        (uhi_done, ulo_done, umm_done, mid_done, left_done, conv_done, gelu_done, glu_done, ahi_done, alo_done, dhi_done,
         dlo_done, share_done, added, zeroed) = (s.sem(n) for n in (
             "uhi_done", "ulo_done", "umm_done", "mid_done", "left_done", "conv_done", "gelu_done", "glu_done", "ahi_done",
             "alo_done", "dhi_done", "dlo_done", "share_done", "added", "zeroed"))
        block = s.block()

        def tile_of(g, j):
            return g * 2 + (j // 2 + (j % 2) * FT)

        @block.sync
        def _(sp):
            def load_up(g, j):
                sp.dma_start(u_raw[:, j], up_v[bass.ds(tile_of(g, j), 1)].rearrange("o p t c -> p (o t) c")).then_inc(u_loaded[j], 16)

            def load_down(g, j):
                sp.dma_start(d_raw[:, j, :], down_v[bass.ds(g * 2 + j, 1)].rearrange("o p n -> p (o n)")).then_inc(d_loaded[j], 16)

            for j in range(4):
                load_up(0, j)
            for j in range(2):
                load_down(0, j)
            with sp.Fori(0, NG - 1) as g:
                for j in range(4):
                    sp.wait_ge(ulo_done, g * 4 + (j + 1))
                    load_up(g + 1, j)
                for j in range(2):
                    sp.wait_ge(dlo_done, g * 2 + (j + 1))
                    load_down(g + 1, j)

        @block.scalar
        def _(act):
            A = nc.scalar.activation

            def split(g, j):
                act.wait_ge(u_loaded[j], g * 16 + 16)
                act.wait_ge(umm_done, g * 4 + (j + 1))
                A(u_hi[:, j % 2], u_raw[:, j], ACT.Copy).then_inc(uhi_done, 1)

            def split_down(g):
                act.wait_ge(share_done, g * (2 * TT) + 1)
                for j in range(2):
                    act.wait_ge(d_loaded[j], g * 16 + 16)
                    A(d_hi[:, j, :], d_raw[:, j, :], ACT.Copy).then_inc(dhi_done, 1)

            def middle(g, j):
                act.wait_ge(umm_done, g * 4 + (j + 3))
                act.wait_ge(alo_done, g * 2 + (j // 2 + 1))
                A(z[:, j, :], ps_u[:, j % 2, :], ACT.Copy, scale=conv_cols[:, 1, bass.ds(tile_of(g, j), 1)]).then_inc(mid_done, 1)

            def gelu(g, p):
                act.wait_ge(conv_done, g * 4 + (2 * p + 3))
                A(z[:, 2 * p, :], z[:, 2 * p, :], ACT.Gelu_apprx_tanh).then_inc(gelu_done, 1)
                act.wait_ge(glu_done, g * 2 + (p + 1))
                act.wait_ge(share_done, g * (2 * TT) + 1)
                A(a_hi[:, p, :], z[:, 2 * p, :], ACT.Copy).then_inc(ahi_done, 1)

            def turn(g, last):
                split(g, 1)
                middle(g, 0)
                split(g, 2)
                middle(g, 1)
                split(g, 3)
                gelu(g, 0)
                split_down(g)
                middle(g, 2)
                if not last:
                    split(g + 1, 0)
                middle(g, 3)
                gelu(g, 1)

            split(0, 0)
            with act.Fori(0, NG - 1) as g:
                turn(g, False)
            turn(NG - 1, True)

        @block.gpsimd
        def _(pool):
            G = nc.gpsimd

            def split(g, j):
                pool.wait_ge(uhi_done, g * 4 + (j + 1))
                G.tensor_tensor(u_lo[:, j % 2], u_raw[:, j], u_hi[:, j % 2].bitcast(F32), ALU.subtract).then_inc(ulo_done, 1)

            def split_down(g):
                for j in range(2):
                    pool.wait_ge(dhi_done, g * 2 + (j + 1))
                    G.tensor_tensor(d_lo[:, j, :], d_raw[:, j, :], d_hi[:, j, :].bitcast(F32), ALU.subtract).then_inc(dlo_done, 1)

            def split_product(g, p):
                pool.wait_ge(ahi_done, g * 2 + (p + 1))
                G.tensor_tensor(a_lo[:, p, :], z[:, 2 * p, :], a_hi[:, p, :].bitcast(F32), ALU.subtract).then_inc(alo_done, 1)

            def turn(g, last):
                split(g, 1)
                split(g, 2)
                split(g, 3)
                split_product(g, 0)
                split_down(g)
                if not last:
                    split(g + 1, 0)
                split_product(g, 1)

            pool.sem_inc(alo_done, 2)
            split(0, 0)
            with pool.Fori(0, NG - 1) as g:
                turn(g, False)
            turn(NG - 1, True)

        @block.vector
        def _(dve):
            V = nc.vector

            def convolve(g, j):
                dve.wait_ge(mid_done, g * 4 + (j + 1))
                V.scalar_tensor_tensor(z[:, j, 1:S], ps_u[:, j % 2, 0:S - 1], conv_cols[:, 0, bass.ds(tile_of(g, j), 1)],
                                       z[:, j, 1:S], ALU.mult, ALU.add).then_inc(left_done, 1)
                dve.wait_ge(left_done, g * 4 + (j + 1))
                V.scalar_tensor_tensor(z[:, j, 0:S - 1], ps_u[:, j % 2, 1:S], conv_cols[:, 2, bass.ds(tile_of(g, j), 1)],
                                       z[:, j, 0:S - 1], ALU.mult, ALU.add).then_inc(conv_done, 1)

            def product(g, p):
                dve.wait_ge(conv_done, g * 4 + (2 * p + 4))
                dve.wait_ge(gelu_done, g * 2 + (p + 1))
                V.tensor_tensor(z[:, 2 * p, :], z[:, 2 * p, :], z[:, 2 * p + 1, :], ALU.mult).then_inc(glu_done, 1)

            def add_share(g):
                for n in range(2 * TT):
                    t, half = divmod(n, 2)
                    dst = y[:, t, half * HALF:(half + 1) * HALF]
                    dve.wait_ge(share_done, g * (2 * TT) + (n + 2))
                    V.tensor_tensor(dst, ps_d[:, n % 4, :], dst, ALU.add).then_inc(added, 1)

            def rest(g):
                convolve(g, 1)
                product(g, 0)
                convolve(g, 2)
                convolve(g, 3)
                product(g, 1)

            V.memset(y[:, :, :], 0.0).then_inc(zeroed, 1)
            dve.sem_inc(conv_done, 2)
            dve.sem_inc(added, 4)
            dve.wait_ge(zeroed, 1)
            convolve(0, 0)
            with dve.Fori(0, NG - 1) as g:
                rest(g)
                convolve(g + 1, 0)
                add_share(g)
            rest(NG - 1)
            add_share(NG - 1)

        @block.tensor
        def _(pe):
            def up(g, j):
                pe.wait_ge(ulo_done, g * 4 + (j + 1))
                pe.wait_ge(conv_done, g * 4 + (j + 1))
                for half in range(2):
                    span = slice(half * HALF, (half + 1) * HALF)
                    for k in range(KT):
                        ins = split_products(nc, ps_u[:, j % 2, span], u_hi[:, j % 2, k, :], u_lo[:, j % 2, k, :],
                                             h_hi[:, k, span], h_lo[:, k, span], k == 0, k == KT - 1)
                ins.then_inc(umm_done, 1)

            def share(g):
                pe.wait_ge(dlo_done, g * 2 + 2)
                pe.wait_ge(alo_done, g * 2 + 4)
                for n in range(2 * TT):
                    t, half = divmod(n, 2)
                    span = slice(half * HALF, (half + 1) * HALF)
                    pe.wait_ge(added, g * (2 * TT) + (n + 1))
                    for p in range(2):
                        ins = split_products(nc, ps_d[:, n % 4, :], a_hi[:, p, t * P:(t + 1) * P], a_lo[:, p, t * P:(t + 1) * P],
                                             d_hi[:, p, span], d_lo[:, p, span], p == 0, p == 1)
                    ins.then_inc(share_done, 1)

            pe.sem_inc(umm_done, 2)
            pe.sem_inc(share_done, 1)
            up(0, 0)
            with pe.Fori(0, NG - 1) as g:
                for j in range(1, 4):
                    up(g, j)
                up(g + 1, 0)
                share(g)
            for j in range(1, 4):
                up(NG - 1, j)
            share(NG - 1)


def fourier(nc, tab, h_hi, h_lo):
    GR = KT
    H = S // 2
    with ExitStack() as ctx:
        s = Scope(nc, ctx, "fft")
        raw = s.sb("raw", [P, 4, H])
        fe_raw = s.sb("fe_raw", [P, 2 * P])
        al_raw = s.sb("al_raw", [P, TT, 2])
        fe_hi, fe_lo = s.sb("fe_hi", [P, 2 * P], F32R), s.sb("fe_lo", [P, 2 * P], F32R)
        al_hi, al_lo = s.sb("al_hi", [P, TT, 2], F32R), s.sb("al_lo", [P, TT, 2], F32R)
        tk_hi, tk_lo = s.sb("tk_hi", [P, 2, TT, H], F32R), s.sb("tk_lo", [P, 2, TT, H], F32R)
        uv_hi, uv_lo = s.sb("uv_hi", [P, 2, TT, 2, P], F32R), s.sb("uv_lo", [P, 2, TT, 2, P], F32R)
        e = s.sb("e", [P, H + 2])
        f32 = s.sb("f32", [P, S])
        ps_uv = s.ps("uv", [P, TT // 2, 512])
        ps_e, ps_o, ps_m = s.ps("pe", [P, H]), s.ps("po", [P, H]), s.ps("pm", [P, 512])
        NR = 2 * TT
        small_loaded, small_hi, small_lo = s.sem("small_loaded"), s.sem("small_hi"), s.sem("small_lo")
        raw_loaded = [s.sem(f"raw_loaded{j}") for j in range(4)]
        tk_hi_done, tk_lo_done, uv_mm, uv_hi_done, uv_lo_done = (s.sem(n) for n in (
            "tk_hi_done", "tk_lo_done", "uv_mm", "uv_hi_done", "uv_lo_done"))
        e_mm, o_mm, e_copied, f_done, f_hi_done, f_lo_done = (s.sem(n) for n in (
            "e_mm", "o_mm", "e_copied", "f_done", "f_hi_done", "f_lo_done"))
        block = s.block()
        tok_v = tab["fft_tokens"].rearrange("a (t p) k -> a t p k", p=P)

        @block.sync
        def _(sp):
            sp.dma_start(fe_raw[:, :], tab["fft_features"]).then_inc(small_loaded, 16)
            sp.dma_start(al_raw[:, :, :], tab["fft_middle"].rearrange("(t p) k -> p t k", p=P)).then_inc(small_loaded, 16)
            for n in range(NR):
                a, t = divmod(n, TT)
                if n >= 4:
                    sp.wait_ge(tk_lo_done, n - 3)
                sp.dma_start(raw[:, n % 4, :], tok_v[a, t]).then_inc(raw_loaded[n % 4], 16)

        @block.scalar
        def _(act):
            A = nc.scalar.activation
            act.wait_ge(small_loaded, 32)
            A(fe_hi[:, :], fe_raw[:, :], ACT.Copy)
            A(al_hi[:, :, :], al_raw[:, :, :], ACT.Copy).then_inc(small_hi, 1)

            def split_tables(lo, hi):
                for n in range(lo, hi):
                    a, t = divmod(n, TT)
                    act.wait_ge(raw_loaded[n % 4], 16 * (n // 4 + 1))
                    A(tk_hi[:, a, t, :], raw[:, n % 4, :], ACT.Copy).then_inc(tk_hi_done, 1)

            def split_uv(g):
                for q in range(TT // 2):
                    act.wait_ge(uv_mm, g * (TT // 2) + q + 1)
                    dst = uv_hi[:, g % 2, 2 * q:2 * q + 2].rearrange("p t a e -> p (t a e)")
                    A(dst, ps_uv[:, q, :], ACT.Copy).then_inc(uv_hi_done, 1)

            split_tables(0, TT)
            split_uv(0)
            split_tables(TT, NR)
            for g in range(GR):
                act.wait_ge(e_mm, g + 1)
                if g:
                    act.wait_ge(f_done, g)
                A(e[:, 0:H], ps_e[:, :], ACT.Copy)
                A(e[:, H:H + 2], ps_m[:, 0:2], ACT.Copy).then_inc(e_copied, 1)
                if g + 1 < GR:
                    split_uv(g + 1)
                act.wait_ge(f_done, g + 1)
                A(h_hi[:, g, :], f32[:, :], ACT.Copy).then_inc(f_hi_done, 1)

        @block.gpsimd
        def _(pool):
            G = nc.gpsimd
            pool.wait_ge(small_hi, 1)
            G.tensor_tensor(fe_lo[:, :], fe_raw[:, :], fe_hi[:, :].bitcast(F32), ALU.subtract)
            G.tensor_tensor(al_lo[:, :, :], al_raw[:, :, :], al_hi[:, :, :].bitcast(F32), ALU.subtract).then_inc(small_lo, 1)
            for n in range(NR):
                a, t = divmod(n, TT)
                pool.wait_ge(tk_hi_done, n + 1)
                G.tensor_tensor(tk_lo[:, a, t, :], raw[:, n % 4, :], tk_hi[:, a, t, :].bitcast(F32), ALU.subtract).then_inc(tk_lo_done, 1)
            for g in range(GR):
                pool.wait_ge(f_hi_done, g + 1)
                G.tensor_tensor(h_lo[:, g, :], f32[:, :], h_hi[:, g, :].bitcast(F32), ALU.subtract).then_inc(f_lo_done, 1)

        @block.vector
        def _(dve):
            V = nc.vector

            def split_uv(g):
                for q in range(TT // 2):
                    n = g * (TT // 2) + q
                    dve.wait_ge(uv_hi_done, n + 1)
                    hi = uv_hi[:, g % 2, 2 * q:2 * q + 2].rearrange("p t a e -> p (t a e)")
                    lo = uv_lo[:, g % 2, 2 * q:2 * q + 2].rearrange("p t a e -> p (t a e)")
                    V.tensor_tensor(lo, ps_uv[:, q, :], hi.bitcast(F32), ALU.subtract).then_inc(uv_lo_done, 1)

            split_uv(0)
            for g in range(GR):
                if g + 1 < GR:
                    split_uv(g + 1)
                dve.wait_ge(o_mm, g + 1)
                dve.wait_ge(e_copied, g + 1)
                if g:
                    dve.wait_ge(f_lo_done, g)
                V.tensor_tensor(f32[:, 0:H], e[:, 0:H], ps_o[:, :], ALU.subtract)
                V.tensor_tensor(f32[:, :H:-1], e[:, 1:H], ps_o[:, 1:H], ALU.add)
                V.tensor_copy(f32[:, H:H + 1], e[:, H:H + 1]).then_inc(f_done, 1)

        @block.tensor
        def _(pe):
            def over_features(g):
                for t in range(TT):
                    if t % 2 == 0 and g:
                        pe.wait_ge(uv_lo_done, (g - 1) * (TT // 2) + t // 2 + 1)
                    out = ps_uv[:, t // 2, (t % 2) * 2 * P:(t % 2 + 1) * 2 * P]
                    ins = split_products(nc, out, h_hi[:, g, t * P:(t + 1) * P], h_lo[:, g, t * P:(t + 1) * P], fe_hi[:, :], fe_lo[:, :], True, True)
                    if t % 2 == 1:
                        ins.then_inc(uv_mm, 1)

            def over_tokens(g, a, out):
                for t in range(TT):
                    if g == 0:
                        pe.wait_ge(tk_lo_done, a * TT + t + 1)
                    ins = split_products(nc, out, uv_hi[:, g % 2, t, a, :], uv_lo[:, g % 2, t, a, :], tk_hi[:, a, t, :], tk_lo[:, a, t, :],
                                         t == 0, t == TT - 1)
                return ins

            pe.wait_ge(small_lo, 1)
            over_features(0)
            for g in range(GR):
                pe.wait_ge(uv_lo_done, (g + 1) * (TT // 2))
                if g:
                    pe.wait_ge(e_copied, g)
                over_tokens(g, 0, ps_e[:, :])
                for t in range(TT):
                    ins = split_products(nc, ps_m[:, 0:2], uv_hi[:, g % 2, t, 0, :], uv_lo[:, g % 2, t, 0, :], al_hi[:, t, :], al_lo[:, t, :],
                                         t == 0, t == TT - 1)
                ins.then_inc(e_mm, 1)
                if g + 1 < GR:
                    over_features(g + 1)
                if g:
                    pe.wait_ge(f_done, g)
                over_tokens(g, 1, ps_o[:, :]).then_inc(o_mm, 1)


SCRATCH = {
    "mod": (2, 6 * D),
    "qk": (2, WA, S),
    "v": (S, WA),
    "z": (4 * WA // P, P, S),
    "st": (2, (WA // P) * (S // (2 * P)), 4, P, 2 * P),
    "ya": (WA, S),
    "yb": (S, WA),
    "x1": (S, D),
    "x2": (S, D),
    "x3": (S, D),
}


def tables():
    half = HD // 2
    inv = (np.float32(10000.0) ** (-np.arange(half, dtype=np.float32) / np.float32(half))).astype(np.float32)
    ang = np.arange(S, dtype=np.float32)[:, None] * inv[None, :]
    cos, sin = np.cos(ang), np.sin(ang)
    away = np.arange(2 * S - P)[None, :] - np.arange(P)[:, None] - (S - P)
    n = (np.abs(away) <= 64) * 1 + ((np.abs(away) <= 256) & (away % 4 == 0)) + (away % 16 == 0)
    bias = np.where(n > 0, 8.0 * np.log(np.maximum(n, 1)), NEG_BIG).astype(np.float32)
    row, col = np.arange(P)[:, None], np.arange(P)[None, :]
    pred, first, level = [], [], []
    for g in range(2):
        before = (row < col) if g == 0 else (row > col)
        upto = before | (row == col)
        pred.append(np.concatenate([before, upto, before, upto], 1))
        pair = (row // 2 == col // 2)
        first.append(np.stack([pair & before.T, pair & before]))
        lv = []
        for b in LEVELS:
            c = np.arange(64)[None, :] // b
            lv.append((row // (2 * b) == c) & ((row // b) % 2 == 1 - g))
        level.append(np.stack(lv))
    k = np.arange(S)[:, None] * np.arange(S // 2)[None, :] % S * (2 * np.pi / S)
    q = np.arange(P)[:, None] * np.arange(P)[None, :] % P * (2 * np.pi / P)
    features = np.concatenate([np.cos(q), np.sin(q)], 1) / np.sqrt(float(S * P))
    middle = np.repeat(np.where(np.arange(S) % 2 == 0, 1.0, -1.0)[:, None], 2, 1)
    return {
        "fft_tokens": np.stack([np.cos(k), np.sin(k)]).astype(np.float32),
        "fft_features": features.astype(np.float32),
        "fft_middle": middle.astype(np.float32),
        "att_bias": bias,
        "rwkv_pred": np.stack(pred).astype(np.uint32),
        "rwkv_first": np.stack(first).astype(np.uint32),
        "rwkv_level": np.stack(level).astype(np.float32),
        "rope_cos": np.concatenate([cos, cos], 1).astype(np.float32),
        "rope_sin": np.concatenate([-sin, sin], 1).astype(np.float32),
    }


def glu_layer(nc, l, a, mod, consts, x_src, x_dst, y):
    with ExitStack() as ctx:
        hs = Scope(nc, ctx, f"g{l}")
        h_hi, h_lo = hs.sb("hi", [P, KT, S], F32R), hs.sb("lo", [P, KT, S], F32R)
        norm_to_features(nc, f"ng{l}", x_src, a["norm_g"][l, 2], mod[l], 3 * D, consts, h_hi, h_lo)
        conv_glu(nc, f"cg{l}", l, a["ffn_up"][l], a["ffn_down"][l], consts["conv_f"][:, l], h_hi, h_lo, y)
    residual(nc, f"rg{l}", y, x_src, mod[l, 5 * D:6 * D], a["norm_g"][l, 3], x_dst)


def build(nc, a, tab, out, dbg=()):
    scr = {n: nc.dram_tensor(f"scr_{n}", shape, F32, kind="ExternalOutput" if n in dbg else "Internal").ap()
           for n, shape in SCRATCH.items()}
    x0 = a["x"][0]
    with ExitStack() as ctx:
        top = Scope(nc, ctx, "top")
        consts = {
            "ident": top.sb("ident", [P, P]),
            "heads": top.sb("heads", [P, P]),
            "conv_a": top.sb("conv_a", [P, 3, 4 * WA // P]),
            "conv_f": top.sb("conv_f", [P, 2, 3, 2 * FT]),
            "vec": top.sb("vec", [P, 9, 4]),
        }
        make_constants(nc, consts)
        groups = [(a["mix_conv"][0].rearrange("w (m p) -> (w m) p", p=P), consts["conv_a"][:, :, :].rearrange("p w m -> p (w m)"))]
        for l in range(2):
            for w in range(3):
                groups.append((a["ffn_conv"][l, w].rearrange("(m p) -> m p", p=P), consts["conv_f"][:, l, w, :]))
        vecs = [a["rwkv_w0"][0, 0], a["rwkv_w0"][0, 1], a["rwkv_a0"][0, 0], a["rwkv_a0"][0, 1], a["rwkv_k_k"][0], a["rwkv_k_a"][0],
                a["rwkv_r_k"][0].rearrange("h e -> (h e)"), a["rwkv_lnx_w"][0], a["rwkv_lnx_b"][0]]
        for i, v in enumerate(vecs):
            groups.append((v.rearrange("(m p) -> m p", p=P), consts["vec"][:, i, :]))
        load_columns(nc, groups, consts)
        modulation(nc, a["c"], a["ada_w"], a["ada_b"], scr["mod"])
        with ExitStack() as hctx:
            hs = Scope(nc, hctx, "h0")
            h_hi, h_lo = hs.sb("hi", [P, KT, S], F32R), hs.sb("lo", [P, KT, S], F32R)
            norm_to_features(nc, "n0", x0, a["norm_g"][0, 0], scr["mod"][0], 0, consts, h_hi, h_lo)
            project_qkv(nc, a["mix_in"], h_hi, h_lo, consts, tab["rope_cos"], tab["rope_sin"], scr["qk"], scr["v"])
            project_convolved(nc, a["mix_in"], consts["conv_a"], h_hi, h_lo, scr["z"])
        with ExitStack() as actx:
            dilated_attention(nc, scr["qk"], scr["v"], tab["att_bias"], consts, scr["yb"])
        with ExitStack() as rctx:
            rs = Scope(nc, rctx, "lt")
            tw, ta, tg = (rs.sb(n, [P, S]) for n in ("tw", "ta", "tg"))
            lora_hidden(nc, scr["z"], a["rwkv_w1"], a["rwkv_a1"], a["rwkv_g1"], tw, ta, tg)
            ff = rs.sb("ff", [P, 2, (WA // P) * (S // P)])
            bon, gate_a = rs.sb("bon", [P, WA // P, S]), rs.sb("gate", [P, WA // P, S])
            prepare_recurrence(nc, scr["z"], a["rwkv_w2"], a["rwkv_a2"], a["rwkv_g2"], consts, tw, ta, tg, ff, bon, gate_a, scr["st"])
            ysum = rs.sb("ysum", [P, 2, (WA // P) * (S // P), P])
            recurrence(nc, scr["z"], scr["st"], tab, consts, ff, ysum)
            finish_recurrence(nc, consts, ysum, bon, gate_a, scr["ya"])
        mod = scr["mod"]

        def gate(l, i):
            return mod[l, i * D:(i + 1) * D]

        with ExitStack() as yctx:
            y = Scope(nc, yctx, "y0").sb("y", [P, TT, D])
            with ExitStack() as hctx:
                hs = Scope(nc, hctx, "m0")
                m_hi, m_lo = hs.sb("hi", [P, KT, S], F32R), hs.sb("lo", [P, KT, S], F32R)
                gather_mixed(nc, scr["ya"], scr["yb"], consts, m_hi, m_lo)
                output_product(nc, "mo", a["mix_out"][0], m_hi, m_lo, y)
            residual(nc, "r0", y, x0, gate(0, 2), a["norm_g"][0, 1], scr["x1"])
            glu_layer(nc, 0, a, mod, consts, scr["x1"], scr["x2"], y)
        with ExitStack() as hctx:
            hs = Scope(nc, hctx, "f1")
            h_hi, h_lo = hs.sb("hi", [P, KT, S], F32R), hs.sb("lo", [P, KT, S], F32R)
            norm_to_features(nc, "n2", scr["x2"], a["norm_g"][1, 0], mod[1], 0, consts, h_hi, h_lo)
            fourier(nc, tab, h_hi, h_lo)
            y = hs.sb("y", [P, TT, D])
            output_product(nc, "fo", a["fnet_w"][0], h_hi, h_lo, y)
            residual(nc, "r2", y, scr["x2"], gate(1, 2), a["norm_g"][1, 1], scr["x3"])
        with ExitStack() as yctx:
            y = Scope(nc, yctx, "y1").sb("y", [P, TT, D])
            glu_layer(nc, 1, a, mod, consts, scr["x3"], out[0], y)


def kernel(**inputs):
    import numpy as _np
    import concourse.bacc as _bacc
    from concourse import mybir as _mybir
    from concourse.bass_utils import run_bass_kernel_spmd as _run

    nc = _bacc.Bacc("TRN2", target_bir_lowering=False, num_devices=1)
    arrays = {f"in_{n}": _np.ascontiguousarray(a) for n, a in inputs.items()}
    arrays.update({f"table_{n}": a for n, a in tables().items()})
    aps = {n: nc.dram_tensor(n, a.shape, _mybir.dt.from_np(a.dtype), kind="ExternalInput").ap() for n, a in arrays.items()}
    out = nc.dram_tensor("out_0", (1, S, D), F32, kind="ExternalOutput").ap()
    build(nc, {n[3:]: a for n, a in aps.items() if n.startswith("in_")},
          {n[6:]: a for n, a in aps.items() if n.startswith("table_")}, out)
    r = _run(nc, [arrays], core_ids=[0])
    return r.results[0]["out_0"]
```
